# Optimizing a Trainium2 kernel written in Bass

```python
import math
import jax, jax.numpy as jnp
from jax import lax
import numpy as np

D_MODEL = 1024
BATCH = 1
SEQ = 512
DEPTH = 1

ROPE_THETA = 500000.0
NORM_EPS = 1e-6
BLOCK_Q = 128
MLA_HEADS = 8
MLA_NOPE_DIM = 64
MLA_ROPE_DIM = 32
MLA_QK_DIM = MLA_NOPE_DIM + MLA_ROPE_DIM
MLA_V_DIM = 64
MLA_Q_RANK = 384
MLA_KV_RANK = 256
MLA_WIDTH = MLA_HEADS * MLA_V_DIM
DIFF_HEADS = 4
DIFF_HEAD_DIM = 64
DIFF_V_DIM = 2 * DIFF_HEAD_DIM
DIFF_ROT_DIM = DIFF_HEAD_DIM // 4
DIFF_QK_WIDTH = DIFF_HEADS * 2 * DIFF_HEAD_DIM
DIFF_WIDTH = DIFF_HEADS * DIFF_V_DIM
N_BRANCHES = 2
IN_SIZES = (MLA_Q_RANK, MLA_KV_RANK, MLA_ROPE_DIM, DIFF_QK_WIDTH, DIFF_QK_WIDTH, DIFF_WIDTH, N_BRANCHES * D_MODEL)
IN_WIDTH = MLA_Q_RANK + MLA_KV_RANK + MLA_ROPE_DIM + 2 * DIFF_QK_WIDTH + DIFF_WIDTH + N_BRANCHES * D_MODEL
FFN_HIDDEN = ((-(-8 * D_MODEL // 3) + 255) // 256) * 256


def rmsnorm(x, g):
    xf = x.astype(jnp.float32)
    y = xf * lax.rsqrt(jnp.mean(xf * xf, axis=-1, keepdims=True) + NORM_EPS)
    return (y * g.astype(jnp.float32)).astype(x.dtype)

def apply_rope(x, positions, rot_dim):
    half = rot_dim // 2
    inv_freq = jnp.exp(-math.log(ROPE_THETA) * jnp.arange(half, dtype=jnp.float32) * (2.0 / rot_dim))
    ang = positions.astype(jnp.float32)[..., None] * inv_freq
    ang = ang.reshape(ang.shape[:2] + (1,) * (x.ndim - 3) + (half,))
    cos, sin = jnp.cos(ang), jnp.sin(ang)
    xr = x[..., :rot_dim].astype(jnp.float32)
    x1, x2 = xr[..., :half], xr[..., half:]
    rot = jnp.concatenate([x1 * cos - x2 * sin, x2 * cos + x1 * sin], axis=-1).astype(x.dtype)
    return jnp.concatenate([rot, x[..., rot_dim:]], axis=-1)

def causal_attention(q, k, v):
    B, S, H, Dk = q.shape
    Dv = v.shape[-1]
    nb = S // BLOCK_Q
    scale = Dk ** -0.5
    qb = q.reshape(B, nb, BLOCK_Q, H, Dk).transpose(1, 0, 2, 3, 4)
    kpos = jnp.arange(S)

    def one_block(args):
        qi, i = args
        s = jnp.einsum('bqhd,bkhd->bhqk', qi, k).astype(jnp.float32) * scale
        qpos = i * BLOCK_Q + jnp.arange(BLOCK_Q)
        s = jnp.where(kpos[None, :] <= qpos[:, None], s, -jnp.inf)
        p = jax.nn.softmax(s, axis=-1).astype(v.dtype)
        return jnp.einsum('bhqk,bkhd->bqhd', p, v)

    out = lax.map(one_block, (qb, jnp.arange(nb)))
    return out.transpose(1, 0, 2, 3, 4).reshape(B, S, H, Dv)

def first_inputs(seed: int = 0) -> dict:
    key = jax.random.key(seed)
    ks = jax.random.split(key, 24)

    def dense(k, fan_in, fan_out):
        return jax.random.normal(k, (DEPTH, fan_in, fan_out), jnp.float32) * fan_in ** -0.5

    def gain(k, n):
        return 1.0 + 0.02 * jax.random.normal(k, (DEPTH, n), jnp.float32)

    def small(k, n, s):
        return s * jax.random.normal(k, (DEPTH, n), jnp.float32)

    x = jax.random.normal(ks[0], (BATCH, SEQ, D_MODEL), jnp.float32)
    positions = jnp.broadcast_to(jnp.arange(SEQ, dtype=jnp.int32)[None, :], (BATCH, SEQ))
    return {
        "x": x,
        "positions": positions,
        "norm_mix_g": gain(ks[1], D_MODEL),
        "w_in": dense(ks[2], D_MODEL, IN_WIDTH),
        "b_gate": small(ks[3], N_BRANCHES * D_MODEL, 0.1),
        "mla_q_norm_g": gain(ks[4], MLA_Q_RANK),
        "mla_w_uq": dense(ks[5], MLA_Q_RANK, MLA_HEADS * MLA_QK_DIM),
        "mla_kv_norm_g": gain(ks[6], MLA_KV_RANK),
        "mla_w_ukv": dense(ks[7], MLA_KV_RANK, MLA_HEADS * (MLA_NOPE_DIM + MLA_V_DIM)),
        "diff_lambda_q1": small(ks[8], DIFF_HEAD_DIM, 0.1),
        "diff_lambda_k1": small(ks[9], DIFF_HEAD_DIM, 0.1),
        "diff_lambda_q2": small(ks[10], DIFF_HEAD_DIM, 0.1),
        "diff_lambda_k2": small(ks[11], DIFF_HEAD_DIM, 0.1),
        "diff_subln_g": gain(ks[12], DIFF_V_DIM),
        "w_branch_mla": dense(ks[13], MLA_WIDTH, D_MODEL),
        "w_branch_diff": dense(ks[14], DIFF_WIDTH, D_MODEL),
        "w_out": dense(ks[15], D_MODEL, D_MODEL),
        "norm_ffn_g": gain(ks[16], D_MODEL),
        "w_ffn_gate": dense(ks[17], D_MODEL, FFN_HIDDEN),
        "w_ffn_up": dense(ks[18], D_MODEL, FFN_HIDDEN),
        "w_ffn_down": dense(ks[19], FFN_HIDDEN, D_MODEL),
        "norm_final_g": 1.0 + 0.02 * jax.random.normal(ks[20], (D_MODEL,), jnp.float32),
    }

def first_block(x, positions, norm_mix_g, w_in, b_gate, mla_q_norm_g, mla_w_uq, mla_kv_norm_g, mla_w_ukv,
              diff_lambda_q1, diff_lambda_k1, diff_lambda_q2, diff_lambda_k2, diff_subln_g,
              w_branch_mla, w_branch_diff, w_out, norm_ffn_g, w_ffn_gate, w_ffn_up, w_ffn_down, norm_final_g):
    B, S, _ = x.shape
    split_idx = [int(v) for v in np.cumsum(IN_SIZES)[:-1]]
    for l in range(DEPTH):
        xn = rmsnorm(x, norm_mix_g[l])
        proj = jnp.einsum('bsd,de->bse', xn, w_in[l])
        q_lat, kv_lat, k_rope, dq, dk, dv, gate_pre = jnp.split(proj, split_idx, axis=-1)

        q = jnp.einsum('bsr,re->bse', rmsnorm(q_lat, mla_q_norm_g[l]), mla_w_uq[l])
        q = q.reshape(B, S, MLA_HEADS, MLA_QK_DIM)
        q_nope, q_pe = q[..., :MLA_NOPE_DIM], apply_rope(q[..., MLA_NOPE_DIM:], positions, MLA_ROPE_DIM)
        kv = jnp.einsum('bsr,re->bse', rmsnorm(kv_lat, mla_kv_norm_g[l]), mla_w_ukv[l])
        kv = kv.reshape(B, S, MLA_HEADS, MLA_NOPE_DIM + MLA_V_DIM)
        k_nope, v_mla = kv[..., :MLA_NOPE_DIM], kv[..., MLA_NOPE_DIM:]
        k_pe = apply_rope(k_rope[:, :, None, :], positions, MLA_ROPE_DIM)
        q_mla = jnp.concatenate([q_nope, q_pe], axis=-1)
        k_mla = jnp.concatenate([k_nope, jnp.broadcast_to(k_pe, (B, S, MLA_HEADS, MLA_ROPE_DIM))], axis=-1)
        o_mla = causal_attention(q_mla, k_mla, v_mla).reshape(B, S, MLA_WIDTH)

        dq = apply_rope(dq.reshape(B, S, DIFF_HEADS, 2, DIFF_HEAD_DIM), positions, DIFF_ROT_DIM)
        dk = apply_rope(dk.reshape(B, S, DIFF_HEADS, 2, DIFF_HEAD_DIM), positions, DIFF_ROT_DIM)
        dv = dv.reshape(B, S, DIFF_HEADS, DIFF_V_DIM)
        o1 = causal_attention(dq[..., 0, :], dk[..., 0, :], dv)
        o2 = causal_attention(dq[..., 1, :], dk[..., 1, :], dv)
        lambda_init = 0.8 - 0.6 * math.exp(-0.3 * l)
        lam = (jnp.exp(jnp.sum(diff_lambda_q1[l].astype(jnp.float32) * diff_lambda_k1[l].astype(jnp.float32)))
               - jnp.exp(jnp.sum(diff_lambda_q2[l].astype(jnp.float32) * diff_lambda_k2[l].astype(jnp.float32)))
               + lambda_init).astype(o1.dtype)
        o_diff = rmsnorm(o1 - lam * o2, diff_subln_g[l]) * (1.0 - lambda_init)
        o_diff = o_diff.reshape(B, S, DIFF_WIDTH)

        gates = jax.nn.sigmoid(gate_pre + b_gate[l])
        g_mla, g_diff = gates[..., :D_MODEL], gates[..., D_MODEL:]
        merged = (g_mla * jnp.einsum('bse,ed->bsd', o_mla, w_branch_mla[l])
                  + g_diff * jnp.einsum('bse,ed->bsd', o_diff, w_branch_diff[l]))
        x = x + jnp.einsum('bsd,de->bse', merged, w_out[l])

        hn = rmsnorm(x, norm_ffn_g[l])
        hid = jax.nn.silu(jnp.einsum('bsd,df->bsf', hn, w_ffn_gate[l])) * jnp.einsum('bsd,df->bsf', hn, w_ffn_up[l])
        x = x + jnp.einsum('bsf,fd->bsd', hid, w_ffn_down[l])
    return rmsnorm(x, norm_final_g)


CHUNK = 64
EPS = 1e-6

ATT_HEADS = 16
ATT_KV_HEADS = 2
HEAD_DIM = 64
ATT_GROUP = ATT_HEADS // ATT_KV_HEADS
ATT_WIDTH = ATT_HEADS * HEAD_DIM
KV_WIDTH = ATT_KV_HEADS * HEAD_DIM
WINDOW = 128
WINDOW_CHUNKS = WINDOW // CHUNK
KEY_BLOCK = (WINDOW_CHUNKS + 1) * CHUNK
ROPE_DIM = HEAD_DIM // 4

SG_BLOCK = 128
SG_GROUPS = 8
SG_WIDTH = 1024
SG_GROUP_WIDTH = SG_WIDTH // SG_GROUPS

IN_SIZES_2 = [ATT_WIDTH, KV_WIDTH, KV_WIDTH, ATT_WIDTH,
            SG_WIDTH, SG_WIDTH, SG_WIDTH,
            N_BRANCHES * D_MODEL]
IN_WIDTH_2 = int(sum(IN_SIZES_2))
IN_SPLITS = [int(s) for s in np.cumsum(IN_SIZES_2)[:-1]]


def rmsnorm_2(x, g):
    xf = x.astype(jnp.float32)
    y = xf * lax.rsqrt(jnp.mean(xf * xf, axis=-1, keepdims=True) + EPS)
    return (y * g.astype(jnp.float32)).astype(x.dtype)

def layernorm(x, g, b):
    xf = x.astype(jnp.float32)
    mu = jnp.mean(xf, axis=-1, keepdims=True)
    xc = xf - mu
    y = xc * lax.rsqrt(jnp.mean(xc * xc, axis=-1, keepdims=True) + EPS)
    return (y * g.astype(jnp.float32) + b.astype(jnp.float32)).astype(x.dtype)

def partial_rope(x, pos):
    half = ROPE_DIM // 2
    inv_freq = ROPE_THETA ** (-(jnp.arange(half, dtype=jnp.float32) * 2.0) / ROPE_DIM)
    ang = pos.astype(jnp.float32)[:, None] * inv_freq[None, :]
    cos = jnp.cos(ang)[None, :, None, :]
    sin = jnp.sin(ang)[None, :, None, :]
    xf = x.astype(jnp.float32)
    x1, x2, rest = xf[..., :half], xf[..., half:ROPE_DIM], xf[..., ROPE_DIM:]
    out = jnp.concatenate([x1 * cos - x2 * sin, x2 * cos + x1 * sin, rest], axis=-1)
    return out.astype(x.dtype)

def window_sink_attention(q, k, v, sinks):
    B, S = q.shape[0], q.shape[1]
    nc = S // CHUNK
    qc = q.reshape(B, nc, CHUNK, ATT_KV_HEADS, ATT_GROUP, HEAD_DIM)
    pad = ((0, 0), (WINDOW_CHUNKS, 0), (0, 0), (0, 0), (0, 0))
    kc = jnp.pad(k.reshape(B, nc, CHUNK, ATT_KV_HEADS, HEAD_DIM), pad)
    vc = jnp.pad(v.reshape(B, nc, CHUNK, ATT_KV_HEADS, HEAD_DIM), pad)
    kb = jnp.concatenate([kc[:, j:j + nc] for j in range(WINDOW_CHUNKS + 1)], axis=2)
    vb = jnp.concatenate([vc[:, j:j + nc] for j in range(WINDOW_CHUNKS + 1)], axis=2)
    s = jnp.einsum('bnqhgd,bnkhd->bhgnqk', qc, kb,
                   preferred_element_type=jnp.float32) * (HEAD_DIM ** -0.5)
    key_chunk = jnp.arange(nc)[:, None] - WINDOW_CHUNKS + jnp.arange(WINDOW_CHUNKS + 1)[None, :]
    valid = jnp.repeat(key_chunk >= 0, CHUNK, axis=1)
    s = jnp.where(valid[None, None, None, :, None, :], s, -1e30)
    sink = sinks.astype(jnp.float32).reshape(ATT_KV_HEADS, ATT_GROUP)[None, :, :, None, None, None]
    m = jnp.maximum(jnp.max(s, axis=-1, keepdims=True), sink)
    p = jnp.exp(s - m)
    denom = jnp.sum(p, axis=-1, keepdims=True) + jnp.exp(sink - m)
    o = jnp.einsum('bhgnqk,bnkhd->bnqhgd', p / denom, vb.astype(jnp.float32))
    return o.reshape(B, S, ATT_WIDTH).astype(q.dtype)

def chunked_spatial_gating(u, v, w_s, b_s, ln_g, ln_b):
    B, S = u.shape[0], u.shape[1]
    nb = S // SG_BLOCK
    v = layernorm(v, ln_g, ln_b)
    vb = v.reshape(B, nb, SG_BLOCK, SG_GROUPS, SG_GROUP_WIDTH)
    cidx = np.arange(SG_BLOCK) // CHUNK
    mask = jnp.asarray(cidx[None, :] <= cidx[:, None])
    w = jnp.where(mask[None], w_s, jnp.zeros_like(w_s))
    mixed = jnp.einsum('gij,bnjgc->bnigc', w, vb) + jnp.transpose(b_s)[None, None, :, :, None]
    return u * mixed.reshape(B, S, SG_WIDTH)

def second_inputs(seed: int = 0) -> dict:
    key = jax.random.key(seed)
    ks = jax.random.split(key, 16)
    f32 = jnp.float32
    d = D_MODEL
    x = jax.random.normal(ks[0], (BATCH, SEQ, d), f32)
    norm_g = 1.0 + 0.05 * jax.random.normal(ks[1], (DEPTH, d), f32)
    w_in = jax.random.normal(ks[2], (DEPTH, d, IN_WIDTH_2), f32) * d ** -0.5
    b_merge = 0.01 * jax.random.normal(ks[3], (DEPTH, N_BRANCHES * d), f32)
    att_sinks = 0.5 * jax.random.normal(ks[4], (DEPTH, ATT_HEADS), f32)
    sg_w = jax.random.normal(ks[5], (DEPTH, SG_GROUPS, SG_BLOCK, SG_BLOCK), f32) * (0.5 * SG_BLOCK ** -0.5)
    sg_b = 1.0 + 0.1 * jax.random.normal(ks[6], (DEPTH, SG_GROUPS, SG_BLOCK), f32)
    sg_ln_g = 1.0 + 0.05 * jax.random.normal(ks[7], (DEPTH, SG_WIDTH), f32)
    sg_ln_b = 0.02 * jax.random.normal(ks[8], (DEPTH, SG_WIDTH), f32)
    w_att_out = jax.random.normal(ks[9], (DEPTH, ATT_WIDTH, d), f32) * ATT_WIDTH ** -0.5
    w_sg_out = jax.random.normal(ks[10], (DEPTH, SG_WIDTH, d), f32) * SG_WIDTH ** -0.5
    w_o = jax.random.normal(ks[11], (DEPTH, d, d), f32) * d ** -0.5
    final_g = 1.0 + 0.05 * jax.random.normal(ks[12], (d,), f32)
    return {"x": x, "norm_g": norm_g, "w_in": w_in, "b_merge": b_merge,
            "att_sinks": att_sinks, "sg_w": sg_w, "sg_b": sg_b, "sg_ln_g": sg_ln_g,
            "sg_ln_b": sg_ln_b, "w_att_out": w_att_out, "w_sg_out": w_sg_out,
            "w_o": w_o, "final_g": final_g}

def second_block(x, norm_g, w_in, b_merge, att_sinks, sg_w, sg_b, sg_ln_g, sg_ln_b,
              w_att_out, w_sg_out, w_o, final_g):
    B, S = x.shape[0], x.shape[1]
    pos = jnp.arange(S)
    for l in range(DEPTH):
        h = rmsnorm_2(x, norm_g[l])
        proj = h @ w_in[l]
        q, k, v, za, u, vs, zs, gm = jnp.split(proj, IN_SPLITS, axis=-1)
        q = partial_rope(q.reshape(B, S, ATT_HEADS, HEAD_DIM), pos)
        k = partial_rope(k.reshape(B, S, ATT_KV_HEADS, HEAD_DIM), pos)
        v = v.reshape(B, S, ATT_KV_HEADS, HEAD_DIM)
        a = window_sink_attention(q, k, v, att_sinks[l])
        a = (a * jax.nn.silu(za)) @ w_att_out[l]
        sgo = chunked_spatial_gating(jax.nn.gelu(u, approximate=False),
                                     jax.nn.gelu(vs, approximate=False),
                                     sg_w[l], sg_b[l], sg_ln_g[l], sg_ln_b[l])
        sgo = (sgo * jax.nn.silu(zs)) @ w_sg_out[l]
        ga, gs = jnp.split(jax.nn.sigmoid(gm + b_merge[l]), N_BRANCHES, axis=-1)
        y = ga * a + gs * sgo
        x = x + y @ w_o[l]
    return rmsnorm_2(x, final_g)


def setup_inputs(seed=0):
    out = dict(first_inputs(seed))
    for name, value in second_inputs(seed + 1).items():
        if name != "x":
            out[name + "_2"] = value
    return out


def reference(
    x, positions, norm_mix_g, w_in, b_gate, mla_q_norm_g, mla_w_uq, mla_kv_norm_g, mla_w_ukv,
    diff_lambda_q1, diff_lambda_k1, diff_lambda_q2, diff_lambda_k2, diff_subln_g, w_branch_mla,
    w_branch_diff, w_out, norm_ffn_g, w_ffn_gate, w_ffn_up, w_ffn_down, norm_final_g, norm_g_2,
    w_in_2, b_merge_2, att_sinks_2, sg_w_2, sg_b_2, sg_ln_g_2, sg_ln_b_2, w_att_out_2,
    w_sg_out_2, w_o_2, final_g_2,
):
    x = first_block(
        x, positions, norm_mix_g, w_in, b_gate, mla_q_norm_g, mla_w_uq, mla_kv_norm_g,
        mla_w_ukv, diff_lambda_q1, diff_lambda_k1, diff_lambda_q2, diff_lambda_k2, diff_subln_g,
        w_branch_mla, w_branch_diff, w_out, norm_ffn_g, w_ffn_gate, w_ffn_up, w_ffn_down,
        norm_final_g,
    )
    return second_block(
        x, norm_g_2, w_in_2, b_merge_2, att_sinks_2, sg_w_2, sg_b_2, sg_ln_g_2, sg_ln_b_2,
        w_att_out_2, w_sg_out_2, w_o_2, final_g_2,
    )


_drawn_inputs = setup_inputs


def setup_inputs(seed=0):
    import zlib

    import numpy as np

    out = dict(_drawn_inputs(seed))
    spreads = {}
    factors = {'norm_mix_g': 3.063,
     'b_gate': 3.195,
     'mla_q_norm_g': 8.0,
     'mla_kv_norm_g': 8.0,
     'diff_lambda_k1': 8.0,
     'diff_lambda_q2': 8.0,
     'diff_subln_g': 6.647,
     'norm_ffn_g': 3.972,
     'norm_final_g': 2.842,
     'norm_g_2': 3.021,
     'b_merge_2': 24.562,
     'att_sinks_2': 64.0,
     'sg_b_2': 2.905,
     'sg_ln_g_2': 8.0,
     'sg_ln_b_2': 29.666}
    for name, (base, spread) in spreads.items():
        noise = np.random.default_rng([zlib.crc32(name.encode()), seed]).standard_normal(out[name].shape)
        drawn = base * np.exp(spread * noise) if base else spread * noise
        out[name] = __import__('jax').numpy.asarray(drawn.astype(out[name].dtype))
    for name, factor in factors.items():
        out[name] = (out[name] * factor).astype(out[name].dtype)
    return out
```

```python
import math
from contextlib import ExitStack

import concourse.bass as bass
from concourse import mybir

ALU = mybir.AluOpType
ACT = mybir.ActivationFunctionType
AX = mybir.AxisListType
F32 = mybir.dt.float32
F32R = mybir.dt.float32r
I32 = mybir.dt.int32

P = 128
S = 512
TT = S // P
D = 1024
KD = D // P
UNIT = 2048
EPS = 1e-6
NEG = -1e30

MH, MN, MR, MV = 8, 64, 32, 64
MQ = MN + MR
QR, KVR = 384, 256
LAT = QR + KVR + MR
DH, DD, DV = 4, 64, 128
FF = 2816
KF = FF // P
LAMBDA_INIT = 0.8 - 0.6 * math.exp(0.0)
AH, AG, AD = 16, 2, 64
CHUNK = 64

ROWS = [("norm_mix_g", 8), ("b_gate", 16), ("mla_q_norm_g", 3), ("mla_kv_norm_g", 2), ("diff_subln_g", 1),
        ("norm_ffn_g", 8), ("norm_g_2", 8), ("b_merge_2", 16)]
ROW0 = {}
for _n, _c in ROWS:
    ROW0[_n] = sum(c for _, c in ROWS[:len(ROW0)])
NROWS = sum(c for _, c in ROWS)

COUNTS = [("lat", 3), ("gate_a", 4), ("uq", 4), ("kn", 2), ("mv", 2), ("gate_b", 4), ("dq", 2), ("dk", 2),
          ("dv", 2), ("mrg_m", 4), ("mrg_d", 4), ("out", 4), ("ffn", 22), ("down", 12),
          ("q2", 4), ("kv2", 1), ("za", 4), ("zs", 4), ("u2", 4), ("vs", 4), ("ga", 4), ("att", 4), ("gs", 4),
          ("sgo", 4), ("wo", 4)]
U0 = {}
_u = 0
for _n, _c in COUNTS:
    U0[_n] = _u
    _u += _c
NU = _u
DOWN_GROUPS = 4
DOWN_K = (8, 8, 6)


def group_of(u):
    d = U0["down"]
    if u < d:
        return u
    if u < d + 12:
        return d + (u - d) // 3
    return u - 12 + DOWN_GROUPS


def window_head(i, e):
    return 4 * (i // 2) + i % 2 + 2 * e


ACT_FREED = ([group_of(U0["ffn"]) + 2 * j for j in range(KF // 2)]
             + [group_of(U0[n]) + i for n in ("ga", "gs") for i in range(4)])


def act_freed(g, m):
    return 2 * sum(a < g for a in ACT_FREED) + m + 1


def dve_freed(g, m):
    return 2 * (g - sum(a < g for a in ACT_FREED)) + m + 1


def freed(u, m):
    return dve_freed(group_of(u), m)


def build(nc, A):
    with ExitStack() as ctx:
        def sem(name):
            return ctx.enter_context(nc.semaphore(name))

        def keep(name, shape, dt=F32):
            return ctx.enter_context(nc.sbuf_tensor(name, shape, dt))

        def overlay(*tensors):
            with ExitStack() as sub:
                return [sub.enter_context(nc.sbuf_tensor(n, s, d)) for n, s, d in tensors]

        stage = keep("stage", [P, 2, UNIT])
        w_hi = keep("w_hi", [P, 2, UNIT], F32R)
        w_lo = keep("w_lo", [P, 2, UNIT], F32R)
        act_hi = keep("act_hi", [P, KD, S], F32R)
        act_lo = keep("act_lo", [P, KD, S], F32R)
        ident = keep("ident", [P, P])
        ident_r = keep("ident_r", [P, P], F32R)
        causal_r = keep("causal_r", [P, P], F32R)
        window_r = keep("window_r", [P, 2, 2 * P], F32R)
        col = keep("col", [P, NROWS])
        ncol = keep("ncol", [P, NROWS])
        freq = keep("freq", [P, 2])
        small = keep("small", [P, 384])
        rope2 = keep("rope2", [P, 2, S])
        tmp = keep("tmp", [P, 2, S])

        (rope_m, rope_d, pt) = overlay(("rope_m", [P, 2, S], F32), ("rope_d", [P, 2, S], F32), ("pt", [P, 2, S], F32))
        (p2, o_sb, o_sq) = overlay(("p2", [P, 2, S], F32), ("o_sb", [P, S], F32), ("o_sq", [P, S], F32))
        res = keep("res", [P, TT, D])

        (x_in, x_sc, rows, lamv, pos_i, pos_i2, pos_f, rt) = overlay(
            ("x_in", [P, TT, D], F32), ("x_sc", [P, TT, D], F32), ("rows", [P, P], F32), ("lamv", [P, 4, DD], F32),
            ("pos_i", [P, S], I32), ("pos_i2", [P, S], I32), ("pos_f", [P, 2, S], F32), ("rt", [P, 4, S], F32))
        with ExitStack() as b1:
            def b1keep(name, shape, dt=F32):
                return b1.enter_context(nc.sbuf_tensor(name, shape, dt))

            gates = b1keep("gates", [P, 16, S])
            with ExitStack() as sub:
                lt_hi = sub.enter_context(nc.sbuf_tensor("lt_hi", [P, 5, S], F32R))
                lt_lo = sub.enter_context(nc.sbuf_tensor("lt_lo", [P, 5, S], F32R))
            om_hi = b1keep("om_hi", [P, 4, S], F32R)
            om_lo = b1keep("om_lo", [P, 4, S], F32R)
            prob = b1keep("prob", [P, 4, S])
            with ExitStack() as sub:
                qm, km, vm = [sub.enter_context(nc.sbuf_tensor(n, s, F32)) for n, s in (
                    ("qm", [P, MH, S]), ("km", [P, MH, S]), ("vm", [P, TT, MH * MV]))]
            with ExitStack() as sub:
                sub.enter_context(nc.sbuf_tensor("pad_lat", [P, MH, S], F32))
                lat = sub.enter_context(nc.sbuf_tensor("lat", [P, TT, LAT], F32))
            with ExitStack() as sub:
                dq, dk, dv = [sub.enter_context(nc.sbuf_tensor(n, [P, TT, S], F32)) for n in ("dq", "dk", "dv")]
                od_hi = sub.enter_context(nc.sbuf_tensor("od_hi", [P, DH, S], F32R))
                od_lo = sub.enter_context(nc.sbuf_tensor("od_lo", [P, DH, S], F32R))
        (h_hi, h_lo, sl, gf_b) = overlay(("h_hi", [P, KF, S], F32R), ("h_lo", [P, KF, S], F32R),
                                         ("sl", [P, 2, S], F32), ("gf_b", [P, D], F32))
        (n_sc,) = overlay(("n_sc", [P, TT, D], F32))
        with ExitStack() as b2:
            def b2keep(name, shape, dt=F32):
                return b2.enter_context(nc.sbuf_tensor(name, shape, dt))

            def b2share(*tensors):
                with ExitStack() as sub:
                    return [sub.enter_context(nc.sbuf_tensor(n, s, d)) for n, s, d in tensors]

            gz = b2keep("gz", [P, KD, S])
            gu = b2keep("gu", [P, KD, S])
            (q2,) = b2share(("q2", [P, KD, S], F32))
            (gs,) = b2share(("gs", [P, KD, S], F32))
            vs = b2keep("vs", [P, TT, D])
            kdup, v2, vt2, prob2, pt2, a_tok = b2share(
                ("kdup", [P, 2, S], F32), ("v2", [P, TT, P], F32), ("vt2", [P, 2, S], F32),
                ("prob2", [P, 4, S], F32), ("pt2", [P, 2, S], F32), ("a_tok", [P, 2, S], F32))
            (wg_in,) = b2share(("pad_wg", [P, 14 * S], F32), ("wg_in", [P, 8, P], F32))[1:]
            at_hi = b2keep("at_hi", [P, KD, S], F32R)
            at_lo = b2keep("at_lo", [P, KD, S], F32R)
            wg_t = b2keep("wg_t", [P, 8, P])
            sgb_b = b2keep("sgb_b", [P, 8, P])
            lng_b = b2keep("lng_b", [P, D])
            lnb_b = b2keep("lnb_b", [P, D])

        ps_mm = ctx.enter_context(nc.psum_tensor("ps_mm", [P, 4, S], F32))
        ps_s = ctx.enter_context(nc.psum_tensor("ps_s", [P, 2, S], F32))
        ps_t = ctx.enter_context(nc.psum_tensor("ps_t", [P, S], F32))
        ps_o = ctx.enter_context(nc.psum_tensor("ps_o", [P, S], F32))

        def side_bank(k):
            return (ps_s[:, 0, :], ps_s[:, 1, :], ps_t[:, :], ps_o[:, :])[k % 4]

        at = [0]

        def cut(n):
            at[0] += n
            assert at[0] <= 384
            return small[:, at[0] - n:at[0]]

        ssq, var, rstd, nt1 = cut(16), cut(16), cut(16), cut(16)
        seed = cut(16)
        nmx, nbias, rsum, rinv = cut(8), cut(8), cut(8), cut(8)
        lamt = cut(8)
        lsum = cut(2)
        lexp = cut(2)
        neglam = cut(1)
        sinkb, m2, nm2, rs2 = cut(16), cut(32), cut(32), cut(32)
        dsink, esink, den2, rden2 = cut(8), cut(8), cut(8), cut(8)
        vsum, mean, nmean = cut(16), cut(4), cut(4)
        halfpi = cut(1)

        w_landed = [sem("w_landed0"), sem("w_landed1")]
        w_hi_made, w_lo_made, w_used = sem("w_hi_made"), sem("w_lo_made"), sem("w_used")
        first_full, bank_free, bank_free_act = sem("first_full"), sem("bank_free"), sem("bank_free_act")
        x_landed, rows_landed, pos_landed, lam_landed, freq_landed, sink_landed = [
            sem(n) for n in ("x_landed", "rows_landed", "pos_landed", "lam_landed", "freq_landed", "sink_landed")]
        res_landed, gf_landed, wg_landed, sgb_landed, ln_landed, fg_landed, out_written = [
            sem(n) for n in ("res_landed", "gf_landed", "wg_landed", "sgb_landed", "ln_landed", "fg_landed",
                             "out_written")]
        consts_made, ident_made, cols_turned, cols_made = [
            sem(n) for n in ("consts_made", "ident_made", "cols_turned", "cols_made")]
        dve_chain, act_chain, pool_chain = sem("dve_chain"), sem("act_chain"), sem("pool_chain")
        norm_squared, norm_scaled, norm_turned, norm_hi, norm_lo = [
            sem(n) for n in ("norm_squared", "norm_scaled", "norm_turned", "norm_hi", "norm_lo")]
        iota_made = sem("iota_made")
        angle_ready, sincos_made = sem("angle_ready"), sem("sincos_made")
        lam_summed, lam_exp = sem("lam_summed"), sem("lam_exp")
        lat_kept, lat_squared, lat_scaled, lat_turned, lat_hi, lat_lo, kpe_roped, kpe_spread = [
            sem(n) for n in ("lat_kept", "lat_squared", "lat_scaled", "lat_turned", "lat_hi", "lat_lo", "kpe_roped",
                             "kpe_spread")]
        gate_exp, kn_kept = sem("gate_exp"), sem("kn_kept")
        qkv_kept = sem("qkv_kept")
        s_full, max_made, exp_made, p_ready, t_full, pt_made, pv_done, o_hi_made, o_free = [
            sem(n) for n in ("s_full", "max_made", "exp_made", "p_ready", "t_full", "pt_made", "pv_done", "o_hi_made",
                             "o_free")]
        o_scaled, o_turned, od_hi_made, od_made = [sem(n) for n in ("o_scaled", "o_turned", "od_hi_made", "od_made")]
        merged, merged_hi, merged_lo = sem("merged"), sem("merged_hi"), sem("merged_lo")
        silu_made, up_made, h_hi_made, h_lo_made = [
            sem(n) for n in ("silu_made", "up_made", "h_hi_made", "h_lo_made")]
        res_ready, x3_made = sem("res_ready"), sem("x3_made")
        kv_kept, kr_made, kdup_made, v_turned, v2_made, wg_turned, wg_made = [
            sem(n) for n in ("kv_kept", "kr_made", "kdup_made", "v_turned", "v2_made", "wg_turned", "wg_made")]
        z_exp, sink_diff, sink_exp, a_kept, a_turned, a_gated = [
            sem(n) for n in ("z_exp", "sink_diff", "sink_exp", "a_kept", "a_turned", "a_gated")]
        at_hi_made, at_lo_made = sem("at_hi_made"), sem("at_lo_made")
        gelu_made, vs_summed, vs_squared, vs_normed, mix_full, mix_gated, sg_hi_made, sg_lo_made = [
            sem(n) for n in ("gelu_made", "vs_summed", "vs_squared", "vs_normed", "mix_full", "mix_gated",
                             "sg_hi_made", "sg_lo_made")]
        sig_made, y_sum, y_hi_made, y_lo_made = [sem(n) for n in ("sig_made", "y_sum", "y_hi_made", "y_lo_made")]
        fin_squared, fin_made = sem("fin_squared"), sem("fin_made")
        exp2_made, s2_full, max2_made, t2_full, pt2_made, pv2_done = [
            sem(n) for n in ("exp2_made", "s2_full", "max2_made", "t2_full", "pt2_made", "pv2_done")]
        dS, dMax, dExp, dP, dT, dPt, dPv, o_copied, o_squared = [
            sem(n) for n in ("d_s_full", "d_max_made", "d_exp_made", "d_p_ready", "d_t_full", "d_pt_made", "d_pv_done",
                             "o_copied", "o_squared")]

        def chunks(ap):
            return ap.rearrange("a (k p) n -> p (a k) n", p=P)

        w_in, w_in2 = chunks(A["w_in"]), chunks(A["w_in_2"])
        w_gate, w_up, w_down = chunks(A["w_ffn_gate"]), chunks(A["w_ffn_up"]), chunks(A["w_ffn_down"])
        uq = chunks(A["mla_w_uq"])
        ukv = A["mla_w_ukv"].rearrange("a (k p) (h e) -> p (a k) h e", p=P, e=MN + MV)
        wbm, wbd, wout = chunks(A["w_branch_mla"]), chunks(A["w_branch_diff"]), chunks(A["w_out"])
        wao, wso, wo2 = chunks(A["w_att_out_2"]), chunks(A["w_sg_out_2"]), chunks(A["w_o_2"])
        C_DQ, C_DK, C_DV = LAT, LAT + 512, LAT + 1024
        C_G = LAT + 1536
        C2 = {"q2": 0, "kv2": 1024, "za": 1280, "u2": 2304, "vs": 3328, "zs": 4352, "ga": 5376, "gs": 6400}

        def unit_source(u):
            name = [n for n, c in COUNTS if U0[n] <= u < U0[n] + c][0]
            i = u - U0[name]
            w = 256
            c0 = 256 * i
            if name == "lat":
                w = 256 if i < 2 else LAT - 512
                return w_in[:, :, c0:c0 + w], 8, w
            if name == "gate_a":
                return w_in[:, :, C_G + c0:C_G + c0 + w], 8, w
            if name == "gate_b":
                return w_in[:, :, C_G + 1024 + c0:C_G + 1024 + c0 + w], 8, w
            if name == "uq":
                return uq[:, :, 192 * i:192 * i + 192], 3, 192
            if name == "kn":
                return ukv[:, :, 4 * i:4 * i + 4, 0:MN], 2, 256
            if name == "mv":
                return ukv[:, :, 4 * i:4 * i + 4, MN:MN + MV], 2, 256
            if name in ("dq", "dk", "dv"):
                b = {"dq": C_DQ, "dk": C_DK, "dv": C_DV}[name]
                return w_in[:, :, b + c0:b + c0 + w], 8, w
            if name == "mrg_m":
                return wbm[:, :, c0:c0 + w], 4, w
            if name == "mrg_d":
                return wbd[:, :, c0:c0 + w], 4, w
            if name in ("out", "att", "sgo", "wo"):
                m = {"out": wout, "att": wao, "sgo": wso, "wo": wo2}[name]
                return m[:, :, c0:c0 + w], 8, w
            return w_in2[:, :, C2[name] + c0:C2[name] + c0 + w], 8, w

        def slot(t, s, k, w):
            return t[:, s, 0:k * w].rearrange("p (k n) -> p k n", k=k)

        block = ctx.enter_context(nc.Block())

        @block.sync
        def _(sp):
            def load(u, s, src, k, w):
                dst = slot(stage, s, k, w)
                if len(src.shape) == 4:
                    dst = dst.rearrange("p k (h e) -> p k h e", h=src.shape[2])
                    for kk in range(k):
                        sp.dma_start(dst[:, kk], src[:, kk]).then_inc(w_landed[s], 16)
                else:
                    sp.dma_start(dst, src).then_inc(w_landed[s], 16)

            def straight(u, first=False):
                if u >= 2:
                    sp.wait_ge(w_lo_made, u - 1)
                load(u, u % 2, *unit_source(u))

            xv = A["x"].rearrange("a (t p) d -> p (a t) d", p=P)
            for t in range(TT):
                sp.dma_start(x_in[:, t, :], xv[:, t, :]).then_inc(x_landed, 16)
            for name, n in ROWS:
                sp.dma_start(rows[ROW0[name]:ROW0[name] + n, :],
                             A[name].rearrange("a (r p) -> (a r) p", p=P)).then_inc(rows_landed, 16)
            straight(0)
            sp.dma_start(freq[:, :], A["rope_freq"]).then_inc(freq_landed, 16)
            sp.dma_start(pos_i[:, :], A["positions"].broadcast_to([P, S])).then_inc(pos_landed, 16)
            for i, name in enumerate(("diff_lambda_q1", "diff_lambda_k1", "diff_lambda_q2", "diff_lambda_k2")):
                sp.dma_start(lamv[:, i, :], A[name].broadcast_to([P, DD])).then_inc(lam_landed, 16)
            sp.dma_start(sinkb, A["att_sinks_2"].broadcast_to([P, AH])).then_inc(sink_landed, 16)
            for u in range(1, U0["out"]):
                straight(u)
            sp.wait_ge(od_made, DH)
            sp.wait_ge(dPv, 4 * DH)
            for t in range(TT):
                sp.dma_start(res[:, t, :], xv[:, t, :]).then_inc(res_landed, 16)
            for u in range(U0["out"], U0["ffn"]):
                straight(u)
            u0 = U0["ffn"]
            with sp.Fori(0, KF // 2) as j:
                for h, wv in enumerate((w_gate, w_up)):
                    lo_due = sp.snap(j * 2 + (u0 + h - 1))
                    c0 = sp.snap(j * 256)
                    sp.wait_ge(w_lo_made, lo_due)
                    s = (u0 + h) % 2
                    sp.dma_start(slot(stage, s, 8, 256), wv[:, :, bass.ds(c0, 256)]).then_inc(w_landed[s], 16)
            u0 = U0["down"]
            with sp.Fori(0, DOWN_GROUPS // 2) as j:
                for gg in range(2):
                    c0 = sp.snap(j * 512 + gg * 256)
                    for i in range(3):
                        lo_due = sp.snap(j * 6 + (u0 + 3 * gg + i - 1))
                        sp.wait_ge(w_lo_made, lo_due)
                        s = (u0 + 3 * gg + i) % 2
                        k0 = sum(DOWN_K[:i])
                        sp.dma_start(slot(stage, s, DOWN_K[i], 256),
                                     w_down[:, k0:k0 + DOWN_K[i], bass.ds(c0, 256)]).then_inc(w_landed[s], 16)
            for u in range(U0["q2"], NU):
                if u == U0["q2"]:
                    sp.wait_ge(h_lo_made, KF)
                    sp.dma_start(gf_b[:, :], A["norm_final_g"].rearrange("(a d) -> a d", a=1).broadcast_to([P, D])
                                 ).then_inc(gf_landed, 16)
                if u == U0["kv2"]:
                    sp.wait_ge(x3_made, TT)
                    sp.dma_start(wg_in[:, :, :], A["sg_w_2"].rearrange("a g i j -> i (a g) j")).then_inc(wg_landed, 16)
                    sp.dma_start(sgb_b[:, :, :].rearrange("p g i -> p (g i)"),
                                 A["sg_b_2"].rearrange("a g i -> a (g i)").broadcast_to([P, D])
                                 ).then_inc(sgb_landed, 16)
                    sp.dma_start(lng_b[:, :], A["sg_ln_g_2"].broadcast_to([P, D])).then_inc(ln_landed, 16)
                    sp.dma_start(lnb_b[:, :], A["sg_ln_b_2"].broadcast_to([P, D])).then_inc(ln_landed, 16)
                if u == U0["wo"]:
                    sp.wait_ge(vs_normed, TT)
                    sp.dma_start(lng_b[:, :], A["final_g_2"].rearrange("(a d) -> a d", a=1).broadcast_to([P, D])
                                 ).then_inc(fg_landed, 16)
                straight(u)
            ov = A["out"].rearrange("a (t p) d -> p (a t) d", p=P)
            for t in range(TT):
                sp.wait_ge(fin_made, t + 1)
                sp.dma_start(ov[:, t, :], res[:, t, :]).then_inc(out_written, 16)
            sp.wait_ge(out_written, 16 * TT)

        def landed_count(u):
            two = U0["kn"]
            return 16 * sum(2 if two <= v < two + 4 else 1 for v in range(u % 2, u + 1, 2))

        @block.gpsimd
        def _(pool):
            pool.memset(ident[:, :], 1.0).then_inc(pool_chain, 1)
            pool.memset(tmp[:, 0, 0:P], 0.0).then_inc(pool_chain, 1)
            pool.memset(tmp[:, 1, :], 0.0).then_inc(pool_chain, 1)
            pool.memset(halfpi, math.pi / 2).then_inc(pool_chain, 1)
            pool.iota(pos_i2[:, :], pattern=[[1, S]], base=0, channel_multiplier=0).then_inc(iota_made, 1)
            pool.wait_ge(pool_chain, 4)
            pool.affine_select(out=ident[:, :], in_=ident[:, :], compare_op=ALU.is_equal, fill=0.0, base=0,
                               pattern=[[-1, P]], channel_multiplier=1).then_inc(ident_made, 1)
            pool.affine_select(out=tmp[:, 0, 0:P], in_=tmp[:, 0, 0:P], compare_op=ALU.is_ge, fill=NEG, base=0,
                               pattern=[[-1, P]], channel_multiplier=1).then_inc(consts_made, 1)
            wv = tmp[:, 1, :].rearrange("p (e n) -> p e n", e=2)
            for e in range(2):
                pool.wait_ge(consts_made, 2 * e + 1)
                pool.memset(wv[CHUNK:P, e, 0:CHUNK], NEG).then_inc(consts_made, 1)
                pool.wait_ge(consts_made, 2 * e + 2)
                pool.memset(wv[0:CHUNK, e, 2 * P - CHUNK:2 * P], NEG).then_inc(consts_made, 1)

        @block.scalar
        def _(act):
            chain = [0]

            def hi(u):
                s = u % 2
                src, k, w = unit_source(u)
                act.wait_ge(w_landed[s], landed_count(u))
                if u >= 2:
                    act.wait_ge(w_used, u - 1)
                nc.scalar.activation(w_hi[:, s, 0:k * w], stage[:, s, 0:k * w], ACT.Copy).then_inc(w_hi_made, 1)

            def bank(u, m):
                g = group_of(u)
                if m == 0:
                    act.wait_ge(first_full, g + 1)
                else:
                    act.wait_ge(w_used, u + 1)
                return ps_mm[:, 2 * (g % 2) + m, :]

            def squares(src, out, acc, signal):
                nc.scalar.activation(out, src, ACT.Square, accum_out=acc).then_inc(signal, 1)

            def norm_hi_chunks(row, base):
                for k in range(KD):
                    act.wait_ge(norm_turned, base + k + 1)
                    nc.scalar.activation(act_hi[:, k, :], side_bank(k), ACT.Copy,
                                         scale=col[:, ROW0[row] + k:ROW0[row] + k + 1]).then_inc(norm_hi, 1)

            def gate_bank(u, m, c):
                nc.scalar.activation(gates[:, c, :], bank(u, m), ACT.Exp, scale=-1.0,
                                     bias=ncol[:, ROW0["b_gate"] + c:ROW0["b_gate"] + c + 1]).then_inc(gate_exp, 1)

            for t in range(TT):
                act.wait_ge(x_landed, 16 * TT)
                squares(x_in[:, t, :], x_sc[:, t, :], ssq[:, t:t + 1], norm_squared)
            hi(0)
            act.wait_ge(cols_made, 1)
            norm_hi_chunks("norm_mix_g", 0)
            hi(1)
            act.wait_ge(lam_summed, 1)
            nc.scalar.activation(lexp, lsum, ACT.Exp).then_inc(lam_exp, 1)
            for n, tab in enumerate((rope_m, rope_d, rope2)):
                act.wait_ge(angle_ready, n + 1)
                nc.scalar.activation(tab[:, 1, :], rt[:, 2, :], ACT.Sin).then_inc(act_chain, 1)
                nc.scalar.activation(tab[:, 0, :], rt[:, 3, :], ACT.Sin, scale=-1.0, bias=halfpi
                                     ).then_inc(sincos_made, 1)
            hi(2)
            hi(3)
            act.wait_ge(bank_free, freed(2, 1))
            for t in range(TT):
                squares(lat[:, t, 0:QR], tmp[:, 0, 0:QR], ssq[:, t:t + 1], lat_squared)
                act.wait_ge(lat_squared, 2 * t + 1)
                squares(lat[:, t, QR:QR + KVR], tmp[:, 0, 0:KVR], ssq[:, 4 + t:5 + t], lat_squared)
                act.wait_ge(lat_squared, 2 * t + 2)
            hi(4)
            for m in range(2):
                gate_bank(3, m, m)
            hi(5)
            for m in range(2):
                gate_bank(4, m, 2 + m)
            for i in range(5):
                row = ROW0["mla_q_norm_g"] + i
                act.wait_ge(lat_turned, i + 1)
                nc.scalar.activation(lt_hi[:, i, :], side_bank(i), ACT.Copy, scale=col[:, row:row + 1]
                                     ).then_inc(lat_hi, 1)
            hi(6)
            for m in range(2):
                gate_bank(5, m, 4 + m)
            hi(7)
            for m in range(2):
                gate_bank(6, m, 6 + m)
            act.wait_ge(kpe_roped, 1)
            for h in range(MH):
                nc.scalar.activation(km[MN:MQ, h, :], tmp[MN:MQ, 0, :], ACT.Copy).then_inc(kpe_spread, 1)
            for u in range(U0["uq"] + 1, U0["gate_b"] + 1):
                hi(u)
                v = u - 1
                if U0["kn"] <= v < U0["mv"]:
                    for m in range(2):
                        nc.scalar.activation(km[0:MN, 4 * (v - U0["kn"]) + 2 * m + 1, :], bank(v, m)[MN:P, :],
                                             ACT.Copy).then_inc(kn_kept, 1)

            NP = 4 * MH
            for p in range(NP + 3):
                if p >= 3 and (p - 3) % 4 == 3:
                    h = (p - 3) // 4
                    rr = slice((h % 2) * MV, (h % 2) * MV + MV)
                    act.wait_ge(pv_done, p - 2)
                    nc.scalar.activation(om_hi[rr, h // 2, :], ps_o[rr, :], ACT.Copy).then_inc(o_hi_made, 1)
                if p < NP:
                    n = P * (p % 4 + 1)
                    act.wait_ge(max_made, p + 1)
                    if p >= 4:
                        act.wait_ge(t_full, p - 3)
                    nc.scalar.activation(prob[:, p % 4, 0:n], ps_s[:, p % 2, 0:n], ACT.Exp,
                                         bias=nbias[:, p % 4:p % 4 + 1], scale=MQ ** -0.5,
                                         accum_out=rsum[:, p % 4:p % 4 + 1]).then_inc(exp_made, 1)
                if 2 <= p < NP + 2:
                    q = p - 2
                    n = P * (q % 4 + 1)
                    act.wait_ge(t_full, q + 1)
                    if q >= 2:
                        act.wait_ge(pv_done, q - 1)
                    nc.scalar.activation(pt[:, q % 2, 0:n], ps_t[:, 0:n], ACT.Copy).then_inc(pt_made, 1)
                if p < NP:
                    u = U0["gate_b"] + p // 8
                    if p % 8 == 1:
                        hi(u + 1)
                    if p % 8 == 4:
                        gate_bank(u, 0, 8 + 2 * (p // 8))
                if p % 8 == 0 and p:
                    gate_bank(U0["gate_b"] + p // 8 - 1, 1, 8 + 2 * (p // 8 - 1) + 1)
            for u in range(U0["dq"] + 1, U0["mrg_m"] + 1):
                hi(u)

            NP = 4 * DH
            for p in range(NP + 6):
                if p >= 3 and (p - 3) % 4 == 3 and p - 3 < NP:
                    act.wait_ge(dPv, p - 2)
                    hd = (p - 3) // 4
                    if hd:
                        act.wait_ge(o_turned, hd)
                    nc.scalar.activation(o_sb[:, :], ps_o[:, :], ACT.Copy).then_inc(o_copied, 1)
                if p < NP:
                    n = P * (p % 4 + 1)
                    act.wait_ge(dMax, p + 1)
                    if p >= 4:
                        act.wait_ge(dT, p - 3)
                    nc.scalar.activation(prob[:, p % 4, 0:n], ps_s[:, 0, 0:n], ACT.Exp, bias=nbias[:, 2 * (p % 4):2 * (p % 4) + 1],
                                         scale=DD ** -0.5, accum_out=rsum[:, 2 * (p % 4):2 * (p % 4) + 1]).then_inc(dExp, 1)
                    if p >= 2:
                        act.wait_ge(dP, p - 1)
                    nc.scalar.activation(p2[:, p % 2, 0:n], ps_s[:, 1, 0:n], ACT.Exp, bias=nbias[:, 2 * (p % 4) + 1:2 * (p % 4) + 2],
                                         scale=DD ** -0.5, accum_out=rsum[:, 2 * (p % 4) + 1:2 * (p % 4) + 2]).then_inc(dExp, 1)
                if p >= 5 and (p - 5) % 4 == 3:
                    hd = (p - 5) // 4
                    act.wait_ge(o_turned, hd + 1)
                    nc.scalar.activation(od_hi[:, hd, :], ps_t[:, :], ACT.Copy,
                                         scale=col[:, ROW0["diff_subln_g"]:ROW0["diff_subln_g"] + 1]
                                         ).then_inc(od_hi_made, 1)
                if 2 <= p < NP + 2:
                    q = p - 2
                    n = P * (q % 4 + 1)
                    act.wait_ge(dT, q + 1)
                    if q >= 2:
                        act.wait_ge(dPv, q - 1)
                    nc.scalar.activation(pt[:, q % 2, 0:n], ps_t[:, 0:n], ACT.Copy).then_inc(dPt, 1)
                if p < NP and p % 4 == 1:
                    hi(U0["mrg_m"] + p // 4 + 1)
            for i in range(4):
                u = U0["mrg_d"] + i
                hi(u + 1)
                for m in range(2):
                    c = 2 * i + m
                    act.wait_ge(merged, c + 1)
                    nc.scalar.activation(act_hi[:, c, :], gates[:, c, :], ACT.Copy).then_inc(merged_hi, 1)
            for u in range(U0["out"] + 1, U0["ffn"]):
                hi(u)
            def hi_at(u, s, count, k, w):
                act.wait_ge(w_landed[s], count)
                act.wait_ge(w_used, u - 1)
                nc.scalar.activation(w_hi[:, s, 0:k * w], stage[:, s, 0:k * w], ACT.Copy).then_inc(w_hi_made, 1)

            uf = U0["ffn"]
            lc = {uf % 2: landed_count(uf - 2) + 16, (uf + 1) % 2: landed_count(uf - 1) + 16}

            def norm_squares(u):
                act.wait_ge(bank_free, freed(u, 1))
                for t in range(TT):
                    squares(res[:, t, :], n_sc[:, t, :], ssq[:, t:t + 1], norm_squared)

            hi_at(uf, uf % 2, lc[uf % 2], 8, 256)
            norm_squares(uf - 1)
            norm_hi_chunks("norm_ffn_g", KD)
            with act.Fori(0, KF // 2) as j:
                s0, s1 = uf % 2, (uf + 1) % 2
                hi_at(j * 2 + (uf + 1), s1, j * 16 + lc[s1], 8, 256)
                for m in range(2):
                    if m == 0:
                        act.wait_ge(first_full, j * 2 + (uf + 1))
                    else:
                        act.wait_ge(w_used, j * 2 + (uf + 1))
                    act.wait_ge(w_lo_made, j * 2 + (uf + 2))
                    nc.scalar.activation(sl[:, m, :], ps_mm[:, 2 * (uf % 2) + m, :], ACT.Silu).then_inc(bank_free_act, 1)
                with_next = j * 2 + (uf + 2)
                hi_at(with_next, s0, j * 16 + (lc[s0] + 16), 8, 256)
                for m in range(2):
                    act.wait_ge(bank_free, j * 2 + freed(uf + 1, m))
                    nc.scalar.activation(h_hi[:, bass.ds(j * 2 + m, 1), :], sl[:, m:m + 1, :], ACT.Copy
                                         ).then_inc(h_hi_made, 1)
            ud = U0["down"]
            ld = {ud % 2: landed_count(ud), (ud + 1) % 2: landed_count(ud + 1)}
            with act.Fori(0, DOWN_GROUPS // 2) as j:
                for i in range(1, 7):
                    s = (ud + i) % 2
                    kk = DOWN_K[i % 3] if i < 6 else 8
                    cnt = ld[s] + 16 * ((i - (s != ud % 2)) // 2)
                    hi_at(j * 6 + (ud + i), s, j * 48 + cnt, kk, 256)
            norm_squares(U0["q2"] - 1)
            for t in range(TT):
                act.wait_ge(x3_made, t + 1)
                squares(res[:, t, :], n_sc[:, t, :], ssq[:, t:t + 1], norm_squared)
            norm_hi_chunks("norm_g_2", 2 * KD)
            uq2 = U0["q2"]
            for u in range(uq2 + 1, U0["kv2"] + 1):
                hi(u)
            hi(U0["za"])

            def z_bank(u, m):
                n = 2 * (u - U0["za"]) + m
                if n >= 2:
                    act.wait_ge(bank_free, freed(u - 1, m))
                nc.scalar.activation(tmp[:, m, :], bank(u, m), ACT.Exp, scale=-1.0
                                     ).then_inc(z_exp, 1)

            act.wait_ge(bank_free, freed(U0["kv2"], 1))
            for e in range(2):
                for g in range(2):
                    nc.scalar.activation(kdup[e * 64:e * 64 + 64, g, :], vt2[g * 64:g * 64 + 64, 1, :], ACT.Copy
                                         ).then_inc(kdup_made, 1)
            for i in range(4):
                u = U0["za"] + i
                hi(u + 1)
                for m in range(2):
                    z_bank(u, m)
            NP = 32
            for p in range(NP + 6):
                if p < NP:
                    b = p // 8
                    act.wait_ge(max2_made, p + 1)
                    if p >= 4:
                        act.wait_ge(t2_full, p - 3)
                    for e in range(2):
                        j0 = 0 if b else P
                        j = 16 * (b % 2) + window_head(p % 8, e)
                        nc.scalar.activation(prob2[:, p % 4, e * 256 + j0:e * 256 + 256],
                                             ps_s[:, p % 2, e * 256 + j0:e * 256 + 256], ACT.Exp,
                                             bias=nm2[:, j:j + 1], scale=AD ** -0.5, accum_out=rs2[:, j:j + 1]
                                             ).then_inc(exp2_made, 1)
                if 2 <= p < NP + 2:
                    q = p - 2
                    act.wait_ge(t2_full, q + 1)
                    if q >= 2:
                        act.wait_ge(pv2_done, q - 1)
                    if q // 8:
                        nc.scalar.activation(pt2[:, q % 2, :], ps_t[:, :], ACT.Copy).then_inc(pt2_made, 1)
                    else:
                        nc.scalar.activation(pt2[:, q % 2, :].rearrange("p (e n) -> p e n", e=2)[:, :, P:2 * P],
                                             ps_t[:, :].rearrange("p (e n) -> p e n", e=2)[:, :, P:2 * P], ACT.Copy
                                             ).then_inc(pt2_made, 1)
                if p >= 2 and (p - 2) % 4 == 3 and p - 2 < NP:
                    g8 = (p - 2) // 4
                    act.wait_ge(sink_diff, g8 + 1)
                    nc.scalar.activation(esink, dsink, ACT.Exp).then_inc(sink_exp, 1)
                if p < NP:
                    u = U0["zs"] + p // 8
                    if p % 8 == 1:
                        hi(u + 1)
                    if p % 8 == 4:
                        z_bank(u, 0)
                if p % 8 == 0 and 0 < p <= NP:
                    z_bank(U0["zs"] + p // 8 - 1, 1)
            for i in range(4):
                u = U0["u2"] + i
                hi(u + 1)
                for m in range(2):
                    c = 2 * i + m
                    act.wait_ge(bank_free, freed(u - 1, m))
                    nc.scalar.activation(tmp[:, m, :], bank(u, m), ACT.Gelu
                                         ).then_inc(gelu_made, 1)
            for i in range(4):
                u = U0["vs"] + i
                hi(u + 1)
                for m in range(2):
                    nc.scalar.activation(vs[:, 2 * m:2 * m + 2, 256 * i:256 * i + 256],
                                         bank(u, m).rearrange("p (t n) -> p t n", t=2),
                                         ACT.Gelu).then_inc(gelu_made, 1)
            act.wait_ge(a_gated, 8)
            for c in range(KD):
                nc.scalar.activation(at_hi[:, c, :], gz[:, c, :], ACT.Copy).then_inc(at_hi_made, 1)
            act.wait_ge(vs_summed, 1)
            for t in range(TT):
                nc.scalar.activation(tmp[:, :, :].rearrange("p a n -> p (a n)"), vs[:, t, :], ACT.Square, bias=nmean[:, t:t + 1],
                                     accum_out=ssq[:, t:t + 1]).then_inc(vs_squared, 1)
                act.wait_ge(vs_squared, t + 1)

            def sig_bank(u, m, dst, c, row):
                nc.scalar.activation(dst[:, c, :], bank(u, m), ACT.Sigmoid,
                                     bias=col[:, row:row + 1]).then_inc(bank_free_act, 1)

            act.wait_ge(at_lo_made, KD)
            for i in range(4):
                u = U0["ga"] + i
                hi(u + 1)
                for m in range(2):
                    sig_bank(u, m, gz, 2 * i + m, ROW0["b_merge_2"] + 2 * i + m)
            for u in range(U0["att"] + 1, U0["gs"] + 1):
                hi(u)
            for g in range(8):
                act.wait_ge(mix_gated, g + 1)
                nc.scalar.activation(at_hi[:, g, :], tmp[:, g % 2, :], ACT.Copy).then_inc(sg_hi_made, 1)
            for i in range(4):
                u = U0["gs"] + i
                hi(u + 1)
                for m in range(2):
                    sig_bank(u, m, gs, 2 * i + m, ROW0["b_merge_2"] + 8 + 2 * i + m)
            for i in range(4):
                u = U0["sgo"] + i
                hi(u + 1)
                for m in range(2):
                    c = 2 * i + m
                    act.wait_ge(y_sum, c + 1)
                    nc.scalar.activation(act_hi[:, c, :], gs[:, c, :], ACT.Copy).then_inc(y_hi_made, 1)
            for u in range(U0["wo"] + 1, NU):
                hi(u)
            act.wait_ge(bank_free, freed(NU - 1, 1))
            for t in range(TT):
                squares(res[:, t, :], vs[:, t, :], ssq[:, t:t + 1], fin_squared)

        @block.vector
        def _(dve):
            V = nc.vector
            chain = [0]

            def link(ins):
                chain[0] += 1
                ins.then_inc(dve_chain, 1)
                return chain[0]

            def after(n):
                dve.wait_ge(dve_chain, n)

            def lo(u):
                s = u % 2
                src, k, w = unit_source(u)
                dve.wait_ge(w_hi_made, u + 1)
                V.tensor_tensor(w_lo[:, s, 0:k * w], stage[:, s, 0:k * w], w_hi[:, s, 0:k * w].bitcast(F32),
                                ALU.subtract).then_inc(w_lo_made, 1)

            def bank(u, m):
                g = group_of(u)
                if m == 0:
                    dve.wait_ge(first_full, g + 1)
                else:
                    dve.wait_ge(w_used, u + 1)
                return ps_mm[:, 2 * (g % 2) + m, :]

            def rsqrt(n, scale):
                v, y, t = var[:, 0:n], rstd[:, 0:n], nt1[:, 0:n]
                after(link(V.tensor_scalar(v, ssq[:, 0:n], scale, EPS, ALU.mult, ALU.add)))
                after(link(V.tensor_scalar(seed[:, 0:n].bitcast(I32), v.bitcast(I32), 1, None,
                                           ALU.logical_shift_right)))
                after(link(V.tensor_scalar(y.bitcast(I32), seed[:, 0:n].bitcast(I32), -1.0, float(0x5f3759df),
                                           ALU.mult, ALU.add)))
                for _ in range(4):
                    after(link(V.tensor_tensor(t, y, y, ALU.mult)))
                    after(link(V.scalar_tensor_tensor(out=t, in0=t, scalar=-0.5, in1=v, op0=ALU.mult, op1=ALU.mult)))
                    last = link(V.scalar_tensor_tensor(out=y, in0=t, scalar=1.5, in1=y, op0=ALU.add, op1=ALU.mult))
                    after(last)

            def norm_lo_chunks(row, base):
                for k in range(KD):
                    dve.wait_ge(norm_hi, base + k + 1)
                    V.scalar_tensor_tensor(out=act_lo[:, k, :], in0=side_bank(k),
                                           scalar=col[:, ROW0[row] + k:ROW0[row] + k + 1],
                                           in1=act_hi[:, k, :].bitcast(F32), op0=ALU.mult, op1=ALU.subtract
                                           ).then_inc(norm_lo, 1)

            def token_rows(ap, w):
                return ap[:, 0:2 * w].rearrange("p (t n) -> p t n", t=2)

            dve.wait_ge(ident_made, 1)
            link(V.tensor_copy(ident_r[:, :], ident[:, :]))
            dve.wait_ge(consts_made, 5)
            link(V.tensor_copy(causal_r[:, :], tmp[:, 0, 0:P]))
            after(link(V.tensor_copy(window_r[:, :, :], tmp[:, 1, :].rearrange("p (e n) -> p e n", e=2))))
            dve.wait_ge(cols_turned, 1)
            after(link(V.tensor_copy(col[:, :], ps_t[:, 0:NROWS])))
            after(link(V.tensor_scalar(col[:, ROW0["diff_subln_g"]:ROW0["diff_subln_g"] + 1],
                                       col[:, ROW0["diff_subln_g"]:ROW0["diff_subln_g"] + 1], 1.0 - LAMBDA_INIT, None,
                                       ALU.mult)))
            V.tensor_scalar(ncol[:, :], col[:, :], -1.0, None, ALU.mult).then_inc(cols_made, 1)
            dve.wait_ge(norm_squared, TT)
            rsqrt(TT, 1.0 / D)
            for t in range(TT):
                V.tensor_scalar(x_sc[:, t, :], x_in[:, t, :], rstd[:, t:t + 1], None, ALU.mult
                                ).then_inc(norm_scaled, 1)
            lo(0)
            norm_lo_chunks("norm_mix_g", 0)
            dve.wait_ge(lam_landed, 64)
            lt = lamv[:, :, :].rearrange("p (a b) n -> p a b n", b=2)
            after(link(V.tensor_tensor(lt[:, :, 0, :], lt[:, :, 0, :], lt[:, :, 1, :], ALU.mult)))
            V.tensor_reduce(lsum, lt[:, :, 0, :], AX.X, ALU.add).then_inc(lam_summed, 1)
            lo(1)

            def angles(n, table_row, pos):
                two_pi = 2.0 * math.pi
                c1 = 6.28125
                c2 = math.floor((two_pi - c1) * 2 ** 17) / 2 ** 17
                c3 = math.floor((two_pi - c1 - c2) * 2 ** 26) / 2 ** 26
                c4 = two_pi - c1 - c2 - c3
                magic = 1.5 * 2 ** 23
                if n >= 1:
                    dve.wait_ge(sincos_made, n)
                ang, kk, r, ar = rt[:, 0, :], rt[:, 1, :], rt[:, 2, :], rt[:, 3, :]
                after(link(V.tensor_scalar(ang, pos, freq[:, table_row:table_row + 1], None, ALU.mult)))
                after(link(V.tensor_scalar(kk, ang, 1.0 / two_pi, magic, ALU.mult, ALU.add)))
                after(link(V.tensor_scalar(kk, kk, magic, None, ALU.subtract)))
                prev = ang
                for c in (c1, c2, c3, c4):
                    after(link(V.scalar_tensor_tensor(out=r, in0=kk, scalar=-c, in1=prev, op0=ALU.mult, op1=ALU.add)))
                    prev = r
                after(link(V.tensor_scalar(r, r, 3.1415925, -3.1415925, ALU.min, ALU.max)))
                V.scalar_tensor_tensor(out=ar, in0=r, scalar=-1.0, in1=r, op0=ALU.mult, op1=ALU.max
                                       ).then_inc(angle_ready, 1)

            dve.wait_ge(pos_landed, 16)
            dve.wait_ge(freq_landed, 16)
            after(link(V.tensor_copy(pos_f[:, 0, :], pos_i[:, :])))
            angles(0, 0, pos_f[:, 0, :])
            dve.wait_ge(lam_exp, 1)
            after(link(V.tensor_tensor(neglam, lexp[:, 1:2], lexp[:, 0:1], ALU.subtract)))
            link(V.tensor_scalar(neglam, neglam, LAMBDA_INIT, None, ALU.subtract))
            angles(1, 1, pos_f[:, 0, :])
            dve.wait_ge(iota_made, 1)
            after(link(V.tensor_copy(pos_f[:, 1, :], pos_i2[:, :])))
            angles(2, 1, pos_f[:, 1, :])

            dve.wait_ge(sincos_made, 3)
            for u in range(3):
                w = 256 if u < 2 else LAT - 512
                if u >= 1:
                    lo(u + 1)
                for m in range(2):
                    V.tensor_copy(lat[:, 2 * m:2 * m + 2, 256 * u:256 * u + w], token_rows(bank(u, m), w)
                                  ).then_inc(bank_free, 1)
            dve.wait_ge(lat_squared, 8)
            after(link(V.tensor_scalar(ssq[:, 0:4], ssq[:, 0:4], KVR / QR, None, ALU.mult)))
            rsqrt(8, 1.0 / KVR)
            for t in range(TT):
                V.tensor_scalar(lat[:, t, 0:QR], lat[:, t, 0:QR], rstd[:, t:t + 1], None, ALU.mult
                                ).then_inc(lat_scaled, 1)
                V.tensor_scalar(lat[:, t, QR:QR + KVR], lat[:, t, QR:QR + KVR], rstd[:, 4 + t:5 + t], None, ALU.mult
                                ).then_inc(lat_scaled, 1)
            lo(4)

            def gate_bank(u, m, c, n):
                dve.wait_ge(gate_exp, n + 1)
                after(link(V.tensor_scalar(gates[:, c, :], gates[:, c, :], 1.0, None, ALU.add)))
                V.reciprocal(gates[:, c, :], gates[:, c, :]).then_inc(bank_free, 1)

            for m in range(2):
                gate_bank(3, m, m, m)
            lo(5)
            for m in range(2):
                gate_bank(4, m, 2 + m, 2 + m)
            for i in range(5):
                row = ROW0["mla_q_norm_g"] + i
                dve.wait_ge(lat_hi, i + 1)
                V.scalar_tensor_tensor(out=lt_lo[:, i, :], in0=side_bank(i), scalar=col[:, row:row + 1],
                                       in1=lt_hi[:, i, :].bitcast(F32), op0=ALU.mult, op1=ALU.subtract
                                       ).then_inc(lat_lo, 1)
            swap16 = [i ^ 16 for i in range(32)]
            swap8 = [i ^ 8 if i < 16 else i for i in range(32)]

            dve.wait_ge(lat_turned, 6)
            rr = slice(MN, MQ)
            src = side_bank(5)[MN:MQ, :]
            t = tmp[rr, 1, :]
            after(link(V.stream_shuffle(t, src, swap16)))
            after(link(V.tensor_tensor(t, t, rope_m[rr, 1, :], ALU.mult)))
            after(link(V.tensor_tensor(tmp[rr, 0, :], src, rope_m[rr, 0, :], ALU.mult)))
            V.tensor_tensor(tmp[rr, 0, :], tmp[rr, 0, :], t, ALU.add).then_inc(kpe_roped, 1)
            lo(6)
            for m in range(2):
                gate_bank(5, m, 4 + m, 4 + m)
            lo(7)
            for m in range(2):
                gate_bank(6, m, 6 + m, 6 + m)
            dve.wait_ge(kpe_spread, MH)

            def rope_bank(u, m, rr, dst, tab, swap):
                src = bank(u, m)[rr, :]
                t = tmp[rr, m, :]
                c0 = link(V.stream_shuffle(t, src, swap))
                V.tensor_tensor(dst, src, tab[rr, 0, :], ALU.mult).then_inc(bank_free, 1)
                after(c0)
                after(link(V.tensor_tensor(t, t, tab[rr, 1, :], ALU.mult)))
                dve.wait_ge(bank_free, freed(u, m))
                V.tensor_tensor(dst, dst, t, ALU.add).then_inc(dve_chain, 1)
                chain[0] += 1
                after(chain[0])

            for i in range(4):
                u = U0["uq"] + i
                lo(u + 1)
                for m in range(2):
                    rope_bank(u, m, slice(0, MQ), qm[0:MQ, 2 * i + m, :], rope_m, swap16)
            for i in range(2):
                u = U0["kn"] + i
                lo(u + 1)
                for m in range(2):
                    src = bank(u, m)
                    dve.wait_ge(kn_kept, 2 * i + m + 1)
                    V.tensor_copy(km[0:MN, 4 * i + 2 * m, :], src[0:MN, :]).then_inc(bank_free, 1)
            for i in range(2):
                u = U0["mv"] + i
                lo(u + 1)
                for m in range(2):
                    V.tensor_copy(vm[:, 2 * m:2 * m + 2, 256 * i:256 * i + 256], token_rows(bank(u, m), 256)
                                  ).then_inc(bank_free, 1)

            NP = 4 * MH
            for p in range(NP + 3):
                if p >= 3 and (p - 3) % 4 == 3:
                    h = (p - 3) // 4
                    rr = slice((h % 2) * MV, (h % 2) * MV + MV)
                    dve.wait_ge(o_hi_made, h + 1)
                    V.tensor_tensor(om_lo[rr, h // 2, :], ps_o[rr, :], om_hi[rr, h // 2, :].bitcast(F32), ALU.subtract
                                    ).then_inc(o_free, 1)
                if p < NP:
                    n = P * (p % 4 + 1)
                    b = p % 4
                    dve.wait_ge(s_full, p + 1)
                    if p >= 4:
                        dve.wait_ge(exp_made, p - 3)
                    after(link(V.tensor_reduce(nmx[:, b:b + 1], ps_s[:, p % 2, 0:n], AX.X, ALU.max)))
                    V.tensor_scalar(nbias[:, b:b + 1], nmx[:, b:b + 1], -(MQ ** -0.5), None, ALU.mult
                                    ).then_inc(max_made, 1)
                if 1 <= p <= NP:
                    q = p - 1
                    n = P * (q % 4 + 1)
                    b = q % 4
                    dve.wait_ge(exp_made, q + 1)
                    after(link(V.reciprocal(rinv[:, b:b + 1], rsum[:, b:b + 1])))
                    V.tensor_scalar(prob[:, b, 0:n], prob[:, b, 0:n], rinv[:, b:b + 1], None, ALU.mult
                                    ).then_inc(p_ready, 1)
                if p < NP:
                    u = U0["gate_b"] + p // 8
                    if p % 8 == 1:
                        lo(u + 1)
                    if p % 8 == 4:
                        gate_bank(u, 0, 8 + 2 * (p // 8), 8 + 2 * (p // 8))
                if p % 8 == 0 and p:
                    gate_bank(U0["gate_b"] + p // 8 - 1, 1, 8 + 2 * (p // 8) - 1, 8 + 2 * (p // 8) - 1)

            for name, dst in (("dq", dq), ("dk", dk)):
                for i in range(2):
                    u = U0[name] + i
                    lo(u + 1)
                    for m in range(2):
                        rope_bank(u, m, slice(0, P), dst[:, 2 * i + m, :], rope_d, swap8)
            for i in range(2):
                u = U0["dv"] + i
                lo(u + 1)
                for m in range(2):
                    V.tensor_copy(dv[:, 2 * m:2 * m + 2, 256 * i:256 * i + 256], token_rows(bank(u, m), 256)
                                  ).then_inc(bank_free, 1)

            def gated(u, m, c):
                V.tensor_tensor(gates[:, c, :], bank(u, m), gates[:, c, :], ALU.mult).then_inc(bank_free, 1)

            NP = 4 * DH
            for p in range(NP + 6):
                if p >= 3 and (p - 3) % 4 == 3 and p - 3 < NP:
                    dve.wait_ge(o_copied, (p - 3) // 4 + 1)
                    after(link(V.tensor_tensor(o_sq[:, :], o_sb[:, :], o_sb[:, :], ALU.mult)))
                    after(link(V.tensor_reduce(ssq[:, 0:4], o_sq[:, :].rearrange("p (t n) -> p t n", t=4), AX.X,
                                               ALU.add)))
                if p < NP:
                    n = P * (p % 4 + 1)
                    b = 2 * (p % 4)
                    dve.wait_ge(dS, p + 1)
                    if p >= 4:
                        dve.wait_ge(dExp, 2 * (p - 3))
                    after(link(V.tensor_reduce(nmx[:, b:b + 2], ps_s[:, :, 0:n], AX.X, ALU.max)))
                    V.tensor_scalar(nbias[:, b:b + 2], nmx[:, b:b + 2], -(DD ** -0.5), None, ALU.mult
                                    ).then_inc(dMax, 1)
                if 1 <= p <= NP:
                    q = p - 1
                    n = P * (q % 4 + 1)
                    b = q % 4
                    dve.wait_ge(dExp, 2 * q + 2)
                    after(link(V.reciprocal(rinv[:, 2 * b:2 * b + 2], rsum[:, 2 * b:2 * b + 2])))
                    c0 = link(V.tensor_scalar(prob[:, b, 0:n], prob[:, b, 0:n], rinv[:, 2 * b:2 * b + 1], None,
                                              ALU.mult))
                    after(link(V.tensor_scalar(rinv[:, 2 * b + 1:2 * b + 2], rinv[:, 2 * b + 1:2 * b + 2], neglam, None,
                                               ALU.mult)))
                    after(c0)
                    V.scalar_tensor_tensor(out=prob[:, b, 0:n], in0=p2[:, q % 2, 0:n],
                                           scalar=rinv[:, 2 * b + 1:2 * b + 2], in1=prob[:, b, 0:n], op0=ALU.mult,
                                           op1=ALU.add).then_inc(dP, 1)
                if p >= 3 and (p - 3) % 4 == 3 and p - 3 < NP:
                    rsqrt(4, 1.0 / DV)
                    for t in range(TT):
                        V.tensor_scalar(o_sb[:, t * P:t * P + P], o_sb[:, t * P:t * P + P], rstd[:, t:t + 1], None,
                                        ALU.mult).then_inc(o_scaled, 1)
                if p < NP:
                    u = U0["mrg_m"] + p // 4
                    if p % 4 == 1:
                        lo(u + 1)
                    if p % 4 == 2:
                        gated(u, 0, 2 * (p // 4))
                if p % 4 == 0 and 0 < p <= NP:
                    gated(U0["mrg_m"] + p // 4 - 1, 1, 2 * (p // 4 - 1) + 1)
                if p >= 5 and (p - 5) % 4 == 3:
                    hd = (p - 5) // 4
                    dve.wait_ge(od_hi_made, hd + 1)
                    V.scalar_tensor_tensor(out=od_lo[:, hd, :], in0=ps_t[:, :],
                                           scalar=col[:, ROW0["diff_subln_g"]:ROW0["diff_subln_g"] + 1],
                                           in1=od_hi[:, hd, :].bitcast(F32), op0=ALU.mult, op1=ALU.subtract
                                           ).then_inc(od_made, 1)
            for i in range(4):
                u = U0["mrg_d"] + i
                lo(u + 1)
                for m in range(2):
                    c = 2 * i + m
                    gated(u, m, 8 + c)
                    dve.wait_ge(bank_free, freed(u, m))
                    V.tensor_tensor(gates[:, c, :], gates[:, c, :], gates[:, 8 + c, :], ALU.add).then_inc(merged, 1)
                    dve.wait_ge(merged_hi, c + 1)
                    V.tensor_tensor(act_lo[:, c, :], gates[:, c, :], act_hi[:, c, :].bitcast(F32), ALU.subtract
                                    ).then_inc(merged_lo, 1)

            def add_residual(g, m, ps, n0, signal):
                r = res[:, 2 * m:2 * m + 2, bass.ds(n0, 256)]
                return V.tensor_tensor(r, token_rows(ps, 256), r, ALU.add)

            dve.wait_ge(res_landed, 16 * TT)
            for i in range(4):
                u = U0["out"] + i
                if u + 1 < U0["ffn"]:
                    lo(u + 1)
                for m in range(2):
                    add_residual(group_of(u), m, bank(u, m), 256 * i, None).then_inc(bank_free, 1)

            def lo_at(u, s, k, w):
                dve.wait_ge(w_hi_made, u + 1)
                V.tensor_tensor(w_lo[:, s, 0:k * w], stage[:, s, 0:k * w], w_hi[:, s, 0:k * w].bitcast(F32),
                                ALU.subtract).then_inc(w_lo_made, 1)

            uf = U0["ffn"]
            lo_at(uf, uf % 2, 8, 256)

            def norm_scale(base):
                rsqrt(TT, 1.0 / D)
                for t in range(TT):
                    V.tensor_scalar(n_sc[:, t, :], res[:, t, :], rstd[:, t:t + 1], None, ALU.mult
                                    ).then_inc(norm_scaled, 1)

            dve.wait_ge(norm_squared, 2 * TT)
            norm_scale(TT)
            norm_lo_chunks("norm_ffn_g", KD)
            with dve.Fori(0, KF // 2) as j:
                lo_at(j * 2 + (uf + 1), (uf + 1) % 2, 8, 256)
                lo_at(j * 2 + (uf + 2), uf % 2, 8, 256)
                for m in range(2):
                    if m == 0:
                        dve.wait_ge(first_full, j * 2 + (uf + 2))
                    else:
                        dve.wait_ge(w_used, j * 2 + (uf + 2))
                    dve.wait_ge(bank_free_act, j * 2 + (m + 1))
                    V.tensor_tensor(sl[:, m, :], ps_mm[:, 2 * ((uf + 1) % 2) + m, :], sl[:, m, :], ALU.mult
                                    ).then_inc(bank_free, 1)
                    dve.wait_ge(h_hi_made, j * 2 + (m + 1))
                    V.tensor_tensor(h_lo[:, bass.ds(j * 2 + m, 1), :], sl[:, m:m + 1, :],
                                    h_hi[:, bass.ds(j * 2 + m, 1), :].bitcast(F32), ALU.subtract
                                    ).then_inc(h_lo_made, 1)
            ud = U0["down"]
            gd = group_of(ud)
            with dve.Fori(0, DOWN_GROUPS // 2) as j:
                for gg in range(2):
                    for i in range(1, 4):
                        ii = 3 * gg + i
                        kk = DOWN_K[i % 3]
                        lo_at(j * 6 + (ud + ii), (ud + ii) % 2, kk, 256)
                    for m in range(2):
                        if m == 0:
                            dve.wait_ge(first_full, j * 2 + (gd + gg + 1))
                        else:
                            dve.wait_ge(w_used, j * 6 + (ud + 3 * gg + 3))
                        r = res[:, 2 * m:2 * m + 2, bass.ds(j * 512 + gg * 256, 256)]
                        V.tensor_tensor(r, token_rows(ps_mm[:, 2 * ((gd + gg) % 2) + m, :], 256), r, ALU.add
                                        ).then_inc(bank_free, 1)
            dve.wait_ge(norm_squared, 3 * TT)
            rsqrt(TT, 1.0 / D)
            dve.wait_ge(gf_landed, 16)
            for t in range(TT):
                V.scalar_tensor_tensor(out=res[:, t, :], in0=res[:, t, :], scalar=rstd[:, t:t + 1], in1=gf_b[:, :],
                                       op0=ALU.mult, op1=ALU.mult).then_inc(x3_made, 1)
            dve.wait_ge(norm_squared, 4 * TT)
            norm_scale(2 * TT)
            norm_lo_chunks("norm_g_2", 2 * KD)
            dve.wait_ge(norm_turned, 3 * KD)
            for i in range(4):
                u = U0["q2"] + i
                lo(u + 1)
                for m in range(2):
                    rope_bank(u, m, slice(0, P), q2[:, 2 * i + m, :], rope2, swap8)
            u = U0["kv2"]
            lo(u + 1)
            rope_bank(u, 0, slice(0, P), vt2[:, 1, :], rope2, swap8)
            V.tensor_copy(vt2[:, 0, :], bank(u, 1)).then_inc(bank_free, 1)

            def z_bank(u, m, dst, c, n):
                dve.wait_ge(z_exp, n + 1)
                after(link(V.tensor_scalar(tmp[:, m, :], tmp[:, m, :], 1.0, None, ALU.add)))
                after(link(V.reciprocal(tmp[:, m, :], tmp[:, m, :])))
                V.tensor_tensor(dst[:, c, :], bank(u, m), tmp[:, m, :], ALU.mult).then_inc(bank_free, 1)

            dve.wait_ge(v_turned, 1)
            V.tensor_copy(v2[:, :, :], ps_t[:, :].rearrange("p (t n) -> p t n", t=TT)).then_inc(v2_made, 1)
            for i in range(2):
                dve.wait_ge(wg_turned, i + 1)
                link(V.tensor_copy(wg_t[:, 4 * i:4 * i + 4, :],
                                   (ps_t, ps_o)[i][:, :].rearrange("p (g n) -> p g n", g=4)))
            after(chain[0])
            V.memset(wg_t[CHUNK:P, :, 0:CHUNK], 0.0).then_inc(wg_made, 1)
            for i in range(4):
                u = U0["za"] + i
                lo(u + 1)
                for m in range(2):
                    z_bank(u, m, gz, 2 * i + m, 2 * i + m)
            NP = 32
            dve.wait_ge(sink_landed, 16)
            for p in range(NP + 6):
                if p < NP:
                    b, i = p // 8, p % 8
                    h = window_head(i, 0)
                    j = 16 * (b % 2) + h
                    j0 = 0 if b else P
                    dve.wait_ge(s2_full, p + 1)
                    mx = nmx[:, 2 * (p % 4):2 * (p % 4) + 2]
                    after(link(V.tensor_reduce(mx, ps_s[:, p % 2, :].rearrange("p (e n) -> p e n", e=2)[:, :, j0:256],
                                               AX.X, ALU.max)))
                    after(link(V.scalar_tensor_tensor(out=m2[:, j:j + 3:2], in0=mx, scalar=AD ** -0.5,
                                                      in1=sinkb[:, h:h + 3:2], op0=ALU.mult, op1=ALU.max)))
                    V.tensor_scalar(nm2[:, j:j + 3:2], m2[:, j:j + 3:2], -1.0, None, ALU.mult).then_inc(max2_made, 1)
                if p >= 2 and (p - 2) % 4 == 3 and p - 2 < NP:
                    g8 = (p - 2) // 4
                    jj = 16 * (g8 // 2 % 2) + 8 * (g8 % 2)
                    if g8:
                        dve.wait_ge(sink_exp, g8)
                    V.tensor_tensor(dsink, sinkb[:, 8 * (g8 % 2):8 * (g8 % 2) + 8], m2[:, jj:jj + 8], ALU.subtract
                                    ).then_inc(sink_diff, 1)
                if p >= 3 and (p - 3) % 4 == 3 and p - 3 < NP:
                    g8 = (p - 3) // 4
                    jj = 16 * (g8 // 2 % 2) + 8 * (g8 % 2)
                    dve.wait_ge(sink_exp, g8 + 1)
                    after(link(V.tensor_tensor(den2, rs2[:, jj:jj + 8], esink, ALU.add)))
                    after(link(V.reciprocal(rden2, den2)))
                    dve.wait_ge(pv2_done, p - 2)
                    V.tensor_tensor(a_tok[:, g8 % 2, :].rearrange("p (h n) -> p h n", h=8),
                                    ps_o[:, :].rearrange("p (h n) -> p h n", h=8),
                                    rden2.unsqueeze(2).broadcast_to([P, 8, AD]), ALU.mult).then_inc(a_kept, 1)
                if p >= 4 and (p - 4) % 4 == 3 and p - 4 < NP:
                    g8 = (p - 4) // 4
                    b, c0 = g8 // 2, 4 * (g8 % 2)
                    dve.wait_ge(a_turned, g8 + 1)
                    g = gz[:, c0:c0 + 4, b * P:b * P + P]
                    V.tensor_tensor(g, ps_t[:, :].rearrange("p (c n) -> p c n", c=4), g, ALU.mult
                                    ).then_inc(a_gated, 1)
                if p < NP:
                    u = U0["zs"] + p // 8
                    if p % 8 == 1:
                        lo(u + 1)
                    if p % 8 == 4:
                        z_bank(u, 0, gu, 2 * (p // 8), 8 + 2 * (p // 8))
                if p % 8 == 0 and 0 < p <= NP:
                    z_bank(U0["zs"] + p // 8 - 1, 1, gu, 2 * (p // 8) - 1, 8 + 2 * (p // 8) - 1)
            for i in range(4):
                u = U0["u2"] + i
                lo(u + 1)
                for m in range(2):
                    c = 2 * i + m
                    dve.wait_ge(gelu_made, c + 1)
                    V.tensor_tensor(gu[:, c, :], tmp[:, m, :], gu[:, c, :], ALU.mult).then_inc(bank_free, 1)
            for i in range(4):
                u = U0["vs"] + i
                lo(u + 1)
                for m in range(2):
                    dve.wait_ge(gelu_made, 8 + 2 * i + m + 1)
                    V.tensor_reduce(vsum[:, 4 * i + 2 * m:4 * i + 2 * m + 2],
                                    vs[:, 2 * m:2 * m + 2, 256 * i:256 * i + 256], AX.X, ALU.add
                                    ).then_inc(bank_free, 1)
            dve.wait_ge(bank_free, freed(U0["ga"] - 1, 1))
            after(link(V.tensor_reduce(mean, vsum.rearrange("p (i t) -> p t i", i=4), AX.X, ALU.add)))
            after(link(V.tensor_scalar(mean, mean, 1.0 / D, None, ALU.mult)))
            V.tensor_scalar(nmean, mean, -1.0, None, ALU.mult).then_inc(vs_summed, 1)
            for c in range(KD):
                dve.wait_ge(at_hi_made, c + 1)
                V.tensor_tensor(at_lo[:, c, :], gz[:, c, :], at_hi[:, c, :].bitcast(F32), ALU.subtract
                                ).then_inc(at_lo_made, 1)

            def layer_norm(t):
                c0 = link(V.tensor_scalar(vs[:, t, :], vs[:, t, :], mean[:, t:t + 1], rstd[:, t:t + 1], ALU.subtract,
                                          ALU.mult))
                after(c0)
                after(link(V.tensor_tensor(vs[:, t, :], vs[:, t, :], lng_b[:, :], ALU.mult)))
                V.tensor_tensor(vs[:, t, :], vs[:, t, :], lnb_b[:, :], ALU.add).then_inc(vs_normed, 1)

            dve.wait_ge(vs_squared, TT)
            rsqrt(TT, 1.0 / D)
            dve.wait_ge(ln_landed, 32)
            for i in range(4):
                u = U0["ga"] + i
                lo(u + 1)
                layer_norm(i)
            for i in range(4):
                u = U0["att"] + i
                lo(u + 1)
                for m in range(2):
                    c = 2 * i + m
                    dve.wait_ge(bank_free_act, act_freed(group_of(U0["ga"]) + i, m))
                    V.tensor_tensor(gz[:, c, :], bank(u, m), gz[:, c, :], ALU.mult).then_inc(bank_free, 1)
            dve.wait_ge(sgb_landed, 16)
            for g in range(8):
                dve.wait_ge(mix_full, g + 1)
                tb = tmp[:, g % 2, :]
                if g >= 2:
                    dve.wait_ge(sg_lo_made, g - 1)
                after(link(V.tensor_tensor(tb.rearrange("p (b n) -> p b n", b=TT),
                                           side_bank(g).rearrange("p (b n) -> p b n", b=TT),
                                           sgb_b[:, g:g + 1, :].broadcast_to([P, TT, P]), ALU.add)))
                V.tensor_tensor(tb, tb, gu[:, g, :], ALU.mult).then_inc(mix_gated, 1)
                dve.wait_ge(sg_hi_made, g + 1)
                V.tensor_tensor(at_lo[:, g, :], tb, at_hi[:, g, :].bitcast(F32), ALU.subtract).then_inc(sg_lo_made, 1)
            for i in range(4):
                lo(U0["gs"] + i + 1)
            for i in range(4):
                u = U0["sgo"] + i
                lo(u + 1)
                for m in range(2):
                    c = 2 * i + m
                    dve.wait_ge(bank_free_act, act_freed(group_of(U0["gs"]) + i, m))
                    V.tensor_tensor(gs[:, c, :], bank(u, m), gs[:, c, :], ALU.mult).then_inc(bank_free, 1)
                    dve.wait_ge(bank_free, freed(u, m))
                    V.tensor_tensor(gs[:, c, :], gs[:, c, :], gz[:, c, :], ALU.add).then_inc(y_sum, 1)
                    dve.wait_ge(y_hi_made, c + 1)
                    V.tensor_tensor(act_lo[:, c, :], gs[:, c, :], act_hi[:, c, :].bitcast(F32), ALU.subtract
                                    ).then_inc(y_lo_made, 1)
            for i in range(4):
                u = U0["wo"] + i
                if u + 1 < NU:
                    lo(u + 1)
                for m in range(2):
                    add_residual(group_of(u), m, bank(u, m), 256 * i, None).then_inc(bank_free, 1)
            dve.wait_ge(fin_squared, TT)
            rsqrt(TT, 1.0 / D)
            dve.wait_ge(fg_landed, 16)
            for t in range(TT):
                V.scalar_tensor_tensor(out=res[:, t, :], in0=res[:, t, :], scalar=rstd[:, t:t + 1], in1=lng_b[:, :],
                                       op0=ALU.mult, op1=ALU.mult).then_inc(fin_made, 1)

        @block.tensor
        def _(pe):
            T = nc.tensor
            PASSES = ((0, 0), (0, 1), (1, 0))

            def bank_due(g, m):
                if g >= 2:
                    if g - 2 in ACT_FREED:
                        pe.wait_ge(bank_free_act, act_freed(g - 2, m))
                    else:
                        pe.wait_ge(bank_free, dve_freed(g - 2, m))

            def unit(u, s, gs_, due, kind, k, w, acts, a=0, b=None, kacts=None, start=True, stop=True, m_rows=P,
                     chunk_waits=None):
                per = 3 * k if kind == "F" else 6 * k
                b = 2 * per if b is None else b
                if a == 0:
                    pe.wait_ge(w_lo_made, u + 1)
                for n in range(a, b):
                    m, r = n // per, n % per
                    if r == 0 and start:
                        due(m)
                    if kind == "F":
                        kk, (wp, ap) = r // 3, PASSES[r % 3]
                        if chunk_waits is not None and m == 0 and r % 3 == 0:
                            pe.wait_ge(chunk_waits[0], chunk_waits[1] + kk + 1)
                        wt = slot((w_hi, w_lo)[wp], s, k, w)
                        ins = T.matmul(ps_mm[0:m_rows, 2 * gs_ + m, :], wt[:, kk, m * m_rows:(m + 1) * m_rows],
                                       acts[ap][:, kk, :], start=(r == 0), stop=(r == per - 1))
                    else:
                        tt, r2 = r // (3 * k), r % (3 * k)
                        kk, (wp, ap) = r2 // 3, PASSES[r2 % 3]
                        if chunk_waits is not None and n < 3 * k and r % 3 == 0:
                            pe.wait_ge(chunk_waits[0], chunk_waits[1] + kk + 1)
                        t = 2 * m + tt
                        wt = slot((w_hi, w_lo)[wp], s, k, w)
                        k0 = kacts or 0
                        first = r == 0 if kacts is not None else r2 == 0
                        ins = T.matmul(ps_mm[:, 2 * gs_ + m, tt * w:(tt + 1) * w],
                                       acts[ap][:, k0 + kk, t * P:(t + 1) * P], wt[:, kk, :],
                                       start=first and start, stop=(r2 == 3 * k - 1) and stop,
                                       skip_group_check=kacts is not None)
                    if n == 2 * per - 1:
                        ins.then_inc(w_used, 1)
                    elif n == per - 1 and stop:
                        ins.then_inc(first_full, 1)

            acts_x = (act_hi, act_lo)

            def straight(u, kind, acts, a=0, b=None, m_rows=P, chunk_waits=None):
                src, k, w = unit_source(u)
                g = group_of(u)
                unit(u, u % 2, g % 2, lambda m: bank_due(g, m), kind, k, w, acts, a, b, m_rows=m_rows, chunk_waits=chunk_waits)

            def turn_chunks(src, scaled_due, base):
                pe.wait_ge(norm_scaled, scaled_due)
                for k in range(KD):
                    if k >= 4:
                        pe.wait_ge(norm_lo, base + k - 3)
                    for t in range(TT):
                        ins = T.transpose(side_bank(k)[:, t * P:(t + 1) * P], src[:, t, k * P:(k + 1) * P], ident[:, :])
                    ins.then_inc(norm_turned, 1)

            pe.wait_ge(ident_made, 1)
            pe.wait_ge(rows_landed, 16 * len(ROWS))
            T.transpose(ps_t[:, 0:NROWS], rows[0:NROWS, :], ident[0:NROWS, 0:NROWS]).then_inc(cols_turned, 1)
            pe.wait_ge(cols_made, 1)
            turn_chunks(x_sc, TT, 0)
            for u in range(3):
                straight(u, "T", acts_x, chunk_waits=(norm_lo, 0) if u == 0 else None)
            straight(3, "F", acts_x)
            straight(4, "F", acts_x)
            pe.wait_ge(lat_scaled, 2 * TT)
            for i in range(6):
                if i >= 4:
                    pe.wait_ge(lat_lo, i - 3)
                for t in range(TT):
                    if i < 5:
                        ins = T.transpose(side_bank(i)[:, t * P:(t + 1) * P], lat[:, t, i * P:(i + 1) * P], ident[:, :])
                    else:
                        ins = T.transpose(side_bank(i)[0:MQ, t * P:(t + 1) * P], lat[:, t, LAT - MQ:LAT], ident[:, :])
                ins.then_inc(lat_turned, 1)
            straight(5, "F", acts_x)
            straight(6, "F", acts_x)
            lat_q = (lt_hi[:, 0:3, :], lt_lo[:, 0:3, :])
            lat_kv = (lt_hi[:, 3:5, :], lt_lo[:, 3:5, :])
            pe.wait_ge(lat_lo, 5)
            for i in range(4):
                straight(U0["uq"] + i, "F", lat_q, m_rows=MQ)
            for i in range(2):
                straight(U0["kn"] + i, "F", lat_kv)
            for i in range(2):
                straight(U0["mv"] + i, "T", lat_kv)

            pe.wait_ge(bank_free, freed(U0["gate_b"] - 1, 1))
            pe.wait_ge(kpe_spread, MH)
            NP = 4 * MH
            for p in range(NP + 2):
                if p < NP:
                    h, t = p // 4, p % 4
                    n = P * (t + 1)
                    if p >= 2:
                        pe.wait_ge(exp_made, p - 1)
                    sb_ = ps_s[:, p % 2, :]
                    T.matmul(sb_[:, 0:n], qm[0:MQ, h, t * P:(t + 1) * P], km[0:MQ, h, 0:n], start=True, stop=False)
                    T.matmul(sb_[:, n - P:n], ident_r[:, :], causal_r[:, :], start=False, stop=True
                             ).then_inc(s_full, 1)
                if p >= 2:
                    q = p - 2
                    t = q % 4
                    pe.wait_ge(p_ready, q + 1)
                    if q >= 1:
                        pe.wait_ge(pt_made, q)
                    for j in range(t + 1):
                        ins = T.transpose(ps_t[:, j * P:(j + 1) * P], prob[:, q % 4, j * P:(j + 1) * P], ident[:, :])
                    ins.then_inc(t_full, 1)
                if p < NP:
                    straight(U0["gate_b"] + p // 8, "F", acts_x, 6 * (p % 8), 6 * (p % 8) + 6)
                if p >= 2:
                    q = p - 2
                    h, t = q // 4, q % 4
                    pe.wait_ge(pt_made, q + 1)
                    if t == 0 and h:
                        pe.wait_ge(o_free, h)
                    rr = slice((h % 2) * MV, (h % 2) * MV + MV)
                    for j in range(t + 1):
                        ins = T.matmul(ps_o[rr, t * P:(t + 1) * P], vm[:, j, h * MV:(h + 1) * MV],
                                       pt[:, q % 2, j * P:(j + 1) * P], start=(j == 0), stop=(j == t))
                    ins.then_inc(pv_done, 1)
            for name, kind in (("dq", "F"), ("dk", "F"), ("dv", "T")):
                for i in range(2):
                    straight(U0[name] + i, kind, acts_x)

            pe.wait_ge(bank_free, freed(U0["mrg_m"] - 1, 1))
            pe.wait_ge(o_free, MH)
            om = (om_hi, om_lo)
            NP = 4 * DH
            for p in range(NP + 5):
                if p < NP:
                    h, t = p // 4, p % 4
                    n = P * (t + 1)
                    if p >= 1:
                        pe.wait_ge(dExp, 2 * p)
                    for e in range(2):
                        rr = slice(e * DD, e * DD + DD)
                        T.matmul(ps_s[:, e, 0:n], dq[rr, h, t * P:(t + 1) * P], dk[rr, h, 0:n], start=True, stop=False)
                        ins = T.matmul(ps_s[:, e, n - P:n], ident_r[:, :], causal_r[:, :], start=False, stop=True)
                    ins.then_inc(dS, 1)
                if 2 <= p < NP + 2:
                    q = p - 2
                    t = q % 4
                    pe.wait_ge(dP, q + 1)
                    if q >= 1:
                        pe.wait_ge(dPt, q)
                    if q >= 6 and (q - 2) % 4 == 0:
                        pe.wait_ge(od_made, (q - 2) // 4)
                    for j in range(t + 1):
                        ins = T.transpose(ps_t[:, j * P:(j + 1) * P], prob[:, q % 4, j * P:(j + 1) * P], ident[:, :])
                    ins.then_inc(dT, 1)
                if p < NP:
                    straight(U0["mrg_m"] + p // 4, "F", om, 6 * (p % 4), 6 * (p % 4) + 6)
                if 2 <= p < NP + 2:
                    q = p - 2
                    h, t = q // 4, q % 4
                    pe.wait_ge(dPt, q + 1)
                    if t == 0 and h:
                        pe.wait_ge(o_copied, h)
                    for j in range(t + 1):
                        ins = T.matmul(ps_o[:, t * P:(t + 1) * P], pt[:, q % 2, j * P:(j + 1) * P],
                                       dv[:, j, h * DV:(h + 1) * DV], start=(j == 0), stop=(j == t))
                    ins.then_inc(dPv, 1)
                if p >= 4 and (p - 4) % 4 == 3:
                    hd = (p - 4) // 4
                    pe.wait_ge(o_scaled, 4 * hd + 4)
                    pe.wait_ge(dPt, min(p - 1, NP))
                    for t in range(TT):
                        ins = T.transpose(ps_t[:, t * P:(t + 1) * P], o_sb[:, t * P:(t + 1) * P], ident[:, :])
                    ins.then_inc(o_turned, 1)
            pe.wait_ge(od_made, DH)
            for i in range(4):
                straight(U0["mrg_d"] + i, "F", (od_hi, od_lo))
            for i in range(4):
                straight(U0["out"] + i, "T", acts_x, chunk_waits=(merged_lo, 0) if i == 0 else None)
            turn_chunks(n_sc, 2 * TT, KD)
            uf = U0["ffn"]
            for h in range(2):
                unit(uf + h, (uf + h) % 2, (uf + h) % 2, lambda m: bank_due(uf + h, m), "F", 8, 256, acts_x,
                     chunk_waits=(norm_lo, KD) if h == 0 else None)
            with pe.Fori(1, KF // 2) as j:
                for h in range(2):
                    def due(m):
                        if h == 0:
                            pe.wait_ge(bank_free_act, j * 2 + (m - 1))
                        else:
                            pe.wait_ge(bank_free, j * 2 + (freed(uf + 1, m) - 2))
                    unit(j * 2 + (uf + h), (uf + h) % 2, (uf + h) % 2, due, "F", 8, 256, acts_x)
            pe.wait_ge(h_lo_made, KF)
            ud = U0["down"]
            gd = group_of(ud)
            with pe.Fori(0, DOWN_GROUPS // 2) as j:
                for gg in range(2):
                    for i in range(3):
                        n = ud + 3 * gg + i
                        def due(m):
                            pe.wait_ge(bank_free, j * 4 + (dve_freed(gd, m) + 2 * gg - 4))
                        unit(j * 6 + n, n % 2, (gd + gg) % 2, due, "T", DOWN_K[i], 256, (h_hi, h_lo),
                             kacts=sum(DOWN_K[:i]), start=(i == 0), stop=(i == 2))
            turn_chunks(n_sc, 3 * TT, 2 * KD)
            for i in range(4):
                straight(U0["q2"] + i, "F", acts_x, chunk_waits=(norm_lo, 2 * KD) if i == 0 else None)
            straight(U0["kv2"], "F", acts_x)
            straight(U0["za"], "F", acts_x)
            pe.wait_ge(bank_free, freed(U0["kv2"], 1))
            for t in range(TT):
                ins = T.transpose(ps_t[:, t * P:(t + 1) * P], vt2[:, 0, t * P:(t + 1) * P], ident[:, :])
            ins.then_inc(v_turned, 1)
            pe.wait_ge(wg_landed, 16)
            pe.wait_ge(v2_made, 1)
            for i in range(2):
                for g in range(4):
                    ins = T.transpose((ps_t, ps_o)[i][:, g * P:(g + 1) * P], wg_in[:, 4 * i + g, :], ident[:, :])
                ins.then_inc(wg_turned, 1)
            for i in range(1, 4):
                straight(U0["za"] + i, "F", acts_x)
            pe.wait_ge(kdup_made, 4)
            pe.wait_ge(wg_made, 1)
            NP = 32
            for p in range(NP + 4):
                if p < NP:
                    b, i = p // 8, p % 8
                    if p >= 2:
                        pe.wait_ge(exp2_made, 2 * (p - 1))
                    T.matmul(ps_s[:, p % 2, :], ident_r[:, :], window_r[:, :, :].rearrange("p e n -> p (e n)"),
                             start=True, stop=False)
                    j0 = 0 if b else P
                    k0 = (b - 1) * P if b else 0
                    rr = slice((i % 2) * AD, (i % 2) * AD + AD)
                    for e in range(2):
                        ins = T.matmul(ps_s[:, p % 2, e * 256 + j0:e * 256 + 256],
                                       q2[rr, 2 * (i // 2) + e, b * P:(b + 1) * P],
                                       kdup[rr, i // 4, k0:(b + 1) * P], start=False, stop=(e == 1))
                    ins.then_inc(s2_full, 1)
                if 2 <= p < NP + 2:
                    q = p - 2
                    pe.wait_ge(exp2_made, 2 * (q + 1))
                    if q >= 1:
                        pe.wait_ge(pt2_made, q)
                    if q >= 5 and (q - 5) % 4 == 0:
                        pe.wait_ge(a_gated, (q - 5) // 4 + 1)
                    for e in range(2):
                        for kb in range(0 if q // 8 else 1, 2):
                            c = (2 * e + kb) * P
                            ins = T.transpose(ps_t[:, c:c + P], prob2[:, q % 4, c:c + P], ident[:, :])
                    ins.then_inc(t2_full, 1)
                if p < NP:
                    straight(U0["zs"] + p // 8, "F", acts_x, 6 * (p % 8), 6 * (p % 8) + 6)
                if 2 <= p < NP + 2:
                    q = p - 2
                    b, i = q // 8, q % 8
                    pe.wait_ge(pt2_made, q + 1)
                    if q % 4 == 0 and q:
                        pe.wait_ge(a_kept, q // 4)
                    for e in range(2):
                        o = window_head(i % 4, e) * AD
                        for kb in range(0 if b else 1, 2):
                            c = (2 * e + kb) * P
                            ins = T.matmul(ps_o[:, o:o + AD], pt2[:, q % 2, c:c + P],
                                           v2[:, b - 1 + kb, (i // 4) * AD:(i // 4 + 1) * AD],
                                           start=(kb == (0 if b else 1)), stop=(kb == 1))
                    ins.then_inc(pv2_done, 1)
                if p >= 3 and (p - 3) % 4 == 3 and p - 3 < NP:
                    g8 = (p - 3) // 4
                    pe.wait_ge(a_kept, g8 + 1)
                    pe.wait_ge(pt2_made, min(p - 1, NP))
                    for c in range(4):
                        ins = T.transpose(ps_t[:, c * P:(c + 1) * P], a_tok[:, g8 % 2, c * P:(c + 1) * P], ident[:, :])
                    ins.then_inc(a_turned, 1)
            for i in range(4):
                straight(U0["u2"] + i, "F", acts_x)
            for i in range(4):
                straight(U0["vs"] + i, "T", acts_x)
            for i in range(4):
                straight(U0["ga"] + i, "F", acts_x)
            pe.wait_ge(at_lo_made, KD)
            for i in range(4):
                straight(U0["att"] + i, "F", (at_hi, at_lo))
            pe.wait_ge(vs_normed, TT)
            for g in range(8):
                if g >= 4:
                    pe.wait_ge(sg_lo_made, g - 3)
                for b in range(TT):
                    ins = T.matmul(side_bank(g)[:, b * P:(b + 1) * P], vs[:, b, g * P:(g + 1) * P], wg_t[:, g, :],
                                   start=True, stop=True)
                ins.then_inc(mix_full, 1)
            for i in range(4):
                straight(U0["gs"] + i, "F", acts_x)
            pe.wait_ge(sg_lo_made, 8)
            for i in range(4):
                straight(U0["sgo"] + i, "F", (at_hi, at_lo))
            for i in range(4):
                straight(U0["wo"] + i, "T", acts_x, chunk_waits=(y_lo_made, 0) if i == 0 else None)


_INS = ["x", "positions", "norm_mix_g", "w_in", "b_gate", "mla_q_norm_g", "mla_w_uq", "mla_kv_norm_g", "mla_w_ukv",
        "diff_lambda_q1", "diff_lambda_k1", "diff_lambda_q2", "diff_lambda_k2", "diff_subln_g", "w_branch_mla",
        "w_branch_diff", "w_out", "norm_ffn_g", "w_ffn_gate", "w_ffn_up", "w_ffn_down", "norm_final_g", "norm_g_2",
        "w_in_2", "b_merge_2", "att_sinks_2", "sg_w_2", "sg_b_2", "sg_ln_g_2", "sg_ln_b_2", "w_att_out_2",
        "w_sg_out_2", "w_o_2", "final_g_2"]


def rope_frequencies():
    import numpy as np

    f = np.zeros((P, 2), np.float32)
    theta = np.float64(500000.0)
    for i in range(MR // 2):
        w = np.float32(theta ** (-2.0 * i / MR))
        f[MN + i, 0], f[MN + MR // 2 + i, 0] = -w, w
    rot = DD // 4
    for i in range(rot // 2):
        w = np.float32(theta ** (-2.0 * i / rot))
        for r in (0, DD):
            f[r + i, 1], f[r + rot // 2 + i, 1] = -w, w
    return f


def kernel(**inputs):
    import numpy as np
    import concourse.bacc as bacc
    from concourse.bass_utils import run_bass_kernel_spmd

    nc = bacc.Bacc("TRN2", target_bir_lowering=False, num_devices=1)
    arrays, aps = {}, {}
    for name in _INS:
        a = np.ascontiguousarray(inputs[name])
        arrays[f"in_{name}"] = a
        aps[name] = nc.dram_tensor(f"in_{name}", a.shape, mybir.dt.from_np(a.dtype), kind="ExternalInput").ap()
    arrays["rope_freq"] = rope_frequencies()
    aps["rope_freq"] = nc.dram_tensor("rope_freq", (P, 2), F32, kind="ExternalInput").ap()
    aps["out"] = nc.dram_tensor("out", (1, S, D), F32, kind="ExternalOutput").ap()
    build(nc, aps)
    r = run_bass_kernel_spmd(nc, [arrays], core_ids=[0])
    return r.results[0]["out"]
```

```python
import math
from contextlib import ExitStack

import concourse.bass as bass
from concourse import mybir

ALU = mybir.AluOpType
ACT = mybir.ActivationFunctionType
AX = mybir.AxisListType
F32 = mybir.dt.float32
F32R = mybir.dt.float32r
I32 = mybir.dt.int32

P = 128
S = 512
TT = S // P
D = 1024
KD = D // P
UNIT = 2048
EPS = 1e-6
NEG = -1e30

MH, MN, MR, MV = 8, 64, 32, 64
MQ = MN + MR
QR, KVR = 384, 256
LAT = QR + KVR + MR
DH, DD, DV = 4, 64, 128
FF = 2816
KF = FF // P
LAMBDA_INIT = 0.8 - 0.6 * math.exp(0.0)
AH, AG, AD = 16, 2, 64
CHUNK = 64

ROWS = [("norm_mix_g", 8), ("b_gate", 16), ("mla_q_norm_g", 3), ("mla_kv_norm_g", 2), ("diff_subln_g", 1),
        ("norm_ffn_g", 8), ("norm_g_2", 8), ("b_merge_2", 16)]
ROW0 = {}
for _n, _c in ROWS:
    ROW0[_n] = sum(c for _, c in ROWS[:len(ROW0)])
NROWS = sum(c for _, c in ROWS)

COUNTS = [("lat", 3), ("gate_a", 4), ("qn", 2), ("qp", 1), ("kn", 2), ("mv", 2), ("gate_b", 4), ("dq", 2), ("dk", 2),
          ("dv", 2), ("mrg_m", 4), ("mrg_d", 4), ("out", 4), ("ffn", 22), ("down", 12),
          ("q2", 4), ("kv2", 1), ("za", 4), ("zs", 4), ("u2", 4), ("vs", 4), ("ga", 4), ("att", 4), ("gs", 4),
          ("sgo", 4), ("wo", 4)]
U0 = {}
_u = 0
for _n, _c in COUNTS:
    U0[_n] = _u
    _u += _c
NU = _u
DOWN_GROUPS = 4
DOWN_K = (8, 8, 6)


def group_of(u):
    d = U0["down"]
    if u < d:
        return u
    if u < d + 12:
        return d + (u - d) // 3
    return u - 12 + DOWN_GROUPS


def window_head(i, e):
    return 4 * (i // 2) + i % 2 + 2 * e


ACT_FREED = ([group_of(U0[n]) + i for n in ("gate_a", "gate_b") for i in range(4)]
             + [group_of(U0["ffn"]) + 2 * j for j in range(KF // 2)]
             + [group_of(U0[n]) + i for n in ("za", "ga", "gs") for i in range(4)])

LAG = 3


class Stream:

    def __init__(self, name, units, per, weights):
        self.name, self.per = name, per
        self.cuts = [units * per * sum(weights[:p]) // sum(weights) for p in range(len(weights) + 1)]

        def step_of(n):
            return next(p for p in range(len(weights)) if self.cuts[p + 1] > n)

        self.banks = {}
        self.starts = {}
        for i in range(units):
            self.starts[step_of(i * per)] = U0[name] + i
            for m in range(2):
                self.banks.setdefault(step_of(i * per + (m + 1) * per // 2 - 1) + 1, []).append((i, m))

    def started(self, p):
        return self.starts.get(p)


MLA_STEPS = 4 * MH + LAG
MLA_STREAM = Stream("gate_b", 4, 48, [0, 1, 1] + [2] * (MLA_STEPS - 3))
DIFF_STEPS = 4 * DH + LAG + 4
DIFF_STREAM = Stream("mrg_m", 4, 24, [2] * 4 * DH + [4] * (DIFF_STEPS - 4 * DH))
WIN_PIECES = 32
WIN_STEPS = WIN_PIECES + LAG + 2
WIN_STREAM = Stream("zs", 4, 48, [1] * WIN_STEPS)


def act_freed(g, m):
    return 2 * sum(a < g for a in ACT_FREED) + m + 1


def dve_freed(g, m):
    return 2 * (g - sum(a < g for a in ACT_FREED)) + m + 1


def freed(u, m):
    return dve_freed(group_of(u), m)


def build(nc, A):
    with ExitStack() as ctx:
        def sem(name):
            return ctx.enter_context(nc.semaphore(name))

        def keep(name, shape, dt=F32):
            return ctx.enter_context(nc.sbuf_tensor(name, shape, dt))

        def overlay(*tensors):
            with ExitStack() as sub:
                return [sub.enter_context(nc.sbuf_tensor(n, s, d)) for n, s, d in tensors]

        stage = keep("stage", [P, 2, UNIT])
        w_hi = keep("w_hi", [P, 2, UNIT], F32R)
        w_lo = keep("w_lo", [P, 2, UNIT], F32R)
        act_hi = keep("act_hi", [P, KD, S], F32R)
        act_lo = keep("act_lo", [P, KD, S], F32R)
        ident = keep("ident", [P, P])
        ident_r = keep("ident_r", [P, P], F32R)
        causal_r = keep("causal_r", [P, P], F32R)
        window_r = keep("window_r", [P, 2, 2 * P], F32R)
        col = keep("col", [P, NROWS])
        hcol = keep("hcol", [P, NROWS])
        freq = keep("freq", [P, 2])
        small = keep("small", [P, 384])
        rope2 = keep("rope2", [P, 2, S])
        tmp = keep("tmp", [P, 2, S])

        (rope_m, rope_d, pt) = overlay(("rope_m", [P, 2, S], F32), ("rope_d", [P, 2, S], F32), ("pt", [P, 2, S], F32))
        (p2, o_sb, o_sq) = overlay(("p2", [P, 2, S], F32), ("o_sb", [P, S], F32), ("o_sq", [P, S], F32))
        res = keep("res", [P, TT, D])

        (x_in, x_sc, rows, lamv, pos_i, pos_i2, pos_f, rt) = overlay(
            ("x_in", [P, TT, D], F32), ("x_sc", [P, TT, D], F32), ("rows", [P, P], F32), ("lamv", [P, 4, DD], F32),
            ("pos_i", [P, S], I32), ("pos_i2", [P, S], I32), ("pos_f", [P, 2, S], F32), ("rt", [P, 4, S], F32))
        with ExitStack() as b1:
            def b1keep(name, shape, dt=F32):
                return b1.enter_context(nc.sbuf_tensor(name, shape, dt))

            gates = b1keep("gates", [P, 16, S])
            with ExitStack() as sub:
                lt_hi = sub.enter_context(nc.sbuf_tensor("lt_hi", [P, 5, S], F32R))
                lt_lo = sub.enter_context(nc.sbuf_tensor("lt_lo", [P, 5, S], F32R))
            om_hi = b1keep("om_hi", [P, 4, S], F32R)
            om_lo = b1keep("om_lo", [P, 4, S], F32R)
            prob = b1keep("prob", [P, 4, S])
            with ExitStack() as sub:
                qm, km, vm = [sub.enter_context(nc.sbuf_tensor(n, s, F32)) for n, s in (
                    ("qm", [P, MH, S]), ("km", [P, MH, S]), ("vm", [P, TT, MH * MV]))]
            with ExitStack() as sub:
                sub.enter_context(nc.sbuf_tensor("pad_lat", [P, MH, S], F32))
                lat = sub.enter_context(nc.sbuf_tensor("lat", [P, TT, LAT], F32))
            with ExitStack() as sub:
                dq, dk, dv = [sub.enter_context(nc.sbuf_tensor(n, [P, TT, S], F32)) for n in ("dq", "dk", "dv")]
                od_hi = sub.enter_context(nc.sbuf_tensor("od_hi", [P, DH, S], F32R))
                od_lo = sub.enter_context(nc.sbuf_tensor("od_lo", [P, DH, S], F32R))
        (h_hi, h_lo, sl, gf_b) = overlay(("h_hi", [P, KF, S], F32R), ("h_lo", [P, KF, S], F32R),
                                         ("sl", [P, 2, S], F32), ("gf_b", [P, D], F32))
        (n_sc,) = overlay(("n_sc", [P, TT, D], F32))
        with ExitStack() as b2:
            def b2keep(name, shape, dt=F32):
                return b2.enter_context(nc.sbuf_tensor(name, shape, dt))

            def b2share(*tensors):
                with ExitStack() as sub:
                    return [sub.enter_context(nc.sbuf_tensor(n, s, d)) for n, s, d in tensors]

            gz = b2keep("gz", [P, KD, S])
            gu = b2keep("gu", [P, KD, S])
            (q2,) = b2share(("q2", [P, KD, S], F32))
            (gs,) = b2share(("gs", [P, KD, S], F32))
            vs = b2keep("vs", [P, TT, D])
            kdup, v2, vt2, prob2, pt2, a_tok = b2share(
                ("kdup", [P, 2, S], F32), ("v2", [P, TT, P], F32), ("vt2", [P, 2, S], F32),
                ("prob2", [P, 4, S], F32), ("pt2", [P, 2, S], F32), ("a_tok", [P, 2, S], F32))
            (wg_in,) = b2share(("pad_wg", [P, 14 * S], F32), ("wg_in", [P, 8, P], F32))[1:]
            at_hi = b2keep("at_hi", [P, KD, S], F32R)
            at_lo = b2keep("at_lo", [P, KD, S], F32R)
            wg_t = b2keep("wg_t", [P, 8, P])
            sgb_b = b2keep("sgb_b", [P, 8, P])
            lng_b = b2keep("lng_b", [P, D])
            lnb_b = b2keep("lnb_b", [P, D])

        act_y = act_hi[:, :, :].bitcast(F32).rearrange("p (t a) n -> p t (a n)", t=TT)

        ps_mm = ctx.enter_context(nc.psum_tensor("ps_mm", [P, 4, S], F32))
        ps_s = ctx.enter_context(nc.psum_tensor("ps_s", [P, 2, S], F32))
        ps_t = ctx.enter_context(nc.psum_tensor("ps_t", [P, S], F32))
        ps_o = ctx.enter_context(nc.psum_tensor("ps_o", [P, S], F32))

        def side_bank(k):
            return (ps_s[:, 0, :], ps_s[:, 1, :], ps_t[:, :], ps_o[:, :])[k % 4]

        at = [0]

        def cut(n):
            at[0] += n
            assert at[0] <= 384
            return small[:, at[0] - n:at[0]]

        ssq, var, rstd, nt1 = cut(16), cut(16), cut(16), cut(16)
        part = cut(32)
        nmax, rsum, rinv = cut(8), cut(8), cut(8)
        lamt = cut(8)
        lsum = cut(2)
        lexp = cut(2)
        neglam = cut(1)
        sinkb, nsinkb, nm2, rs2 = cut(16), cut(16), cut(32), cut(32)
        dsink, esink, den2, rden2 = cut(8), cut(8), cut(8), cut(8)
        dsum = cut(16)
        drinv, mix = cut(8), cut(4)
        dssq, dvar, drstd, dnt = cut(4), cut(4), cut(4), cut(4)
        vsum, mean, nmean = cut(16), cut(4), cut(4)
        halfpi = cut(1)

        w_landed = [sem("w_landed0"), sem("w_landed1")]
        w_hi_made, w_lo_made, w_used = sem("w_hi_made"), sem("w_lo_made"), sem("w_used")
        first_full, bank_free, bank_free_act = sem("first_full"), sem("bank_free"), sem("bank_free_act")
        x_landed = [sem(f"x_landed{t}") for t in range(TT)]
        rows_landed, pos_landed, lam_landed, freq_landed, sink_landed = [
            sem(n) for n in ("rows_landed", "pos_landed", "lam_landed", "freq_landed", "sink_landed")]
        res_landed, gf_landed, wg_landed, sgb_landed, ln_landed, fg_landed, out_written = [
            sem(n) for n in ("res_landed", "gf_landed", "wg_landed", "sgb_landed", "ln_landed", "fg_landed",
                             "out_written")]
        consts_made, ident_made, cols_turned, cols_made = [
            sem(n) for n in ("consts_made", "ident_made", "cols_turned", "cols_made")]
        dve_chain, act_chain, pool_chain = sem("dve_chain"), sem("act_chain"), sem("pool_chain")
        norm_squared, norm_scaled, norm_scaled_act, rstd_made, norm_turned, norm_hi, norm_lo = [
            sem(n) for n in ("norm_squared", "norm_scaled", "norm_scaled_act", "rstd_made", "norm_turned", "norm_hi", "norm_lo")]
        iota_made = sem("iota_made")
        angle_ready, sincos_made = sem("angle_ready"), sem("sincos_made")
        lam_summed, lam_exp = sem("lam_summed"), sem("lam_exp")
        lat_kept, lat_squared, lat_scaled, lat_turned, lat_hi, lat_lo, kpe_roped, kpe_spread = [
            sem(n) for n in ("lat_kept", "lat_squared", "lat_scaled", "lat_turned", "lat_hi", "lat_lo", "kpe_roped",
                             "kpe_spread")]
        nope_kept, qp_roped, q_spread = sem("nope_kept"), sem("qp_roped"), sem("q_spread")
        qkv_kept = sem("qkv_kept")
        s_full, max_made, exp_made, p_ready, t_full, pt_made, pv_done, o_hi_made, o_free = [
            sem(n) for n in ("s_full", "max_made", "exp_made", "p_ready", "t_full", "pt_made", "pv_done", "o_hi_made",
                             "o_free")]
        drstd_made = sem("drstd_made")
        o_scaled, o_turned, od_hi_made, od_made = [sem(n) for n in ("o_scaled", "o_turned", "od_hi_made", "od_made")]
        x_gained, down_squared, y_read = sem("x_gained"), sem("down_squared"), sem("y_read")
        merged, merged_hi, merged_lo = sem("merged"), sem("merged_hi"), sem("merged_lo")
        silu_made, up_made, h_hi_made, h_lo_made = [
            sem(n) for n in ("silu_made", "up_made", "h_hi_made", "h_lo_made")]
        res_ready, x3_made = sem("res_ready"), sem("x3_made")
        kv_kept, kr_made, kdup_made, v_turned, v2_made, wg_turned, wg_made = [
            sem(n) for n in ("kv_kept", "kr_made", "kdup_made", "v_turned", "v2_made", "wg_turned", "wg_made")]
        z_tanh, sink_diff, sink_exp, a_kept, a_turned, a_gated = [
            sem(n) for n in ("z_tanh", "sink_diff", "sink_exp", "a_kept", "a_turned", "a_gated")]
        at_hi_made, at_lo_made = sem("at_hi_made"), sem("at_lo_made")
        gelu_made, vs_summed, vs_squared, vs_normed, mix_full, mix_gated, sg_hi_made, sg_lo_made = [
            sem(n) for n in ("gelu_made", "vs_summed", "vs_squared", "vs_normed", "mix_full", "mix_gated",
                             "sg_hi_made", "sg_lo_made")]
        sig_made, y_sum, y_hi_made, y_lo_made = [sem(n) for n in ("sig_made", "y_sum", "y_hi_made", "y_lo_made")]
        fin_squared, fin_made, fin_made_act = sem("fin_squared"), sem("fin_made"), sem("fin_made_act")
        exp2_made, s2_full, max2_made, t2_full, pt2_made, pv2_done = [
            sem(n) for n in ("exp2_made", "s2_full", "max2_made", "t2_full", "pt2_made", "pv2_done")]
        dS, dMax, dExp, dP, dT, dPt, dPv, dRinv, o_copied, o_squared = [
            sem(n) for n in ("d_s_full", "d_max_made", "d_exp_made", "d_p_ready", "d_t_full", "d_pt_made", "d_pv_done", "d_rinv_made",
                             "o_copied", "o_squared")]

        def chunks(ap):
            return ap.rearrange("a (k p) n -> p (a k) n", p=P)

        w_in, w_in2 = chunks(A["w_in"]), chunks(A["w_in_2"])
        w_gate, w_up, w_down = chunks(A["w_ffn_gate"]), chunks(A["w_ffn_up"]), chunks(A["w_ffn_down"])
        uq = A["mla_w_uq"].rearrange("a (k p) (h e) -> p (a k) h e", p=P, e=MQ)
        ukv = A["mla_w_ukv"].rearrange("a (k p) (h e) -> p (a k) h e", p=P, e=MN + MV)
        wbm, wbd, wout = chunks(A["w_branch_mla"]), chunks(A["w_branch_diff"]), chunks(A["w_out"])
        wao, wso, wo2 = chunks(A["w_att_out_2"]), chunks(A["w_sg_out_2"]), chunks(A["w_o_2"])
        C_DQ, C_DK, C_DV = LAT, LAT + 512, LAT + 1024
        C_G = LAT + 1536
        C2 = {"q2": 0, "kv2": 1024, "za": 1280, "u2": 2304, "vs": 3328, "zs": 4352, "ga": 5376, "gs": 6400}

        def unit_source(u):
            name = [n for n, c in COUNTS if U0[n] <= u < U0[n] + c][0]
            i = u - U0[name]
            w = 256
            c0 = 256 * i
            if name == "lat":
                w = 256 if i < 2 else LAT - 512
                return w_in[:, :, c0:c0 + w], 8, w
            if name == "gate_a":
                return w_in[:, :, C_G + c0:C_G + c0 + w], 8, w
            if name == "gate_b":
                return w_in[:, :, C_G + 1024 + c0:C_G + 1024 + c0 + w], 8, w
            if name == "qn":
                return uq[:, :, 4 * i:4 * i + 4, 0:MN], 3, 256
            if name == "qp":
                return uq[:, :, :, MN:MQ], 3, 256
            if name == "kn":
                return ukv[:, :, 4 * i:4 * i + 4, 0:MN], 2, 256
            if name == "mv":
                return ukv[:, :, 4 * i:4 * i + 4, MN:MN + MV], 2, 256
            if name in ("dq", "dk", "dv"):
                b = {"dq": C_DQ, "dk": C_DK, "dv": C_DV}[name]
                return w_in[:, :, b + c0:b + c0 + w], 8, w
            if name == "mrg_m":
                return wbm[:, :, c0:c0 + w], 4, w
            if name == "mrg_d":
                return wbd[:, :, c0:c0 + w], 4, w
            if name in ("out", "att", "sgo", "wo"):
                m = {"out": wout, "att": wao, "sgo": wso, "wo": wo2}[name]
                return m[:, :, c0:c0 + w], 8, w
            return w_in2[:, :, C2[name] + c0:C2[name] + c0 + w], 8, w

        def slot(t, s, k, w):
            return t[:, s, 0:k * w].rearrange("p (k n) -> p k n", k=k)

        block = ctx.enter_context(nc.Block())

        @block.sync
        def _(sp):
            def load(u, s, src, k, w):
                dst = slot(stage, s, k, w)
                if len(src.shape) == 4:
                    dst = dst.rearrange("p k (h e) -> p k h e", h=src.shape[2])
                    for kk in range(k):
                        sp.dma_start(dst[:, kk], src[:, kk]).then_inc(w_landed[s], 16)
                else:
                    sp.dma_start(dst, src).then_inc(w_landed[s], 16)

            def straight(u, first=False):
                if u >= 2:
                    sp.wait_ge(w_lo_made, u - 1)
                load(u, u % 2, *unit_source(u))

            xv = A["x"].rearrange("a (t p) d -> p (a t) d", p=P)
            for t in range(TT):
                sp.dma_start(x_in[:, t, :], xv[:, t, :]).then_inc(x_landed[t], 16)
            for name, n in ROWS:
                sp.dma_start(rows[ROW0[name]:ROW0[name] + n, :],
                             A[name].rearrange("a (r p) -> (a r) p", p=P)).then_inc(rows_landed, 16)
            straight(0)
            sp.dma_start(freq[:, :], A["rope_freq"]).then_inc(freq_landed, 16)
            sp.dma_start(pos_i[:, :], A["positions"].broadcast_to([P, S])).then_inc(pos_landed, 16)
            for i, name in enumerate(("diff_lambda_q1", "diff_lambda_k1", "diff_lambda_q2", "diff_lambda_k2")):
                sp.dma_start(lamv[:, i, :], A[name].broadcast_to([P, DD])).then_inc(lam_landed, 16)
            sp.dma_start(sinkb, A["att_sinks_2"].broadcast_to([P, AH])).then_inc(sink_landed, 16)
            for u in range(1, U0["out"]):
                straight(u)
            sp.wait_ge(od_made, DH)
            sp.wait_ge(dPv, 4 * DH)
            for t in range(TT):
                sp.dma_start(res[:, t, :], xv[:, t, :]).then_inc(res_landed, 16)
            for u in range(U0["out"], U0["ffn"]):
                straight(u)
            u0 = U0["ffn"]
            with sp.Fori(0, KF // 2) as j:
                for h, wv in enumerate((w_gate, w_up)):
                    lo_due = sp.snap(j * 2 + (u0 + h - 1))
                    c0 = sp.snap(j * 256)
                    sp.wait_ge(w_lo_made, lo_due)
                    s = (u0 + h) % 2
                    sp.dma_start(slot(stage, s, 8, 256), wv[:, :, bass.ds(c0, 256)]).then_inc(w_landed[s], 16)
            sp.dma_start(gf_b[:, :], A["norm_final_g"].rearrange("(a d) -> a d", a=1).broadcast_to([P, D])
                         ).then_inc(gf_landed, 16)
            u0 = U0["down"]
            with sp.Fori(0, DOWN_GROUPS // 2) as j:
                for gg in range(2):
                    c0 = sp.snap(j * 512 + gg * 256)
                    for i in range(3):
                        lo_due = sp.snap(j * 6 + (u0 + 3 * gg + i - 1))
                        sp.wait_ge(w_lo_made, lo_due)
                        s = (u0 + 3 * gg + i) % 2
                        k0 = sum(DOWN_K[:i])
                        sp.dma_start(slot(stage, s, DOWN_K[i], 256),
                                     w_down[:, k0:k0 + DOWN_K[i], bass.ds(c0, 256)]).then_inc(w_landed[s], 16)
            for u in range(U0["q2"], NU):
                if u == U0["za"] + 1:
                    sp.wait_ge(x3_made, TT)
                    sp.dma_start(wg_in[:, :, :], A["sg_w_2"].rearrange("a g i j -> i (a g) j")).then_inc(wg_landed, 16)
                    sp.dma_start(sgb_b[:, :, :].rearrange("p g i -> p (g i)"),
                                 A["sg_b_2"].rearrange("a g i -> a (g i)").broadcast_to([P, D])
                                 ).then_inc(sgb_landed, 16)
                    sp.dma_start(lng_b[:, :], A["sg_ln_g_2"].broadcast_to([P, D])).then_inc(ln_landed, 16)
                    sp.dma_start(lnb_b[:, :], A["sg_ln_b_2"].broadcast_to([P, D])).then_inc(ln_landed, 16)
                if u == U0["wo"]:
                    sp.wait_ge(vs_normed, TT)
                    sp.dma_start(lng_b[:, :], A["final_g_2"].rearrange("(a d) -> a d", a=1).broadcast_to([P, D])
                                 ).then_inc(fg_landed, 16)
                straight(u)
            ov = A["out"].rearrange("a (t p) d -> p (a t) d", p=P)
            for t in range(TT):
                sp.wait_ge(fin_made_act if t % 2 else fin_made, t // 2 + 1)
                sp.dma_start(ov[:, t, :], res[:, t, :]).then_inc(out_written, 16)
            sp.wait_ge(out_written, 16 * TT)

        def landed_count(u):
            def dmas(v):
                return 3 if U0["qn"] <= v < U0["kn"] else 2 if U0["kn"] <= v < U0["gate_b"] else 1
            return 16 * sum(dmas(v) for v in range(u % 2, u + 1, 2))

        @block.gpsimd
        def _(pool):
            pool.memset(ident[:, :], 1.0).then_inc(pool_chain, 1)
            pool.memset(tmp[:, 0, 0:P], 0.0).then_inc(pool_chain, 1)
            pool.memset(tmp[:, 1, :], 0.0).then_inc(pool_chain, 1)
            pool.memset(halfpi, math.pi / 2).then_inc(pool_chain, 1)
            pool.iota(pos_i2[:, :], pattern=[[1, S]], base=0, channel_multiplier=0).then_inc(iota_made, 1)
            pool.wait_ge(pool_chain, 4)
            pool.affine_select(out=ident[:, :], in_=ident[:, :], compare_op=ALU.is_equal, fill=0.0, base=0,
                               pattern=[[-1, P]], channel_multiplier=1).then_inc(ident_made, 1)
            pool.affine_select(out=tmp[:, 0, 0:P], in_=tmp[:, 0, 0:P], compare_op=ALU.is_ge, fill=NEG, base=0,
                               pattern=[[-1, P]], channel_multiplier=1).then_inc(consts_made, 1)
            wv = tmp[:, 1, :].rearrange("p (e n) -> p e n", e=2)
            for e in range(2):
                pool.wait_ge(consts_made, 2 * e + 1)
                pool.memset(wv[CHUNK:P, e, 0:CHUNK], NEG).then_inc(consts_made, 1)
                pool.wait_ge(consts_made, 2 * e + 2)
                pool.memset(wv[0:CHUNK, e, 2 * P - CHUNK:2 * P], NEG).then_inc(consts_made, 1)

            n_pool = 4

            def link(ins):
                ins.then_inc(pool_chain, 1)
                return 1

            G = nc.gpsimd
            for hd in range(DH):
                pool.wait_ge(o_squared, 4 * hd + 4)
                v, y, t = dvar[:, 0:4], drstd[:, 0:4], dnt[:, 0:4]
                n_pool += link(G.tensor_scalar(v, dssq[:, 0:4], 1.0 / DV, EPS, ALU.mult, ALU.add))
                pool.wait_ge(pool_chain, n_pool)
                n_pool += link(G.tensor_scalar(y.bitcast(I32), v.bitcast(I32), -0.5, float(0x5f3759df), ALU.mult, ALU.add))
                pool.wait_ge(pool_chain, n_pool)
                for step in range(3):
                    n_pool += link(G.tensor_tensor(t, y, y, ALU.mult))
                    pool.wait_ge(pool_chain, n_pool)
                    n_pool += link(G.tensor_tensor(t, t, v, ALU.mult))
                    pool.wait_ge(pool_chain, n_pool)
                    n_pool += link(G.tensor_scalar(t, t, -0.5, 1.5, ALU.mult, ALU.add))
                    pool.wait_ge(pool_chain, n_pool)
                    if step < 2:
                        n_pool += link(G.tensor_tensor(y, y, t, ALU.mult))
                        pool.wait_ge(pool_chain, n_pool)
                    else:
                        G.tensor_tensor(y, y, t, ALU.mult).then_inc(drstd_made, 1)
                        pool.wait_ge(drstd_made, hd + 1)
        @block.scalar
        def _(act):
            chain = [0]

            def hi(u):
                s = u % 2
                src, k, w = unit_source(u)
                act.wait_ge(w_landed[s], landed_count(u))
                if u >= 2:
                    act.wait_ge(w_used, u - 1)
                nc.scalar.activation(w_hi[:, s, 0:k * w], stage[:, s, 0:k * w], ACT.Copy).then_inc(w_hi_made, 1)

            def bank(u, m):
                g = group_of(u)
                if m == 0:
                    act.wait_ge(first_full, g + 1)
                else:
                    act.wait_ge(w_used, u + 1)
                return ps_mm[:, 2 * (g % 2) + m, :]

            def hi_half(u, h):
                s = u % 2
                src, k, w = unit_source(u)
                act.wait_ge(w_landed[s], landed_count(u))
                if u >= 2:
                    act.wait_ge(w_used, u - 1)
                n = k * w // 2
                ins = nc.scalar.activation(w_hi[:, s, h * n:(h + 1) * n], stage[:, s, h * n:(h + 1) * n], ACT.Copy)
                if h:
                    ins.then_inc(w_hi_made, 1)

            def squares(src, out, acc, signal):
                nc.scalar.activation(out, src, ACT.Square, accum_out=acc).then_inc(signal, 1)

            def norm_hi_chunk(row, base, k):
                act.wait_ge(norm_turned, base + k + 1)
                nc.scalar.activation(act_hi[:, k, :], side_bank(k), ACT.Copy,
                                     scale=col[:, ROW0[row] + k:ROW0[row] + k + 1]).then_inc(norm_hi, 1)

            def norm_hi_chunks(row, base):
                for k in range(KD):
                    norm_hi_chunk(row, base, k)

            def gate_bank(u, m, c):
                nc.scalar.activation(gates[:, c, :], bank(u, m), ACT.Tanh, scale=0.5,
                                     bias=hcol[:, ROW0["b_gate"] + c:ROW0["b_gate"] + c + 1]).then_inc(bank_free_act, 1)

            def scale_tile(out, src, c):
                nc.scalar.activation(out, src, ACT.Copy, scale=rstd[:, c:c + 1]).then_inc(norm_scaled_act, 1)

            def part_squares(n0, m, i, kind, src, out, signal):
                for t in (2 * m, 2 * m + 1):
                    c = 16 * kind + 4 * i + t
                    squares(src[:, t, n0:n0 + 256], out[:, 256 * (t % 2):256 * (t % 2) + 256], part[:, c:c + 1], signal)

            for t in range(TT):
                act.wait_ge(x_landed[t], 16)
                squares(x_in[:, t, :], x_sc[:, t, :], ssq[:, t:t + 1], norm_squared)
            act.wait_ge(rstd_made, 1)
            for t in (1, 3):
                scale_tile(x_sc[:, t, :], x_in[:, t, :], t)
            act.wait_ge(cols_made, 1)
            act.wait_ge(w_landed[0], landed_count(0))
            for k in range(KD):
                ins = nc.scalar.activation(w_hi[:, 0, 256 * k:256 * k + 256], stage[:, 0, 256 * k:256 * k + 256], ACT.Copy)
                if k == KD - 1:
                    ins.then_inc(w_hi_made, 1)
                norm_hi_chunk("norm_mix_g", 0, k)
            hi(1)
            act.wait_ge(lam_summed, 1)
            nc.scalar.activation(lexp, lsum, ACT.Exp).then_inc(lam_exp, 1)
            for n, tab in enumerate((rope_m, rope_d, rope2)):
                act.wait_ge(angle_ready, n + 1)
                nc.scalar.activation(tab[:, 1, :], rt[:, 2, :], ACT.Sin).then_inc(act_chain, 1)
                nc.scalar.activation(tab[:, 0, :], rt[:, 3, :], ACT.Sin, scale=-1.0, bias=halfpi
                                     ).then_inc(sincos_made, 1)
                if n < 2:
                    hi(2 + n)
            hi(4)
            act.wait_ge(bank_free, freed(2, 1))
            for t in range(TT):
                squares(lat[:, t, 0:QR], tmp[:, 0, 0:QR], ssq[:, t:t + 1], lat_squared)
                act.wait_ge(lat_squared, 2 * t + 1)
                squares(lat[:, t, QR:QR + KVR], tmp[:, 0, 0:KVR], ssq[:, 4 + t:5 + t], lat_squared)
                act.wait_ge(lat_squared, 2 * t + 2)
            for m in range(2):
                gate_bank(3, m, m)
            hi(5)
            for m in range(2):
                gate_bank(4, m, 2 + m)
            for i in range(5):
                row = ROW0["mla_q_norm_g"] + i
                act.wait_ge(lat_turned, i + 1)
                nc.scalar.activation(lt_hi[:, i, :], side_bank(i), ACT.Copy, scale=col[:, row:row + 1]
                                     ).then_inc(lat_hi, 1)
            hi(6)
            for m in range(2):
                gate_bank(5, m, 4 + m)
            hi(7)
            for m in range(2):
                gate_bank(6, m, 6 + m)
            for u in range(U0["qn"] + 1, U0["gate_b"] + 1):
                hi(u)
                v = u - 1
                if v < U0["qp"] or U0["kn"] <= v < U0["mv"]:
                    dst, i, scale = (qm, v - U0["qn"], MQ ** -0.5) if v < U0["qp"] else (km, v - U0["kn"], 1.0)
                    for m in range(2):
                        nc.scalar.activation(dst[0:MN, 4 * i + 2 * m + 1, :], bank(v, m)[MN:P, :],
                                             ACT.Copy, scale=scale).then_inc(nope_kept, 1)
                if v == U0["kn"]:
                    for h in range(MH):
                        if h % 4 == 0:
                            act.wait_ge(qp_roped, h // 4 + 1)
                        nc.scalar.activation(qm[MN:MQ, h, :], prob[32 * (h % 4):32 * (h % 4) + 32, 2 + h // 4, :],
                                             ACT.Copy).then_inc(q_spread, 1)

            NP = 4 * MH
            for p in range(MLA_STEPS + 1):
                if p > LAG and (p - LAG - 1) % 4 == 3:
                    h = (p - LAG - 1) // 4
                    rr = slice((h % 2) * MV, (h % 2) * MV + MV)
                    act.wait_ge(pv_done, p - LAG)
                    nc.scalar.activation(om_hi[rr, h // 2, :], ps_o[rr, :], ACT.Copy).then_inc(o_hi_made, 1)
                if LAG <= p < NP + LAG:
                    q = p - LAG
                    n = P * (q % 4 + 1)
                    act.wait_ge(t_full, q + 1)
                    if q >= 2:
                        act.wait_ge(pv_done, q - 1)
                    nc.scalar.activation(pt[:, q % 2, 0:n], ps_t[:, 0:n], ACT.Copy).then_inc(pt_made, 1)
                if p < NP:
                    n = P * (p % 4 + 1)
                    act.wait_ge(max_made, p + 1)
                    if p >= 4:
                        act.wait_ge(t_full, p - 3)
                    nc.scalar.activation(prob[:, p % 4, 0:n], ps_s[:, p % 2, 0:n], ACT.Exp,
                                         bias=nmax[:, p % 4:p % 4 + 1],
                                         accum_out=rsum[:, p % 4:p % 4 + 1]).then_inc(exp_made, 1)
                for i, m in MLA_STREAM.banks.get(p, ()):
                    gate_bank(U0["gate_b"] + i, m, 8 + 2 * i + m)
                for h in range(2):
                    if MLA_STREAM.started(p - 1 - h) is not None:
                        hi_half(MLA_STREAM.started(p - 1 - h) + 1, h)
            for u in range(U0["dq"] + 1, U0["mrg_m"] + 1):
                hi(u)

            NP = 4 * DH
            for p in range(DIFF_STEPS + 1):
                hd, r = (p - LAG - 4) // 4, (p - LAG - 4) % 4
                if 0 <= hd < DH and r == 0:
                    act.wait_ge(dPv, 4 * hd + 4)
                    act.wait_ge(dRinv, hd + 1)
                    if hd:
                        act.wait_ge(o_turned, hd)
                    for t in range(TT):
                        c = 4 * (hd % 2) + t
                        nc.scalar.activation(o_sb[:, t * P:(t + 1) * P], ps_o[:, t * P:(t + 1) * P], ACT.Copy,
                                             scale=drinv[:, c:c + 1]).then_inc(o_copied, 1)
                if 0 <= hd < DH and r == 3:
                    act.wait_ge(o_turned, hd + 1)
                    nc.scalar.activation(od_hi[:, hd, :], ps_t[:, :], ACT.Copy,
                                         scale=col[:, ROW0["diff_subln_g"]:ROW0["diff_subln_g"] + 1]
                                         ).then_inc(od_hi_made, 1)
                if LAG <= p < NP + LAG:
                    q = p - LAG
                    n = P * (q % 4 + 1)
                    act.wait_ge(dT, q + 1)
                    if q >= 2:
                        act.wait_ge(dPv, q - 1)
                    nc.scalar.activation(pt[:, q % 2, 0:n], ps_t[:, 0:n], ACT.Copy).then_inc(dPt, 1)
                if p < NP:
                    n = P * (p % 4 + 1)
                    for e, out in enumerate((prob[:, p % 4, 0:n], p2[:, p % 2, 0:n])):
                        act.wait_ge(dMax, 2 * p + e + 1)
                        if e == 0 and p >= 4:
                            act.wait_ge(dT, p - 3)
                        if e == 1 and p >= 2:
                            act.wait_ge(dP, p - 1)
                        b = 2 * (p % 4) + e
                        c = 8 * e + p % 8
                        nc.scalar.activation(out, ps_s[:, e, 0:n], ACT.Exp, bias=nmax[:, b:b + 1],
                                             accum_out=dsum[:, c:c + 1]).then_inc(dExp, 1)
                if 0 <= hd < DH and r == 0:
                    for t in range(TT):
                        act.wait_ge(o_copied, 4 * hd + t + 1)
                        squares(o_sb[:, t * P:(t + 1) * P], o_sq[:, t * P:(t + 1) * P], dssq[:, t:t + 1], o_squared)
                if DIFF_STREAM.started(p - 1) is not None:
                    hi(DIFF_STREAM.started(p - 1) + 1)
            for c in range(-1, 8):
                if c % 2 and c < 7:
                    hi(U0["mrg_d"] + (c + 1) // 2 + 1)
                if c >= 0:
                    act.wait_ge(merged, c + 1)
                    nc.scalar.activation(act_hi[:, c, :], gates[:, c, :], ACT.Copy, scale=0.5).then_inc(merged_hi, 1)
            def hi_at(u, s, count, k, w):
                act.wait_ge(w_landed[s], count)
                act.wait_ge(w_used, u - 1)
                nc.scalar.activation(w_hi[:, s, 0:k * w], stage[:, s, 0:k * w], ACT.Copy).then_inc(w_hi_made, 1)

            uf = U0["ffn"]
            lc = {uf % 2: landed_count(uf - 2) + 16, (uf + 1) % 2: landed_count(uf - 1) + 16}

            for i in range(4):
                u = U0["out"] + i
                if i < 3:
                    hi(u + 1)
                for m in range(2):
                    act.wait_ge(bank_free, freed(u, m))
                    if (i, m) == (3, 0):
                        hi_at(uf, uf % 2, lc[uf % 2], 8, 256)
                    part_squares(256 * i, m, i, 0, res, tmp[:, m, :], norm_squared)
                    act.wait_ge(norm_squared, TT + 4 * i + 2 * m + 2)
            act.wait_ge(rstd_made, 2)
            for t in (1, 3):
                scale_tile(n_sc[:, t, :], res[:, t, :], t)

            norm_hi_chunks("norm_ffn_g", KD)
            with act.Fori(0, KF // 2) as j:
                s0, s1 = uf % 2, (uf + 1) % 2
                hi_at(j * 2 + (uf + 1), s1, j * 16 + lc[s1], 8, 256)
                for m in range(2):
                    if m == 0:
                        act.wait_ge(first_full, j * 2 + (uf + 1))
                    else:
                        act.wait_ge(w_used, j * 2 + (uf + 1))
                    act.wait_ge(w_lo_made, j * 2 + (uf + 2))
                    nc.scalar.activation(sl[:, m, :], ps_mm[:, 2 * (uf % 2) + m, :], ACT.Silu).then_inc(bank_free_act, 1)
                with_next = j * 2 + (uf + 2)
                hi_at(with_next, s0, j * 16 + (lc[s0] + 16), 8, 256)
                for m in range(2):
                    act.wait_ge(bank_free, j * 2 + freed(uf + 1, m))
                    nc.scalar.activation(h_hi[:, bass.ds(j * 2 + m, 1), :], sl[:, m:m + 1, :], ACT.Copy
                                         ).then_inc(h_hi_made, 1)
            ud = U0["down"]
            ld = {ud % 2: landed_count(ud), (ud + 1) % 2: landed_count(ud + 1)}
            gd = group_of(ud)
            with act.Fori(0, DOWN_GROUPS // 2) as j:
                for i in range(1, 7):
                    s = (ud + i) % 2
                    kk = DOWN_K[i % 3] if i < 6 else 8
                    cnt = ld[s] + 16 * ((i - (s != ud % 2)) // 2)
                    hi_at(j * 6 + (ud + i), s, j * 48 + cnt, kk, 256)
                    if i % 3 == 0:
                        gg = i // 3 - 1
                        for m in range(2):
                            act.wait_ge(x_gained, j * 4 + (2 * gg + m + 1))
                            for kind, src in enumerate((res, act_y)):
                                for t in (2 * m, 2 * m + 1):
                                    nc.scalar.activation(
                                        tmp[:, kind, 256 * (t % 2):256 * (t % 2) + 256], src[:, t, bass.ds(j * 512 + 256 * gg, 256)], ACT.Square,
                                        accum_out=part[:, bass.ds(j * 8 + (16 * kind + 4 * gg + t), 1)]
                                        ).then_inc(down_squared, 1)
                            act.wait_ge(down_squared, j * 16 + (8 * gg + 4 * m + 4))
            act.wait_ge(rstd_made, 3)
            for t in (1, 3):
                scale_tile(n_sc[:, t, :], act_y[:, t, :], 4 + t)
            norm_hi_chunks("norm_g_2", 2 * KD)
            uq2 = U0["q2"]
            for u in range(uq2 + 1, U0["kv2"] + 1):
                hi(u)
            hi(U0["za"])

            def z_bank(u, m):
                if u > U0["zs"]:
                    act.wait_ge(bank_free, freed(u - 1, m))
                nc.scalar.activation(tmp[:, m, :], bank(u, m), ACT.Tanh, scale=0.5
                                     ).then_inc(z_tanh, 1)

            act.wait_ge(bank_free, freed(U0["kv2"], 1))
            for e in range(2):
                for g in range(2):
                    nc.scalar.activation(kdup[e * 64:e * 64 + 64, g, :], vt2[g * 64:g * 64 + 64, 1, :], ACT.Copy
                                         ).then_inc(kdup_made, 1)
            for i in range(4):
                u = U0["za"] + i
                hi(u + 1)
                for m in range(2):
                    nc.scalar.activation(gz[:, 2 * i + m, :], bank(u, m), ACT.Silu).then_inc(bank_free_act, 1)
            NP = WIN_PIECES
            for p in range(WIN_STEPS + 1):
                if LAG <= p < NP + LAG:
                    q = p - LAG
                    act.wait_ge(t2_full, q + 1)
                    if q >= 2:
                        act.wait_ge(pv2_done, q - 1)
                    if q // 8:
                        nc.scalar.activation(pt2[:, q % 2, :], ps_t[:, :], ACT.Copy).then_inc(pt2_made, 1)
                    else:
                        nc.scalar.activation(pt2[:, q % 2, :].rearrange("p (e n) -> p e n", e=2)[:, :, P:2 * P],
                                             ps_t[:, :].rearrange("p (e n) -> p e n", e=2)[:, :, P:2 * P], ACT.Copy
                                             ).then_inc(pt2_made, 1)
                if p < NP:
                    b = p // 8
                    act.wait_ge(max2_made, p + 1)
                    if p >= 4:
                        act.wait_ge(t2_full, p - 3)
                    for e in range(2):
                        j0 = 0 if b else P
                        j = 16 * (b % 2) + window_head(p % 8, e)
                        nc.scalar.activation(prob2[:, p % 4, e * 256 + j0:e * 256 + 256],
                                             ps_s[:, p % 2, e * 256 + j0:e * 256 + 256], ACT.Exp,
                                             bias=nm2[:, j:j + 1], accum_out=rs2[:, j:j + 1]
                                             ).then_inc(exp2_made, 1)
                if p >= 1 and (p - 1) % 4 == 3 and p - 1 < NP:
                    act.wait_ge(sink_diff, (p - 1) // 4 + 1)
                    nc.scalar.activation(esink, dsink, ACT.Exp).then_inc(sink_exp, 1)
                for i, m in WIN_STREAM.banks.get(p, ()):
                    z_bank(U0["zs"] + i, m)
                for h in range(2):
                    if WIN_STREAM.started(p - 1 - h) is not None:
                        hi_half(WIN_STREAM.started(p - 1 - h) + 1, h)
            for i in range(4):
                u = U0["u2"] + i
                hi(u + 1)
                for m in range(2):
                    c = 2 * i + m
                    act.wait_ge(bank_free, freed(u - 1, m))
                    nc.scalar.activation(tmp[:, m, :], bank(u, m), ACT.Gelu
                                         ).then_inc(gelu_made, 1)
            for i in range(4):
                u = U0["vs"] + i
                hi(u + 1)
                for m in range(2):
                    nc.scalar.activation(vs[:, 2 * m:2 * m + 2, 256 * i:256 * i + 256],
                                         bank(u, m).rearrange("p (t n) -> p t n", t=2),
                                         ACT.Gelu).then_inc(gelu_made, 1)
            act.wait_ge(a_gated, 8)
            for c in range(KD):
                nc.scalar.activation(at_hi[:, c, :], gz[:, c, :], ACT.Copy).then_inc(at_hi_made, 1)
            act.wait_ge(vs_summed, 1)
            for t in range(TT):
                nc.scalar.activation(tmp[:, :, :].rearrange("p a n -> p (a n)"), vs[:, t, :], ACT.Square, bias=nmean[:, t:t + 1],
                                     accum_out=ssq[:, t:t + 1]).then_inc(vs_squared, 1)
                act.wait_ge(vs_squared, t + 1)

            def sig_bank(u, m, dst, c, row):
                nc.scalar.activation(dst[:, c, :], bank(u, m), ACT.Sigmoid,
                                     bias=col[:, row:row + 1]).then_inc(bank_free_act, 1)

            act.wait_ge(at_lo_made, KD)
            for i in range(4):
                u = U0["ga"] + i
                hi(u + 1)
                for m in range(2):
                    sig_bank(u, m, gz, 2 * i + m, ROW0["b_merge_2"] + 2 * i + m)
            for u in range(U0["att"] + 1, U0["gs"] + 1):
                hi(u)
            for g in range(8):
                act.wait_ge(mix_gated, g + 1)
                nc.scalar.activation(at_hi[:, g, :], tmp[:, g % 2, :], ACT.Copy).then_inc(sg_hi_made, 1)
            for i in range(4):
                u = U0["gs"] + i
                hi(u + 1)
                for m in range(2):
                    sig_bank(u, m, gs, 2 * i + m, ROW0["b_merge_2"] + 8 + 2 * i + m)
            for i in range(4):
                u = U0["sgo"] + i
                hi(u + 1)
                for m in range(2):
                    c = 2 * i + m
                    act.wait_ge(y_sum, c + 1)
                    nc.scalar.activation(act_hi[:, c, :], gs[:, c, :], ACT.Copy).then_inc(y_hi_made, 1)
            for i in range(4):
                u = U0["wo"] + i
                if u + 1 < NU:
                    hi(u + 1)
                for m in range(2):
                    act.wait_ge(bank_free, freed(u, m))
                    part_squares(256 * i, m, i, 0, res, tmp[:, m, :], fin_squared)
                    act.wait_ge(fin_squared, 4 * i + 2 * m + 2)
            act.wait_ge(rstd_made, 4)
            act.wait_ge(x_gained, 16)
            for t in (1, 3):
                nc.scalar.activation(res[:, t, :], vs[:, t, :], ACT.Copy, scale=rstd[:, t:t + 1]).then_inc(fin_made_act, 1)

        @block.vector
        def _(dve):
            V = nc.vector
            chain = [0]

            def link(ins):
                chain[0] += 1
                ins.then_inc(dve_chain, 1)
                return chain[0]

            def after(n):
                dve.wait_ge(dve_chain, n)

            def lo(u):
                s = u % 2
                src, k, w = unit_source(u)
                dve.wait_ge(w_hi_made, u + 1)
                V.tensor_tensor(w_lo[:, s, 0:k * w], stage[:, s, 0:k * w], w_hi[:, s, 0:k * w].bitcast(F32),
                                ALU.subtract).then_inc(w_lo_made, 1)

            def lo_half(u, h):
                s = u % 2
                src, k, w = unit_source(u)
                dve.wait_ge(w_hi_made, u + 1)
                n = k * w // 2
                ins = V.tensor_tensor(w_lo[:, s, h * n:(h + 1) * n], stage[:, s, h * n:(h + 1) * n],
                                      w_hi[:, s, h * n:(h + 1) * n].bitcast(F32), ALU.subtract)
                if h:
                    ins.then_inc(w_lo_made, 1)

            def bank(u, m):
                g = group_of(u)
                if m == 0:
                    dve.wait_ge(first_full, g + 1)
                else:
                    dve.wait_ge(w_used, u + 1)
                return ps_mm[:, 2 * (g % 2) + m, :]

            def rsqrt_of(n, made=None):
                v, y, t = var[:, 0:n], rstd[:, 0:n], nt1[:, 0:n]
                after(link(V.tensor_scalar(y.bitcast(I32), v.bitcast(I32), -0.5, float(0x5f3759df),
                                           ALU.mult, ALU.add)))
                for step in range(3):
                    after(link(V.tensor_tensor(t, y, y, ALU.mult)))
                    after(link(V.scalar_tensor_tensor(out=t, in0=t, scalar=-0.5, in1=v, op0=ALU.mult, op1=ALU.mult)))
                    ins = V.scalar_tensor_tensor(out=y, in0=t, scalar=1.5, in1=y, op0=ALU.add, op1=ALU.mult)
                    if step == 2 and made is not None:
                        ins.then_inc(rstd_made, 1)
                        dve.wait_ge(rstd_made, made)
                    else:
                        after(link(ins))

            def rsqrt(n, scale, made=None):
                after(link(V.tensor_scalar(var[:, 0:n], ssq[:, 0:n], scale, EPS, ALU.mult, ALU.add)))
                rsqrt_of(n, made)

            def add_parts(kinds=1):
                after(link(V.tensor_reduce(ssq[:, 0:4 * kinds],
                                           part[:, 0:16 * kinds].rearrange("p (c i t) -> p c t i", c=kinds, i=4),
                                           AX.X, ALU.add)))

            def norm_lo_chunk(row, base, k):
                dve.wait_ge(norm_hi, base + k + 1)
                V.scalar_tensor_tensor(out=act_lo[:, k, :], in0=side_bank(k),
                                       scalar=col[:, ROW0[row] + k:ROW0[row] + k + 1],
                                       in1=act_hi[:, k, :].bitcast(F32), op0=ALU.mult, op1=ALU.subtract
                                       ).then_inc(norm_lo, 1)

            def norm_lo_chunks(row, base):
                for k in range(KD):
                    norm_lo_chunk(row, base, k)

            def token_rows(ap, w):
                return ap[:, 0:2 * w].rearrange("p (t n) -> p t n", t=2)

            dve.wait_ge(ident_made, 1)
            link(V.tensor_copy(ident_r[:, :], ident[:, :]))
            dve.wait_ge(consts_made, 5)
            link(V.tensor_copy(causal_r[:, :], tmp[:, 0, 0:P]))
            after(link(V.tensor_copy(window_r[:, :, :], tmp[:, 1, :].rearrange("p (e n) -> p e n", e=2))))
            dve.wait_ge(cols_turned, 1)
            after(link(V.tensor_copy(col[:, :], ps_t[:, 0:NROWS])))
            after(link(V.tensor_scalar(col[:, ROW0["diff_subln_g"]:ROW0["diff_subln_g"] + 1],
                                       col[:, ROW0["diff_subln_g"]:ROW0["diff_subln_g"] + 1], 1.0 - LAMBDA_INIT, None,
                                       ALU.mult)))
            V.tensor_scalar(hcol[:, :], col[:, :], 0.5, None, ALU.mult).then_inc(cols_made, 1)
            def scale_tiles(out, src, c0=0):
                for t in (0, 2):
                    V.tensor_scalar(out[:, t, :], src[:, t, :], rstd[:, c0 + t:c0 + t + 1], None, ALU.mult
                                    ).then_inc(norm_scaled, 1)

            dve.wait_ge(norm_squared, TT)
            rsqrt(TT, 1.0 / D, made=1)
            scale_tiles(x_sc, x_in)
            for k in range(KD):
                dve.wait_ge(norm_hi, k + 1)
                ins = V.tensor_tensor(w_lo[:, 0, 256 * k:256 * k + 256], stage[:, 0, 256 * k:256 * k + 256],
                                      w_hi[:, 0, 256 * k:256 * k + 256].bitcast(F32), ALU.subtract)
                if k == KD - 1:
                    ins.then_inc(w_lo_made, 1)
                norm_lo_chunk("norm_mix_g", 0, k)
            dve.wait_ge(lam_landed, 64)
            lt = lamv[:, :, :].rearrange("p (a b) n -> p a b n", b=2)
            after(link(V.tensor_tensor(lt[:, :, 0, :], lt[:, :, 0, :], lt[:, :, 1, :], ALU.mult)))
            V.tensor_reduce(lsum, lt[:, :, 0, :], AX.X, ALU.add).then_inc(lam_summed, 1)
            lo(1)

            def angles(n, table_row, pos):
                two_pi = 2.0 * math.pi
                c1 = 6.28125
                c2 = math.floor((two_pi - c1) * 2 ** 17) / 2 ** 17
                c3 = math.floor((two_pi - c1 - c2) * 2 ** 26) / 2 ** 26
                c4 = two_pi - c1 - c2 - c3
                magic = 1.5 * 2 ** 23
                if n >= 1:
                    dve.wait_ge(sincos_made, n)
                ang, kk, r, ar = rt[:, 0, :], rt[:, 1, :], rt[:, 2, :], rt[:, 3, :]
                after(link(V.tensor_scalar(ang, pos, freq[:, table_row:table_row + 1], None, ALU.mult)))
                after(link(V.tensor_scalar(kk, ang, 1.0 / two_pi, magic, ALU.mult, ALU.add)))
                after(link(V.tensor_scalar(kk, kk, magic, None, ALU.subtract)))
                prev = ang
                for c in (c1, c2, c3, c4):
                    after(link(V.scalar_tensor_tensor(out=r, in0=kk, scalar=-c, in1=prev, op0=ALU.mult, op1=ALU.add)))
                    prev = r
                after(link(V.tensor_scalar(r, r, 3.1415925, -3.1415925, ALU.min, ALU.max)))
                V.scalar_tensor_tensor(out=ar, in0=r, scalar=-1.0, in1=r, op0=ALU.mult, op1=ALU.max
                                       ).then_inc(angle_ready, 1)

            dve.wait_ge(pos_landed, 16)
            dve.wait_ge(freq_landed, 16)
            after(link(V.tensor_copy(pos_f[:, 0, :], pos_i[:, :])))
            angles(0, 0, pos_f[:, 0, :])

            def keep_latents(u):
                w = 256 if u < 2 else LAT - 512
                for m in range(2):
                    V.tensor_copy(lat[:, 2 * m:2 * m + 2, 256 * u:256 * u + w], token_rows(bank(u, m), w)
                                  ).then_inc(bank_free, 1)

            keep_latents(0)
            lo(2)
            dve.wait_ge(lam_exp, 1)
            after(link(V.tensor_tensor(neglam, lexp[:, 1:2], lexp[:, 0:1], ALU.subtract)))
            link(V.tensor_scalar(neglam, neglam, LAMBDA_INIT, None, ALU.subtract))
            angles(1, 1, pos_f[:, 0, :])
            keep_latents(1)
            lo(3)
            dve.wait_ge(iota_made, 1)
            after(link(V.tensor_copy(pos_f[:, 1, :], pos_i2[:, :])))
            angles(2, 1, pos_f[:, 1, :])
            keep_latents(2)
            lo(4)
            dve.wait_ge(lat_squared, 8)
            after(link(V.tensor_scalar(ssq[:, 0:4], ssq[:, 0:4], KVR / QR, None, ALU.mult)))
            rsqrt(8, 1.0 / KVR)
            for t in range(TT):
                V.tensor_scalar(lat[:, t, 0:QR], lat[:, t, 0:QR], rstd[:, t:t + 1], None, ALU.mult
                                ).then_inc(lat_scaled, 1)
                V.tensor_scalar(lat[:, t, QR:QR + KVR], lat[:, t, QR:QR + KVR], rstd[:, 4 + t:5 + t], None, ALU.mult
                                ).then_inc(lat_scaled, 1)
            lo(5)
            for i in range(5):
                row = ROW0["mla_q_norm_g"] + i
                dve.wait_ge(lat_hi, i + 1)
                V.scalar_tensor_tensor(out=lt_lo[:, i, :], in0=side_bank(i), scalar=col[:, row:row + 1],
                                       in1=lt_hi[:, i, :].bitcast(F32), op0=ALU.mult, op1=ALU.subtract
                                       ).then_inc(lat_lo, 1)
            swap16 = [i ^ 16 for i in range(32)]
            swap8 = [i ^ 8 if i < 16 else i for i in range(32)]

            lo(6)
            dve.wait_ge(lat_turned, 6)
            rr = slice(MN, MQ)
            src = side_bank(5)[MN:MQ, :]
            t = tmp[rr, 1, :]
            after(link(V.stream_shuffle(t, src, swap16)))
            after(link(V.tensor_tensor(t, t, rope_m[rr, 1, :], ALU.mult)))
            after(link(V.tensor_tensor(tmp[rr, 0, :], src, rope_m[rr, 0, :], ALU.mult)))
            after(link(V.tensor_tensor(tmp[rr, 0, :], tmp[rr, 0, :], t, ALU.add)))
            for h in range(MH):
                V.tensor_copy(km[MN:MQ, h, :], tmp[rr, 0, :]).then_inc(kpe_spread, 1)
            lo(7)
            dve.wait_ge(kpe_spread, MH)

            def rope_bank(u, m, dst, tab, swap, scale=1.0, signal=None):
                src = bank(u, m)
                t = tmp[:, m, :]
                c0 = link(V.stream_shuffle(t, src, swap))
                V.scalar_tensor_tensor(out=dst, in0=src, scalar=scale, in1=tab[:, 0, :], op0=ALU.mult, op1=ALU.mult
                                       ).then_inc(bank_free, 1)
                after(c0)
                after(link(V.scalar_tensor_tensor(out=t, in0=t, scalar=scale, in1=tab[:, 1, :], op0=ALU.mult,
                                                  op1=ALU.mult)))
                dve.wait_ge(bank_free, freed(u, m))
                if signal is not None:
                    V.tensor_tensor(dst, dst, t, ALU.add).then_inc(signal, 1)
                    dve.wait_ge(signal, m + 1)
                else:
                    after(link(V.tensor_tensor(dst, dst, t, ALU.add)))

            for u in range(U0["qn"], U0["mv"]):
                lo(u + 1)
                for m in range(2):
                    if u == U0["qp"]:
                        rope_bank(u, m, prob[:, 2 + m, :], rope_m, swap16, MQ ** -0.5, qp_roped)
                        continue
                    src = bank(u, m)
                    if u < U0["qp"]:
                        i = u - U0["qn"]
                        dve.wait_ge(nope_kept, 2 * i + m + 1)
                        V.tensor_scalar(qm[0:MN, 4 * i + 2 * m, :], src[0:MN, :], MQ ** -0.5, None, ALU.mult
                                        ).then_inc(bank_free, 1)
                    else:
                        i = u - U0["kn"]
                        dve.wait_ge(nope_kept, 4 + 2 * i + m + 1)
                        V.tensor_copy(km[0:MN, 4 * i + 2 * m, :], src[0:MN, :]).then_inc(bank_free, 1)
            for i in range(2):
                u = U0["mv"] + i
                if i == 0:
                    lo(u + 1)
                for m in range(2):
                    V.tensor_copy(vm[:, 2 * m:2 * m + 2, 256 * i:256 * i + 256], token_rows(bank(u, m), 256)
                                  ).then_inc(bank_free, 1)

            NP = 4 * MH
            for p in range(MLA_STEPS + 3):
                if p < NP:
                    n = P * (p % 4 + 1)
                    b = p % 4
                    dve.wait_ge(s_full, p + 1)
                    if p >= 4:
                        dve.wait_ge(exp_made, p - 3)
                    V.tensor_reduce(nmax[:, b:b + 1], ps_s[:, p % 2, 0:n], AX.X, ALU.max, negate=True
                                    ).then_inc(max_made, 1)
                if p > LAG and (p - LAG - 1) % 4 == 3 and p - LAG - 1 < NP:
                    h = (p - LAG - 1) // 4
                    rr = slice((h % 2) * MV, (h % 2) * MV + MV)
                    dve.wait_ge(o_hi_made, h + 1)
                    V.tensor_tensor(om_lo[rr, h // 2, :], ps_o[rr, :], om_hi[rr, h // 2, :].bitcast(F32), ALU.subtract
                                    ).then_inc(o_free, 1)
                if 1 <= p <= NP:
                    q = p - 1
                    n = P * (q % 4 + 1)
                    b = q % 4
                    dve.wait_ge(exp_made, q + 1)
                    after(link(V.reciprocal(rinv[:, b:b + 1], rsum[:, b:b + 1])))
                    V.tensor_scalar(prob[:, b, 0:n], prob[:, b, 0:n], rinv[:, b:b + 1], None, ALU.mult
                                    ).then_inc(p_ready, 1)
                if p == 0:
                    lo(U0["gate_b"])
                for h in range(2):
                    if MLA_STREAM.started(p - 3 - h) is not None:
                        lo_half(MLA_STREAM.started(p - 3 - h) + 1, h)

            for name, dst in (("dq", dq), ("dk", dk)):
                for i in range(2):
                    u = U0[name] + i
                    lo(u + 1)
                    for m in range(2):
                        rope_bank(u, m, dst[:, 2 * i + m, :], rope_d, swap8, DD ** -0.5 if name == "dq" else 1.0)
            for i in range(2):
                u = U0["dv"] + i
                lo(u + 1)
                for m in range(2):
                    V.tensor_copy(dv[:, 2 * m:2 * m + 2, 256 * i:256 * i + 256], token_rows(bank(u, m), 256)
                                  ).then_inc(bank_free, 1)

            def gated(u, m, c):
                V.scalar_tensor_tensor(out=gates[:, c, :], in0=gates[:, c, :], scalar=1.0, in1=bank(u, m),
                                       op0=ALU.add, op1=ALU.mult).then_inc(bank_free, 1)

            NP = 4 * DH
            for p in range(DIFF_STEPS + 1):
                hd, r = (p - LAG - 4) // 4, (p - LAG - 4) % 4
                if 0 <= hd < DH and r == 3:
                    dve.wait_ge(od_hi_made, hd + 1)
                    V.scalar_tensor_tensor(out=od_lo[:, hd, :], in0=ps_t[:, :],
                                           scalar=col[:, ROW0["diff_subln_g"]:ROW0["diff_subln_g"] + 1],
                                           in1=od_hi[:, hd, :].bitcast(F32), op0=ALU.mult, op1=ALU.subtract
                                           ).then_inc(od_made, 1)
                if p < NP:
                    n = P * (p % 4 + 1)
                    for e in range(2):
                        b = 2 * (p % 4) + e
                        dve.wait_ge(dS, 2 * p + e + 1)
                        if p >= 4:
                            dve.wait_ge(dExp, 2 * (p - 4) + e + 1)
                        V.tensor_reduce(nmax[:, b:b + 1], ps_s[:, e, 0:n], AX.X, ALU.max, negate=True
                                        ).then_inc(dMax, 1)
                if 1 <= p <= NP:
                    q = p - 1
                    n = P * (q % 4 + 1)
                    b, c = q % 4, q % 8
                    dve.wait_ge(dExp, 2 * q + 2)
                    after(link(V.reciprocal(rinv[:, b:b + 1], dsum[:, 8 + c:9 + c])))
                    after(link(V.scalar_tensor_tensor(out=mix[:, b:b + 1], in0=rinv[:, b:b + 1], scalar=neglam,
                                                      in1=dsum[:, c:c + 1], op0=ALU.mult, op1=ALU.mult)))
                    V.scalar_tensor_tensor(out=prob[:, b, 0:n], in0=p2[:, q % 2, 0:n],
                                           scalar=mix[:, b:b + 1], in1=prob[:, b, 0:n], op0=ALU.mult,
                                           op1=ALU.add).then_inc(dP, 1)
                    if b == 3:
                        c = 4 * (q // 4 % 2)
                        V.reciprocal(drinv[:, c:c + 4], dsum[:, c:c + 4]).then_inc(dRinv, 1)
                if 0 <= hd < DH and r == 2:
                    dve.wait_ge(drstd_made, hd + 1)
                    for t in range(TT):
                        V.tensor_scalar(o_sb[:, t * P:t * P + P], o_sb[:, t * P:t * P + P], drstd[:, t:t + 1], None,
                                        ALU.mult).then_inc(o_scaled, 1)
                for i, m in DIFF_STREAM.banks.get(p, ()):
                    gated(U0["mrg_m"] + i, m, 2 * i + m)
                if DIFF_STREAM.started(p - 2) is not None:
                    lo(DIFF_STREAM.started(p - 2) + 1)
            for c in range(-1, 8):
                if c >= 0:
                    u, m = U0["mrg_d"] + c // 2, c % 2
                    gated(u, m, 8 + c)
                    dve.wait_ge(bank_free, freed(u, m))
                    V.tensor_tensor(gates[:, c, :], gates[:, c, :], gates[:, 8 + c, :], ALU.add).then_inc(merged, 1)
                    dve.wait_ge(merged_hi, c + 1)
                    V.scalar_tensor_tensor(out=act_lo[:, c, :], in0=gates[:, c, :], scalar=0.5,
                                           in1=act_hi[:, c, :].bitcast(F32), op0=ALU.mult, op1=ALU.subtract
                                           ).then_inc(merged_lo, 1)
                if c % 2 and c < 7:
                    lo(U0["mrg_d"] + (c + 1) // 2 + 1)

            def add_residual(m, ps, n0):
                r = res[:, 2 * m:2 * m + 2, bass.ds(n0, 256)]
                return V.tensor_tensor(r, token_rows(ps, 256), r, ALU.add)

            dve.wait_ge(res_landed, 16 * TT)
            for i in range(4):
                u = U0["out"] + i
                if u + 1 < U0["ffn"]:
                    lo(u + 1)
                for m in range(2):
                    add_residual(m, bank(u, m), 256 * i).then_inc(bank_free, 1)

            def lo_at(u, s, k, w):
                dve.wait_ge(w_hi_made, u + 1)
                V.tensor_tensor(w_lo[:, s, 0:k * w], stage[:, s, 0:k * w], w_hi[:, s, 0:k * w].bitcast(F32),
                                ALU.subtract).then_inc(w_lo_made, 1)

            uf = U0["ffn"]
            lo_at(uf, uf % 2, 8, 256)
            dve.wait_ge(norm_squared, TT + 16)
            add_parts()
            rsqrt(TT, 1.0 / D, made=2)
            scale_tiles(n_sc, res)
            norm_lo_chunks("norm_ffn_g", KD)
            with dve.Fori(0, KF // 2) as j:
                lo_at(j * 2 + (uf + 1), (uf + 1) % 2, 8, 256)
                lo_at(j * 2 + (uf + 2), uf % 2, 8, 256)
                for m in range(2):
                    if m == 0:
                        dve.wait_ge(first_full, j * 2 + (uf + 2))
                    else:
                        dve.wait_ge(w_used, j * 2 + (uf + 2))
                    dve.wait_ge(bank_free_act, j * 2 + (m + 1))
                    V.tensor_tensor(sl[:, m, :], ps_mm[:, 2 * ((uf + 1) % 2) + m, :], sl[:, m, :], ALU.mult
                                    ).then_inc(bank_free, 1)
                    dve.wait_ge(h_hi_made, j * 2 + (m + 1))
                    V.tensor_tensor(h_lo[:, bass.ds(j * 2 + m, 1), :], sl[:, m:m + 1, :],
                                    h_hi[:, bass.ds(j * 2 + m, 1), :].bitcast(F32), ALU.subtract
                                    ).then_inc(h_lo_made, 1)
            ud = U0["down"]
            gd = group_of(ud)
            dve.wait_ge(gf_landed, 16)
            with dve.Fori(0, DOWN_GROUPS // 2) as j:
                for gg in range(2):
                    for i in range(1, 4):
                        ii = 3 * gg + i
                        kk = DOWN_K[i % 3]
                        lo_at(j * 6 + (ud + ii), (ud + ii) % 2, kk, 256)
                    for m in range(2):
                        if m == 0:
                            dve.wait_ge(first_full, j * 2 + (gd + gg + 1))
                        else:
                            dve.wait_ge(w_used, j * 6 + (ud + 3 * gg + 3))
                        r = res[:, 2 * m:2 * m + 2, bass.ds(j * 512 + gg * 256, 256)]
                        V.tensor_tensor(r, token_rows(ps_mm[:, 2 * ((gd + gg) % 2) + m, :], 256), r, ALU.add
                                        ).then_inc(bank_free, 1)
                        dve.wait_ge(bank_free, j * 4 + (dve_freed(gd + gg, m)))
                        V.tensor_tensor(act_y[:, 2 * m:2 * m + 2, bass.ds(j * 512 + gg * 256, 256)], r,
                                        gf_b[:, bass.ds(j * 512 + gg * 256, 256)].unsqueeze(1).broadcast_to([P, 2, 256]),
                                        ALU.mult).then_inc(x_gained, 1)
            dve.wait_ge(down_squared, 32)
            add_parts(2)
            after(link(V.tensor_scalar(var[:, 0:4], ssq[:, 0:4], 1.0 / D, EPS, ALU.mult, ALU.add)))
            after(link(V.tensor_scalar(var[:, 4:8], var[:, 0:4], EPS, None, ALU.mult)))
            after(link(V.scalar_tensor_tensor(out=var[:, 4:8], in0=ssq[:, 4:8], scalar=1.0 / D, in1=var[:, 4:8],
                                              op0=ALU.mult, op1=ALU.add)))
            rsqrt_of(8, made=3)
            scale_tiles(n_sc, act_y, 4)
            norm_lo_chunks("norm_g_2", 2 * KD)
            dve.wait_ge(norm_turned, 3 * KD)
            for i in range(4):
                u = U0["q2"] + i
                lo(u + 1)
                for m in range(2):
                    rope_bank(u, m, q2[:, 2 * i + m, :], rope2, swap8, AD ** -0.5)
                V.scalar_tensor_tensor(out=res[:, i, :], in0=res[:, i, :], scalar=rstd[:, i:i + 1], in1=gf_b[:, :],
                                       op0=ALU.mult, op1=ALU.mult).then_inc(x3_made, 1)
            u = U0["kv2"]
            lo(u + 1)
            rope_bank(u, 0, vt2[:, 1, :], rope2, swap8)
            V.tensor_copy(vt2[:, 0, :], bank(u, 1)).then_inc(bank_free, 1)

            def z_bank(u, m, c, n):
                dve.wait_ge(z_tanh, n + 1)
                V.scalar_tensor_tensor(out=gu[:, c, :], in0=tmp[:, m, :], scalar=1.0, in1=bank(u, m), op0=ALU.add,
                                       op1=ALU.mult).then_inc(bank_free, 1)

            dve.wait_ge(v_turned, 1)
            V.tensor_copy(v2[:, :, :], ps_t[:, :].rearrange("p (t n) -> p t n", t=TT)).then_inc(v2_made, 1)
            for i in range(4):
                u = U0["za"] + i
                lo(u + 1)
                if i == 2:
                    for hb in range(2):
                        dve.wait_ge(wg_turned, hb + 1)
                        link(V.tensor_copy(wg_t[:, 4 * hb:4 * hb + 4, :],
                                           (ps_t, ps_o)[hb][:, :].rearrange("p (g n) -> p g n", g=4)))
                    after(chain[0])
                    V.memset(wg_t[CHUNK:P, :, 0:CHUNK], 0.0).then_inc(wg_made, 1)
            NP = WIN_PIECES
            dve.wait_ge(sink_landed, 16)
            after(link(V.tensor_scalar(nsinkb, sinkb, -1.0, None, ALU.mult)))
            for p in range(WIN_STEPS + 2):
                if p >= LAG + 2 and (p - LAG - 2) % 4 == 3 and p - LAG - 2 < NP:
                    g8 = (p - LAG - 2) // 4
                    b, c0 = g8 // 2, 4 * (g8 % 2)
                    dve.wait_ge(a_turned, g8 + 1)
                    if g8 == 0:
                        dve.wait_ge(bank_free_act, act_freed(group_of(U0["za"]) + 3, 1))
                    g = gz[:, c0:c0 + 4, b * P:b * P + P]
                    V.tensor_tensor(g, ps_t[:, :].rearrange("p (c n) -> p c n", c=4), g, ALU.mult
                                    ).then_inc(a_gated, 1)
                if p < NP:
                    b, i = p // 8, p % 8
                    h = window_head(i, 0)
                    j = 16 * (b % 2) + h
                    j0 = 0 if b else P
                    dve.wait_ge(s2_full, p + 1)
                    mx = nmax[:, 2 * (p % 4):2 * (p % 4) + 2]
                    after(link(V.tensor_reduce(mx, ps_s[:, p % 2, :].rearrange("p (e n) -> p e n", e=2)[:, :, j0:256],
                                               AX.X, ALU.max, negate=True)))
                    V.tensor_tensor(nm2[:, j:j + 3:2], mx, nsinkb[:, h:h + 3:2], ALU.min).then_inc(max2_made, 1)
                if p >= 1 and (p - 1) % 4 == 3 and p - 1 < NP:
                    g8 = (p - 1) // 4
                    jj = 16 * (g8 // 2 % 2) + 8 * (g8 % 2)
                    if g8:
                        dve.wait_ge(sink_exp, g8)
                    V.tensor_tensor(dsink, sinkb[:, 8 * (g8 % 2):8 * (g8 % 2) + 8], nm2[:, jj:jj + 8], ALU.add
                                    ).then_inc(sink_diff, 1)
                if p >= LAG and (p - LAG) % 4 == 3 and p - LAG < NP:
                    g8 = (p - LAG) // 4
                    jj = 16 * (g8 // 2 % 2) + 8 * (g8 % 2)
                    dve.wait_ge(sink_exp, g8 + 1)
                    after(link(V.tensor_tensor(den2, rs2[:, jj:jj + 8], esink, ALU.add)))
                    after(link(V.reciprocal(rden2, den2)))
                if p >= LAG + 1 and (p - LAG - 1) % 4 == 3 and p - LAG - 1 < NP:
                    g8 = (p - LAG - 1) // 4
                    dve.wait_ge(pv2_done, 4 * g8 + 4)
                    V.tensor_tensor(a_tok[:, g8 % 2, :].rearrange("p (h n) -> p h n", h=8),
                                    ps_o[:, :].rearrange("p (h n) -> p h n", h=8),
                                    rden2.unsqueeze(2).broadcast_to([P, 8, AD]), ALU.mult).then_inc(a_kept, 1)
                for i, m in WIN_STREAM.banks.get(p, ()):
                    z_bank(U0["zs"] + i, m, 2 * i + m, 2 * i + m)
                for h in range(2):
                    if WIN_STREAM.started(p - 3 - h) is not None:
                        lo_half(WIN_STREAM.started(p - 3 - h) + 1, h)
            for i in range(4):
                u = U0["u2"] + i
                lo(u + 1)
                for m in range(2):
                    c = 2 * i + m
                    dve.wait_ge(gelu_made, c + 1)
                    V.scalar_tensor_tensor(out=gu[:, c, :], in0=tmp[:, m, :], scalar=0.5, in1=gu[:, c, :],
                                           op0=ALU.mult, op1=ALU.mult).then_inc(bank_free, 1)
            for i in range(4):
                u = U0["vs"] + i
                lo(u + 1)
                for m in range(2):
                    dve.wait_ge(gelu_made, 8 + 2 * i + m + 1)
                    V.tensor_reduce(vsum[:, 4 * i + 2 * m:4 * i + 2 * m + 2],
                                    vs[:, 2 * m:2 * m + 2, 256 * i:256 * i + 256], AX.X, ALU.add
                                    ).then_inc(bank_free, 1)
            dve.wait_ge(bank_free, freed(U0["ga"] - 1, 1))
            after(link(V.tensor_reduce(mean, vsum.rearrange("p (i t) -> p t i", i=4), AX.X, ALU.add)))
            after(link(V.tensor_scalar(mean, mean, 1.0 / D, None, ALU.mult)))
            V.tensor_scalar(nmean, mean, -1.0, None, ALU.mult).then_inc(vs_summed, 1)
            for c in range(KD):
                dve.wait_ge(at_hi_made, c + 1)
                V.tensor_tensor(at_lo[:, c, :], gz[:, c, :], at_hi[:, c, :].bitcast(F32), ALU.subtract
                                ).then_inc(at_lo_made, 1)

            def layer_norm(t):
                c0 = link(V.tensor_scalar(vs[:, t, :], vs[:, t, :], mean[:, t:t + 1], rstd[:, t:t + 1], ALU.subtract,
                                          ALU.mult))
                after(c0)
                after(link(V.tensor_tensor(vs[:, t, :], vs[:, t, :], lng_b[:, :], ALU.mult)))
                V.tensor_tensor(vs[:, t, :], vs[:, t, :], lnb_b[:, :], ALU.add).then_inc(vs_normed, 1)

            dve.wait_ge(vs_squared, TT)
            rsqrt(TT, 1.0 / D)
            dve.wait_ge(ln_landed, 32)
            for i in range(4):
                u = U0["ga"] + i
                lo(u + 1)
                layer_norm(i)
            for i in range(4):
                u = U0["att"] + i
                lo(u + 1)
                for m in range(2):
                    c = 2 * i + m
                    dve.wait_ge(bank_free_act, act_freed(group_of(U0["ga"]) + i, m))
                    V.tensor_tensor(gz[:, c, :], bank(u, m), gz[:, c, :], ALU.mult).then_inc(bank_free, 1)
            dve.wait_ge(sgb_landed, 16)
            for g in range(8):
                dve.wait_ge(mix_full, g + 1)
                tb = tmp[:, g % 2, :]
                if g >= 2:
                    dve.wait_ge(sg_lo_made, g - 1)
                after(link(V.tensor_tensor(tb.rearrange("p (b n) -> p b n", b=TT),
                                           side_bank(g).rearrange("p (b n) -> p b n", b=TT),
                                           sgb_b[:, g:g + 1, :].broadcast_to([P, TT, P]), ALU.add)))
                V.tensor_tensor(tb, tb, gu[:, g, :], ALU.mult).then_inc(mix_gated, 1)
                dve.wait_ge(sg_hi_made, g + 1)
                V.tensor_tensor(at_lo[:, g, :], tb, at_hi[:, g, :].bitcast(F32), ALU.subtract).then_inc(sg_lo_made, 1)
            for i in range(4):
                lo(U0["gs"] + i + 1)
            for i in range(4):
                u = U0["sgo"] + i
                lo(u + 1)
                for m in range(2):
                    c = 2 * i + m
                    dve.wait_ge(bank_free_act, act_freed(group_of(U0["gs"]) + i, m))
                    V.tensor_tensor(gs[:, c, :], bank(u, m), gs[:, c, :], ALU.mult).then_inc(bank_free, 1)
                    dve.wait_ge(bank_free, freed(u, m))
                    V.tensor_tensor(gs[:, c, :], gs[:, c, :], gz[:, c, :], ALU.add).then_inc(y_sum, 1)
                    dve.wait_ge(y_hi_made, c + 1)
                    V.tensor_tensor(act_lo[:, c, :], gs[:, c, :], act_hi[:, c, :].bitcast(F32), ALU.subtract
                                    ).then_inc(y_lo_made, 1)
            for i in range(4):
                u = U0["wo"] + i
                if u + 1 < NU:
                    lo(u + 1)
                if i == 0:
                    dve.wait_ge(fg_landed, 16)
                for m in range(2):
                    add_residual(m, bank(u, m), 256 * i).then_inc(bank_free, 1)
                    dve.wait_ge(bank_free, freed(u, m))
                    V.tensor_tensor(vs[:, 2 * m:2 * m + 2, 256 * i:256 * i + 256],
                                    res[:, 2 * m:2 * m + 2, 256 * i:256 * i + 256],
                                    lng_b[:, 256 * i:256 * i + 256].unsqueeze(1).broadcast_to([P, 2, 256]), ALU.mult
                                    ).then_inc(x_gained, 1)
            dve.wait_ge(fin_squared, 16)
            add_parts()
            rsqrt(TT, 1.0 / D, made=4)
            dve.wait_ge(x_gained, 16)
            for t in (0, 2):
                V.tensor_scalar(res[:, t, :], vs[:, t, :], rstd[:, t:t + 1], None, ALU.mult).then_inc(fin_made, 1)

        @block.tensor
        def _(pe):
            T = nc.tensor
            PASSES = ((0, 0), (0, 1), (1, 0))

            def bank_due(g, m):
                if g >= 2:
                    if g - 2 in ACT_FREED:
                        pe.wait_ge(bank_free_act, act_freed(g - 2, m))
                    else:
                        pe.wait_ge(bank_free, dve_freed(g - 2, m))

            def unit(u, s, gs_, due, kind, k, w, acts, a=0, b=None, kacts=None, start=True, stop=True,
                     chunk_waits=None, w_by_chunk=False):
                per = 3 * k if kind == "F" else 6 * k
                b = 2 * per if b is None else b
                if a == 0 and not w_by_chunk:
                    pe.wait_ge(w_lo_made, u + 1)
                order = range(a, b)
                if chunk_waits is not None:
                    order = sorted(order, key=lambda n: (n % (3 * k)) // 3)
                    due(0)
                    due(1)
                full_at = [max(i for i, n in enumerate(order) if n // per == m) if any(n // per == m for n in order)
                           else None for m in range(2)]
                seen = 0
                for i, n in enumerate(order):
                    m, r = n // per, n % per
                    kk = (n % (3 * k)) // 3
                    if chunk_waits is not None and kk == seen:
                        pe.wait_ge(chunk_waits[0], chunk_waits[1] + kk + 1)
                        seen += 1
                    if r == 0 and start and chunk_waits is None:
                        due(m)
                    if kind == "F":
                        kk, (wp, ap) = r // 3, PASSES[r % 3]
                        wt = slot((w_hi, w_lo)[wp], s, k, w)
                        ins = T.matmul(ps_mm[:, 2 * gs_ + m, :], wt[:, kk, m * P:(m + 1) * P],
                                       acts[ap][:, kk, :], start=(r == 0), stop=(r == per - 1),
                                       skip_group_check=chunk_waits is not None)
                    else:
                        tt, r2 = r // (3 * k), r % (3 * k)
                        kk, (wp, ap) = r2 // 3, PASSES[r2 % 3]
                        t = 2 * m + tt
                        wt = slot((w_hi, w_lo)[wp], s, k, w)
                        k0 = kacts or 0
                        first = r == 0 if kacts is not None or chunk_waits is not None else r2 == 0
                        ins = T.matmul(ps_mm[:, 2 * gs_ + m, tt * w:(tt + 1) * w],
                                       acts[ap][:, k0 + kk, t * P:(t + 1) * P], wt[:, kk, :],
                                       start=first and start, stop=(r2 == 3 * k - 1) and stop,
                                       skip_group_check=kacts is not None or chunk_waits is not None)
                    if i == full_at[1] and b == 2 * per:
                        ins.then_inc(w_used, 1)
                    elif i == full_at[0] and b >= per and stop:
                        ins.then_inc(first_full, 1)

            acts_x = (act_hi, act_lo)

            def straight(u, kind, acts, a=0, b=None, chunk_waits=None, w_by_chunk=False):
                src, k, w = unit_source(u)
                g = group_of(u)
                unit(u, u % 2, g % 2, lambda m: bank_due(g, m), kind, k, w, acts, a, b,
                     chunk_waits=chunk_waits, w_by_chunk=w_by_chunk)

            def stream(st, p, acts):
                a, b = st.cuts[p], st.cuts[p + 1]
                while a < b:
                    i = a // st.per
                    e = min(b, (i + 1) * st.per)
                    straight(U0[st.name] + i, "F", acts, a - i * st.per, e - i * st.per)
                    a = e

            def turn_chunks(src, scaled, base):
                for t in range(TT):
                    pe.wait_ge(*scaled[t])
                    for k in range(4):
                        ins = T.transpose(side_bank(k)[:, t * P:(t + 1) * P], src[:, t, k * P:(k + 1) * P],
                                          ident[:, :])
                        if t == TT - 1:
                            ins.then_inc(norm_turned, 1)
                for k in range(4, KD):
                    pe.wait_ge(norm_lo, base + k - 3)
                    for t in range(TT):
                        ins = T.transpose(side_bank(k)[:, t * P:(t + 1) * P], src[:, t, k * P:(k + 1) * P], ident[:, :])
                    ins.then_inc(norm_turned, 1)

            def scaled_tiles(n):
                return [(norm_scaled_act if t % 2 else norm_scaled, 2 * n + t // 2 + 1) for t in range(TT)]

            pe.wait_ge(ident_made, 1)
            pe.wait_ge(rows_landed, 16 * len(ROWS))
            T.transpose(ps_t[:, 0:NROWS], rows[0:NROWS, :], ident[0:NROWS, 0:NROWS]).then_inc(cols_turned, 1)
            pe.wait_ge(cols_made, 1)
            turn_chunks(x_sc, scaled_tiles(0), 0)
            straight(0, "T", acts_x, chunk_waits=(norm_lo, 0), w_by_chunk=True)
            for u in range(1, 3):
                straight(u, "T", acts_x)
            straight(3, "F", acts_x)
            straight(4, "F", acts_x)
            pe.wait_ge(lat_scaled, 2 * TT)
            for i in range(6):
                if i >= 4:
                    pe.wait_ge(lat_lo, i - 3)
                for t in range(TT):
                    if i < 5:
                        ins = T.transpose(side_bank(i)[:, t * P:(t + 1) * P], lat[:, t, i * P:(i + 1) * P], ident[:, :])
                    else:
                        ins = T.transpose(side_bank(i)[0:MQ, t * P:(t + 1) * P], lat[:, t, LAT - MQ:LAT], ident[:, :])
                ins.then_inc(lat_turned, 1)
            straight(5, "F", acts_x)
            straight(6, "F", acts_x)
            lat_q = (lt_hi[:, 0:3, :], lt_lo[:, 0:3, :])
            lat_kv = (lt_hi[:, 3:5, :], lt_lo[:, 3:5, :])
            pe.wait_ge(lat_lo, 5)
            for i in range(3):
                straight(U0["qn"] + i, "F", lat_q)
            for i in range(2):
                straight(U0["kn"] + i, "F", lat_kv)
            for i in range(2):
                straight(U0["mv"] + i, "T", lat_kv)

            pe.wait_ge(bank_free, freed(U0["mv"] - 1, 1))
            pe.wait_ge(kpe_spread, MH)
            NP = 4 * MH
            for p in range(MLA_STEPS):
                if p < NP:
                    h, t = p // 4, p % 4
                    n = P * (t + 1)
                    if p >= 2:
                        pe.wait_ge(exp_made, p - 1)
                    if t == 0:
                        pe.wait_ge(q_spread, h + 1)
                    sb_ = ps_s[:, p % 2, :]
                    T.matmul(sb_[:, 0:n], qm[0:MQ, h, t * P:(t + 1) * P], km[0:MQ, h, 0:n], start=True, stop=False)
                    T.matmul(sb_[:, n - P:n], ident_r[:, :], causal_r[:, :], start=False, stop=True
                             ).then_inc(s_full, 1)
                q = p - LAG
                if q >= 0:
                    t = q % 4
                    pe.wait_ge(p_ready, q + 1)
                    if q >= 1:
                        pe.wait_ge(pt_made, q)
                    for j in range(t + 1):
                        ins = T.transpose(ps_t[:, j * P:(j + 1) * P], prob[:, q % 4, j * P:(j + 1) * P], ident[:, :])
                    ins.then_inc(t_full, 1)
                stream(MLA_STREAM, p, acts_x)
                if q >= 0:
                    h, t = q // 4, q % 4
                    if q == 0:
                        pe.wait_ge(bank_free, freed(U0["gate_b"] - 1, 1))
                    pe.wait_ge(pt_made, q + 1)
                    if t == 0 and h:
                        pe.wait_ge(o_free, h)
                    rr = slice((h % 2) * MV, (h % 2) * MV + MV)
                    for j in range(t + 1):
                        ins = T.matmul(ps_o[rr, t * P:(t + 1) * P], vm[:, j, h * MV:(h + 1) * MV],
                                       pt[:, q % 2, j * P:(j + 1) * P], start=(j == 0), stop=(j == t))
                    ins.then_inc(pv_done, 1)
            for name, kind in (("dq", "F"), ("dk", "F"), ("dv", "T")):
                for i in range(2):
                    straight(U0[name] + i, kind, acts_x)

            pe.wait_ge(bank_free, freed(U0["mrg_m"] - 1, 1))
            pe.wait_ge(o_free, MH)
            om = (om_hi, om_lo)
            NP = 4 * DH
            for p in range(DIFF_STEPS):
                if p < NP:
                    h, t = p // 4, p % 4
                    n = P * (t + 1)
                    for e in range(2):
                        if p >= 1:
                            pe.wait_ge(dExp, 2 * (p - 1) + e + 1)
                        rr = slice(e * DD, e * DD + DD)
                        T.matmul(ps_s[:, e, 0:n], dq[rr, h, t * P:(t + 1) * P], dk[rr, h, 0:n], start=True, stop=False)
                        T.matmul(ps_s[:, e, n - P:n], ident_r[:, :], causal_r[:, :], start=False, stop=True
                                 ).then_inc(dS, 1)
                q = p - LAG
                if 0 <= q < NP:
                    t = q % 4
                    pe.wait_ge(dP, q + 1)
                    if q >= 1:
                        pe.wait_ge(dPt, q)
                    if q >= 7 and (q - 7) % 4 == 0:
                        pe.wait_ge(od_made, (q - 7) // 4 + 1)
                    for j in range(t + 1):
                        ins = T.transpose(ps_t[:, j * P:(j + 1) * P], prob[:, q % 4, j * P:(j + 1) * P], ident[:, :])
                    ins.then_inc(dT, 1)
                stream(DIFF_STREAM, p, om)
                if 0 <= q < NP:
                    h, t = q // 4, q % 4
                    pe.wait_ge(dPt, q + 1)
                    if t == 0 and h:
                        pe.wait_ge(o_copied, 4 * h)
                    for j in range(t + 1):
                        ins = T.matmul(ps_o[:, t * P:(t + 1) * P], pt[:, q % 2, j * P:(j + 1) * P],
                                       dv[:, j, h * DV:(h + 1) * DV], start=(j == 0), stop=(j == t))
                    ins.then_inc(dPv, 1)
                if q >= 6 and (q - 6) % 4 == 0:
                    hd = (q - 6) // 4
                    pe.wait_ge(o_scaled, 4 * hd + 4)
                    pe.wait_ge(dPt, min(q + 1, NP))
                    for t in range(TT):
                        ins = T.transpose(ps_t[:, t * P:(t + 1) * P], o_sb[:, t * P:(t + 1) * P], ident[:, :])
                    ins.then_inc(o_turned, 1)
            for i in range(4):
                straight(U0["mrg_d"] + i, "F", (od_hi, od_lo), chunk_waits=(od_made, 0) if i == 0 else None)
            for i in range(4):
                straight(U0["out"] + i, "T", acts_x, chunk_waits=(merged_lo, 0) if i == 0 else None)
            turn_chunks(n_sc, scaled_tiles(1), KD)
            uf = U0["ffn"]
            for h in range(2):
                unit(uf + h, (uf + h) % 2, (uf + h) % 2, lambda m: bank_due(uf + h, m), "F", 8, 256, acts_x,
                     chunk_waits=(norm_lo, KD) if h == 0 else None)
            with pe.Fori(1, KF // 2) as j:
                for h in range(2):
                    def due(m):
                        if h == 0:
                            pe.wait_ge(bank_free_act, j * 2 + (m - 1))
                        else:
                            pe.wait_ge(bank_free, j * 2 + (freed(uf + 1, m) - 2))
                    unit(j * 2 + (uf + h), (uf + h) % 2, (uf + h) % 2, due, "F", 8, 256, acts_x)
            pe.wait_ge(bank_free_act, act_freed(group_of(U0["down"]) - 2, 1))
            pe.wait_ge(h_lo_made, sum(DOWN_K[:2]))
            ud = U0["down"]
            gd = group_of(ud)
            with pe.Fori(0, DOWN_GROUPS // 2) as j:
                for gg in range(2):
                    for i in range(3):
                        n = ud + 3 * gg + i
                        if i == 2:
                            pe.wait_ge(h_lo_made, KF)
                        def due(m):
                            pe.wait_ge(bank_free, j * 4 + (dve_freed(gd, m) + 2 * gg - 4))
                        unit(j * 6 + n, n % 2, (gd + gg) % 2, due, "T", DOWN_K[i], 256, (h_hi, h_lo),
                             kacts=sum(DOWN_K[:i]), start=(i == 0), stop=(i == 2))
            turn_chunks(n_sc, scaled_tiles(2), 2 * KD)
            for i in range(4):
                straight(U0["q2"] + i, "F", acts_x, chunk_waits=(norm_lo, 2 * KD) if i == 0 else None)
            straight(U0["kv2"], "F", acts_x)
            straight(U0["za"], "F", acts_x)
            pe.wait_ge(bank_free, freed(U0["kv2"], 1))
            for t in range(TT):
                ins = T.transpose(ps_t[:, t * P:(t + 1) * P], vt2[:, 0, t * P:(t + 1) * P], ident[:, :])
            ins.then_inc(v_turned, 1)
            for i in range(1, 4):
                straight(U0["za"] + i, "F", acts_x)
                if i == 2:
                    pe.wait_ge(wg_landed, 16)
                    pe.wait_ge(v2_made, 1)
                    for hb in range(2):
                        for g in range(4):
                            ins = T.transpose((ps_t, ps_o)[hb][:, g * P:(g + 1) * P], wg_in[:, 4 * hb + g, :],
                                              ident[:, :])
                        ins.then_inc(wg_turned, 1)
            pe.wait_ge(kdup_made, 4)
            pe.wait_ge(wg_made, 1)
            NP = WIN_PIECES
            for p in range(WIN_STEPS):
                if p < NP:
                    b, i = p // 8, p % 8
                    if p >= 2:
                        pe.wait_ge(exp2_made, 2 * (p - 1))
                    T.matmul(ps_s[:, p % 2, :], ident_r[:, :], window_r[:, :, :].rearrange("p e n -> p (e n)"),
                             start=True, stop=False)
                    j0 = 0 if b else P
                    k0 = (b - 1) * P if b else 0
                    rr = slice((i % 2) * AD, (i % 2) * AD + AD)
                    for e in range(2):
                        ins = T.matmul(ps_s[:, p % 2, e * 256 + j0:e * 256 + 256],
                                       q2[rr, 2 * (i // 2) + e, b * P:(b + 1) * P],
                                       kdup[rr, i // 4, k0:(b + 1) * P], start=False, stop=(e == 1))
                    ins.then_inc(s2_full, 1)
                q = p - LAG
                if 0 <= q < NP:
                    pe.wait_ge(exp2_made, 2 * (q + 1))
                    if q >= 1:
                        pe.wait_ge(pt2_made, q)
                    if q >= 5 and (q - 5) % 4 == 0:
                        pe.wait_ge(a_gated, (q - 5) // 4 + 1)
                    for e in range(2):
                        for kb in range(0 if q // 8 else 1, 2):
                            c = (2 * e + kb) * P
                            ins = T.transpose(ps_t[:, c:c + P], prob2[:, q % 4, c:c + P], ident[:, :])
                    ins.then_inc(t2_full, 1)
                stream(WIN_STREAM, p, acts_x)
                if 0 <= q < NP:
                    b, i = q // 8, q % 8
                    pe.wait_ge(pt2_made, q + 1)
                    if q % 4 == 0 and q:
                        pe.wait_ge(a_kept, q // 4)
                    for e in range(2):
                        o = window_head(i % 4, e) * AD
                        for kb in range(0 if b else 1, 2):
                            c = (2 * e + kb) * P
                            ins = T.matmul(ps_o[:, o:o + AD], pt2[:, q % 2, c:c + P],
                                           v2[:, b - 1 + kb, (i // 4) * AD:(i // 4 + 1) * AD],
                                           start=(kb == (0 if b else 1)), stop=(kb == 1))
                    ins.then_inc(pv2_done, 1)
                if q >= 4 and q % 4 == 0:
                    g8 = (q - 4) // 4
                    pe.wait_ge(a_kept, g8 + 1)
                    pe.wait_ge(pt2_made, min(q + 1, NP))
                    for c in range(4):
                        ins = T.transpose(ps_t[:, c * P:(c + 1) * P], a_tok[:, g8 % 2, c * P:(c + 1) * P], ident[:, :])
                    ins.then_inc(a_turned, 1)
            for i in range(4):
                straight(U0["u2"] + i, "F", acts_x)
            for i in range(4):
                straight(U0["vs"] + i, "T", acts_x)
            for i in range(4):
                straight(U0["ga"] + i, "F", acts_x)
            pe.wait_ge(at_lo_made, KD)
            for i in range(4):
                straight(U0["att"] + i, "F", (at_hi, at_lo))
            pe.wait_ge(vs_normed, TT)
            for g in range(8):
                if g >= 4:
                    pe.wait_ge(sg_lo_made, g - 3)
                for b in range(TT):
                    ins = T.matmul(side_bank(g)[:, b * P:(b + 1) * P], vs[:, b, g * P:(g + 1) * P], wg_t[:, g, :],
                                   start=True, stop=True)
                ins.then_inc(mix_full, 1)
            for i in range(4):
                straight(U0["gs"] + i, "F", acts_x)
            pe.wait_ge(sg_lo_made, 8)
            for i in range(4):
                straight(U0["sgo"] + i, "F", (at_hi, at_lo))
            for i in range(4):
                straight(U0["wo"] + i, "T", acts_x, chunk_waits=(y_lo_made, 0) if i == 0 else None)


_INS = ["x", "positions", "norm_mix_g", "w_in", "b_gate", "mla_q_norm_g", "mla_w_uq", "mla_kv_norm_g", "mla_w_ukv",
        "diff_lambda_q1", "diff_lambda_k1", "diff_lambda_q2", "diff_lambda_k2", "diff_subln_g", "w_branch_mla",
        "w_branch_diff", "w_out", "norm_ffn_g", "w_ffn_gate", "w_ffn_up", "w_ffn_down", "norm_final_g", "norm_g_2",
        "w_in_2", "b_merge_2", "att_sinks_2", "sg_w_2", "sg_b_2", "sg_ln_g_2", "sg_ln_b_2", "w_att_out_2",
        "w_sg_out_2", "w_o_2", "final_g_2"]


def rope_frequencies():
    import numpy as np

    f = np.zeros((P, 2), np.float32)
    theta = np.float64(500000.0)
    for i in range(MR // 2):
        w = np.float32(theta ** (-2.0 * i / MR))
        for r in range(0, P, MR):
            f[r + i, 0], f[r + MR // 2 + i, 0] = -w, w
    rot = DD // 4
    for i in range(rot // 2):
        w = np.float32(theta ** (-2.0 * i / rot))
        for r in (0, DD):
            f[r + i, 1], f[r + rot // 2 + i, 1] = -w, w
    return f


def kernel(**inputs):
    import numpy as np
    import concourse.bacc as bacc
    from concourse.bass_utils import run_bass_kernel_spmd

    nc = bacc.Bacc("TRN2", target_bir_lowering=False, num_devices=1)
    arrays, aps = {}, {}
    for name in _INS:
        a = np.ascontiguousarray(inputs[name])
        arrays[f"in_{name}"] = a
        aps[name] = nc.dram_tensor(f"in_{name}", a.shape, mybir.dt.from_np(a.dtype), kind="ExternalInput").ap()
    arrays["rope_freq"] = rope_frequencies()
    aps["rope_freq"] = nc.dram_tensor("rope_freq", (P, 2), F32, kind="ExternalInput").ap()
    aps["out"] = nc.dram_tensor("out", (1, S, D), F32, kind="ExternalOutput").ap()
    build(nc, aps)
    r = run_bass_kernel_spmd(nc, [arrays], core_ids=[0])
    return r.results[0]["out"]
```

```python
import math
from contextlib import ExitStack

import concourse.bass as bass
from concourse import mybir

ALU = mybir.AluOpType
ACT = mybir.ActivationFunctionType
AX = mybir.AxisListType
F32 = mybir.dt.float32
F32R = mybir.dt.float32r
I32 = mybir.dt.int32

P = 128
S = 512
TT = S // P
D = 1024
KD = D // P
UNIT = 2048
EPS = 1e-6
NEG = -1e30

MH, MN, MR, MV = 8, 64, 32, 64
MQ = MN + MR
QR, KVR = 384, 256
LAT = QR + KVR + MR
DH, DD, DV = 4, 64, 128
FF = 2816
KF = FF // P
LAMBDA_INIT = 0.8 - 0.6 * math.exp(0.0)
AH, AG, AD = 16, 2, 64
CHUNK = 64

ROWS = [("norm_mix_g", 8), ("b_gate", 16), ("mla_q_norm_g", 3), ("mla_kv_norm_g", 2), ("diff_subln_g", 1),
        ("norm_ffn_g", 8), ("norm_g_2", 8), ("b_merge_2", 16)]
ROW0 = {}
for _n, _c in ROWS:
    ROW0[_n] = sum(c for _, c in ROWS[:len(ROW0)])
NROWS = sum(c for _, c in ROWS)

COUNTS = [("lat", 3), ("gate_a", 4), ("qn", 2), ("qp", 1), ("kn", 2), ("mv", 2), ("gate_b", 4), ("dq", 2), ("dk", 2),
          ("dv", 2), ("mrg_m", 4), ("mrg_d", 4), ("out", 4), ("ffn", 22), ("down", 12),
          ("q2", 4), ("kv2", 1), ("za", 4), ("zs", 4), ("u2", 4), ("vs", 4), ("ga", 4), ("att", 4), ("gs", 4),
          ("sgo", 4), ("wo", 4)]
U0 = {}
_u = 0
for _n, _c in COUNTS:
    U0[_n] = _u
    _u += _c
NU = _u
DOWN_GROUPS = 4
DOWN_K = (8, 8, 6)


def group_of(u):
    d = U0["down"]
    if u < d:
        return u
    if u < d + 12:
        return d + (u - d) // 3
    return u - 12 + DOWN_GROUPS


def window_head(i, e):
    return 4 * (i // 2) + i % 2 + 2 * e


ACT_FREED = ([group_of(U0[n]) + i for n in ("gate_a", "gate_b") for i in range(4)]
             + [group_of(U0["ffn"]) + 2 * j for j in range(KF // 2)]
             + [group_of(U0[n]) + i for n in ("za", "ga", "gs") for i in range(4)])

LAG = 3


class Stream:

    def __init__(self, name, units, per, weights):
        self.name, self.per = name, per
        self.cuts = [units * per * sum(weights[:p]) // sum(weights) for p in range(len(weights) + 1)]

        def step_of(n):
            return next(p for p in range(len(weights)) if self.cuts[p + 1] > n)

        self.banks = {}
        self.starts = {}
        for i in range(units):
            self.starts[step_of(i * per)] = U0[name] + i
            for m in range(2):
                self.banks.setdefault(step_of(i * per + (m + 1) * per // 2 - 1) + 1, []).append((i, m))

    def started(self, p):
        return self.starts.get(p)


MLA_STEPS = 4 * MH + LAG
MLA_STREAM = Stream("gate_b", 4, 48, [0, 0, 1] + [2] * (MLA_STEPS - 3))
DIFF_STEPS = 4 * DH + LAG + 4
DIFF_STREAM = Stream("mrg_m", 4, 24, [2] * 4 * DH + [3] * LAG + [4, 4, 4, 0])
WIN_PIECES = 32
WIN_STEPS = WIN_PIECES + LAG + 2
WIN_STREAM = Stream("zs", 4, 48, [1] * WIN_STEPS)


def act_freed(g, m):
    return 2 * sum(a < g for a in ACT_FREED) + m + 1


def dve_freed(g, m):
    return 2 * (g - sum(a < g for a in ACT_FREED)) + m + 1


def scaled_when(t, n, by_dve, by_act):
    d, a = 3 * (n - 1), 2 * (n - 1)
    return (((by_dve, d + 1),), ((by_act, a + 1),), ((by_dve, d + 2),), ((by_dve, d + 3), (by_act, a + 2)))[t]


def freed(u, m):
    return dve_freed(group_of(u), m)


def build(nc, A):
    with ExitStack() as ctx:
        def sem(name):
            return ctx.enter_context(nc.semaphore(name))

        def sems(names):
            return [sem(n) for n in names.split()]

        def keep(name, shape, dt=F32):
            return ctx.enter_context(nc.sbuf_tensor(name, shape, dt))

        def overlay(*tensors):
            with ExitStack() as sub:
                return [sub.enter_context(nc.sbuf_tensor(n, s, d)) for n, s, d in tensors]

        stage = keep("stage", [P, 2, UNIT])
        w_hi = keep("w_hi", [P, 2, UNIT], F32R)
        w_lo = keep("w_lo", [P, 2, UNIT], F32R)
        act_hi = keep("act_hi", [P, KD, S], F32R)
        act_lo = keep("act_lo", [P, KD, S], F32R)
        ident = keep("ident", [P, P])
        ident_r = keep("ident_r", [P, P], F32R)
        causal_r = keep("causal_r", [P, P], F32R)
        window_r = keep("window_r", [P, 2, 2 * P], F32R)
        col = keep("col", [P, NROWS])
        hcol = keep("hcol", [P, NROWS])
        freq = keep("freq", [P, 2])
        small = keep("small", [P, 384])
        rope2 = keep("rope2", [P, 2, S])
        tmp = keep("tmp", [P, 2, S])

        (rope_m, rope_d, pt) = overlay(("rope_m", [P, 2, S], F32), ("rope_d", [P, 2, S], F32), ("pt", [P, 2, S], F32))
        (p2, o_sb, o_sq) = overlay(("p2", [P, 2, S], F32), ("o_sb", [P, S], F32), ("o_sq", [P, S], F32))
        res = keep("res", [P, TT, D])

        (x_in, x_sc, rows, lamv, pos_i, pos_i2, pos_f, rt) = overlay(
            ("x_in", [P, TT, D], F32), ("x_sc", [P, TT, D], F32), ("rows", [P, P], F32), ("lamv", [P, 4, DD], F32),
            ("pos_i", [P, S], I32), ("pos_i2", [P, S], I32), ("pos_f", [P, 2, S], F32), ("rt", [P, 4, S], F32))
        with ExitStack() as b1:
            def b1keep(name, shape, dt=F32):
                return b1.enter_context(nc.sbuf_tensor(name, shape, dt))

            gates = b1keep("gates", [P, 16, S])
            with ExitStack() as sub:
                lt_hi = sub.enter_context(nc.sbuf_tensor("lt_hi", [P, 5, S], F32R))
                lt_lo = sub.enter_context(nc.sbuf_tensor("lt_lo", [P, 5, S], F32R))
            om_hi = b1keep("om_hi", [P, 4, S], F32R)
            om_lo = b1keep("om_lo", [P, 4, S], F32R)
            prob = b1keep("prob", [P, 4, S])
            with ExitStack() as sub:
                qm, km, vm = [sub.enter_context(nc.sbuf_tensor(n, s, F32)) for n, s in (
                    ("qm", [P, MH, S]), ("km", [P, MH, S]), ("vm", [P, TT, MH * MV]))]
            with ExitStack() as sub:
                sub.enter_context(nc.sbuf_tensor("pad_lat", [P, MH, S], F32))
                lat = sub.enter_context(nc.sbuf_tensor("lat", [P, TT, LAT], F32))
            with ExitStack() as sub:
                dq, dk, dv = [sub.enter_context(nc.sbuf_tensor(n, [P, TT, S], F32)) for n in ("dq", "dk", "dv")]
                od_hi = sub.enter_context(nc.sbuf_tensor("od_hi", [P, DH, S], F32R))
                od_lo = sub.enter_context(nc.sbuf_tensor("od_lo", [P, DH, S], F32R))
        (h_hi, h_lo, sl, gf_b) = overlay(("h_hi", [P, KF, S], F32R), ("h_lo", [P, KF, S], F32R),
                                         ("sl", [P, 2, S], F32), ("gf_b", [P, D], F32))
        (n_sc,) = overlay(("n_sc", [P, TT, D], F32))
        with ExitStack() as b2:
            def b2keep(name, shape, dt=F32):
                return b2.enter_context(nc.sbuf_tensor(name, shape, dt))

            def b2share(*tensors):
                with ExitStack() as sub:
                    return [sub.enter_context(nc.sbuf_tensor(n, s, d)) for n, s, d in tensors]

            gz = b2keep("gz", [P, KD, S])
            (wg_in,) = b2share(("pad_wg", [P, 6 * S], F32), ("wg_in", [P, 8, P], F32))[1:]
            gu = b2keep("gu", [P, KD, S])
            q_split, k_hi, k_lo, v2, prob2, pt2, a_tok = b2share(
                ("q_split", [P, AH, S], F32R), ("k_hi", [P, AG, S], F32R), ("k_lo", [P, AG, S], F32R),
                ("v2", [P, TT, P], F32), ("prob2", [P, 4, S], F32), ("pt2", [P, 2, S], F32), ("a_tok", [P, 2, S], F32))
            (kv,) = b2share(("pad_kv", [P, 27 * S], F32), ("kv", [P, 2, S], F32))[1:]
            vs = b2keep("vs", [P, TT, D])
            at_hi = b2keep("at_hi", [P, KD, S], F32R)
            at_lo = b2keep("at_lo", [P, KD, S], F32R)
            sgb_b = b2keep("sgb_b", [P, 8, P])
            lng_b = b2keep("lng_b", [P, D])
            lnb_b = b2keep("lnb_b", [P, D])
            wg_t = b2keep("wg_t", [P, 8, P])
        act_y = act_hi[:, :, :].bitcast(F32).rearrange("p (t a) n -> p t (a n)", t=TT)

        ps_mm = ctx.enter_context(nc.psum_tensor("ps_mm", [P, 4, S], F32))
        ps_s = ctx.enter_context(nc.psum_tensor("ps_s", [P, 2, S], F32))
        ps_t = ctx.enter_context(nc.psum_tensor("ps_t", [P, S], F32))
        ps_o = ctx.enter_context(nc.psum_tensor("ps_o", [P, S], F32))

        def side_bank(k):
            return (ps_s[:, 0, :], ps_s[:, 1, :], ps_t[:, :], ps_o[:, :])[k % 4]

        at = [0]

        def cut(n):
            at[0] += n
            assert at[0] <= 384
            return small[:, at[0] - n:at[0]]

        ssq, var, rstd, newton = cut(16), cut(16), cut(16), cut(16)
        part = cut(32)
        nmax, rsum, rinv = cut(8), cut(8), cut(8)
        lsum, lexp, neglam = cut(2), cut(2), cut(1)
        sinkb, nsinkb, nm2, rs2 = cut(16), cut(16), cut(32), cut(32)
        dsink, esink, den2, rden2 = cut(8), cut(8), cut(8), cut(8)
        diff_sum = cut(16)
        diff_rinv, mix = cut(8), cut(4)
        diff_ssq, diff_var, diff_rstd, diff_nt = cut(4), cut(4), cut(4), cut(4)
        vsum, mean, nmean = cut(16), cut(4), cut(4)
        halfpi = cut(1)

        w_landed = [sem("w_landed0"), sem("w_landed1")]
        w_hi_made, w_lo_made, w_used = sems("w_hi_made w_lo_made w_used")
        first_bank_full, bank_free, bank_free_act = sems("first_bank_full bank_free bank_free_act")
        x_landed = [sem(f"x_landed{t}") for t in range(TT)]
        (rows_landed, pos_landed, lam_landed, freq_landed, sink_landed, res_landed, gf_landed, wg_landed,
         sgb_landed, ln_landed, fg_landed, out_written) = sems(
            "rows_landed pos_landed lam_landed freq_landed sink_landed res_landed gf_landed wg_landed "
            "sgb_landed ln_landed fg_landed out_written")
        (ident_made, consts_made, iota_made, cols_turned, cols_made) = sems(
            "ident_made consts_made iota_made cols_turned cols_made")
        dve_chain, act_chain, pool_chain = sems("dve_chain act_chain pool_chain")
        (norm_squared, rstd_made, norm_scaled, norm_scaled_act, norm_turned, norm_hi, norm_lo) = sems(
            "norm_squared rstd_made norm_scaled norm_scaled_act norm_turned norm_hi norm_lo")
        angle_ready, sincos_made, lam_summed, lam_exp = sems("angle_ready sincos_made lam_summed lam_exp")
        (lat_squared, lat_scaled, lat_turned, lat_hi, lat_lo, kpe_spread) = sems(
            "lat_squared lat_scaled lat_turned lat_hi lat_lo kpe_spread")
        nope_kept, qp_roped, q_spread = sems("nope_kept qp_roped q_spread")
        (s_full, max_made, exp_made, p_ready, t_full, pt_made, pv_done, o_hi_made, o_free) = sems(
            "s_full max_made exp_made p_ready t_full pt_made pv_done o_hi_made o_free")
        (diff_s_full, diff_max_made, diff_exp_made, diff_p_ready, diff_t_full, diff_pt_made, diff_pv_done,
         diff_rinv_made) = sems(
            "diff_s_full diff_max_made diff_exp_made diff_p_ready diff_t_full diff_pt_made diff_pv_done "
            "diff_rinv_made")
        (o_copied, o_squared, diff_rstd_made, o_scaled, o_turned, od_hi_made, od_made) = sems(
            "o_copied o_squared diff_rstd_made o_scaled o_turned od_hi_made od_made")
        merged, merged_hi, merged_lo, h_hi_made, h_lo_made = sems("merged merged_hi merged_lo h_hi_made h_lo_made")
        x_gained, down_squared, x3_made = sems("x_gained down_squared x3_made")
        (q2_roped, q2_hi_made, q2_lo_made, k_roped, k_hi_made, k_lo_made, v_turned, v2_made, wg_turned, wg_made) = sems(
            "q2_roped q2_hi_made q2_lo_made k_roped k_hi_made k_lo_made v_turned v2_made wg_turned wg_made")
        (win_s_full, win_max_made, win_exp_made, win_t_full, win_pt_made, win_pv_done, z_tanh, sink_diff,
         sink_exp, a_kept, a_turned, a_gated, at_hi_made, at_lo_made) = sems(
            "win_s_full win_max_made win_exp_made win_t_full win_pt_made win_pv_done z_tanh sink_diff sink_exp "
            "a_kept a_turned a_gated at_hi_made at_lo_made")
        (gelu_made, vs_summed, vs_squared, vs_normed, mix_full, mix_gated, sg_hi_made, sg_lo_made) = sems(
            "gelu_made vs_summed vs_squared vs_normed mix_full mix_gated sg_hi_made sg_lo_made")
        (y_sum, y_hi_made, y_lo_made, fin_squared, fin_made, fin_made_act) = sems(
            "y_sum y_hi_made y_lo_made fin_squared fin_made fin_made_act")

        def chunks(ap):
            return ap.rearrange("a (k p) n -> p (a k) n", p=P)

        w_in, w_in2 = chunks(A["w_in"]), chunks(A["w_in_2"])
        w_gate, w_up, w_down = chunks(A["w_ffn_gate"]), chunks(A["w_ffn_up"]), chunks(A["w_ffn_down"])
        uq = A["mla_w_uq"].rearrange("a (k p) (h e) -> p (a k) h e", p=P, e=MQ)
        ukv = A["mla_w_ukv"].rearrange("a (k p) (h e) -> p (a k) h e", p=P, e=MN + MV)
        wbm, wbd, wout = chunks(A["w_branch_mla"]), chunks(A["w_branch_diff"]), chunks(A["w_out"])
        wao, wso, wo2 = chunks(A["w_att_out_2"]), chunks(A["w_sg_out_2"]), chunks(A["w_o_2"])
        C_DQ, C_DK, C_DV = LAT, LAT + 512, LAT + 1024
        C_G = LAT + 1536
        C2 = {"q2": 0, "kv2": 1024, "za": 1280, "u2": 2304, "vs": 3328, "zs": 4352, "ga": 5376, "gs": 6400}

        def unit_source(u):
            name = [n for n, c in COUNTS if U0[n] <= u < U0[n] + c][0]
            i = u - U0[name]
            w = 256
            c0 = 256 * i
            if name == "lat":
                w = 256 if i < 2 else LAT - 512
                return w_in[:, :, c0:c0 + w], 8, w
            if name == "gate_a":
                return w_in[:, :, C_G + c0:C_G + c0 + w], 8, w
            if name == "gate_b":
                return w_in[:, :, C_G + 1024 + c0:C_G + 1024 + c0 + w], 8, w
            if name == "qn":
                return uq[:, :, 4 * i:4 * i + 4, 0:MN], 3, 256
            if name == "qp":
                return uq[:, :, :, MN:MQ], 3, 256
            if name == "kn":
                return ukv[:, :, 4 * i:4 * i + 4, 0:MN], 2, 256
            if name == "mv":
                return ukv[:, :, 4 * i:4 * i + 4, MN:MN + MV], 2, 256
            if name in ("dq", "dk", "dv"):
                b = {"dq": C_DQ, "dk": C_DK, "dv": C_DV}[name]
                return w_in[:, :, b + c0:b + c0 + w], 8, w
            if name == "mrg_m":
                return wbm[:, :, c0:c0 + w], 4, w
            if name == "mrg_d":
                return wbd[:, :, c0:c0 + w], 4, w
            if name in ("out", "att", "sgo", "wo"):
                m = {"out": wout, "att": wao, "sgo": wso, "wo": wo2}[name]
                return m[:, :, c0:c0 + w], 8, w
            return w_in2[:, :, C2[name] + c0:C2[name] + c0 + w], 8, w

        def slot(t, s, k, w):
            return t[:, s, 0:k * w].rearrange("p (k n) -> p k n", k=k)

        block = ctx.enter_context(nc.Block())

        @block.sync
        def _(sp):
            def load(u, s, src, k, w):
                dst = slot(stage, s, k, w)
                if len(src.shape) == 4:
                    dst = dst.rearrange("p k (h e) -> p k h e", h=src.shape[2])
                    for kk in range(k):
                        sp.dma_start(dst[:, kk], src[:, kk]).then_inc(w_landed[s], 16)
                else:
                    sp.dma_start(dst, src).then_inc(w_landed[s], 16)

            def straight(u):
                if u >= 2:
                    sp.wait_ge(w_lo_made, u - 1)
                load(u, u % 2, *unit_source(u))

            xv = A["x"].rearrange("a (t p) d -> p (a t) d", p=P)
            for t in range(TT):
                sp.dma_start(x_in[:, t, :], xv[:, t, :]).then_inc(x_landed[t], 16)
            for name, n in ROWS:
                sp.dma_start(rows[ROW0[name]:ROW0[name] + n, :],
                             A[name].rearrange("a (r p) -> (a r) p", p=P)).then_inc(rows_landed, 16)
            straight(0)
            sp.dma_start(freq[:, :], A["rope_freq"]).then_inc(freq_landed, 16)
            sp.dma_start(pos_i[:, :], A["positions"].broadcast_to([P, S])).then_inc(pos_landed, 16)
            for i, name in enumerate(("diff_lambda_q1", "diff_lambda_k1", "diff_lambda_q2", "diff_lambda_k2")):
                sp.dma_start(lamv[:, i, :], A[name].broadcast_to([P, DD])).then_inc(lam_landed, 16)
            sp.dma_start(sinkb, A["att_sinks_2"].broadcast_to([P, AH])).then_inc(sink_landed, 16)
            for u in range(1, U0["out"]):
                straight(u)
            sp.wait_ge(od_made, DH)
            sp.wait_ge(diff_pv_done, 4 * DH)
            for t in range(TT):
                sp.dma_start(res[:, t, :], xv[:, t, :]).then_inc(res_landed, 16)
            for u in range(U0["out"], U0["ffn"]):
                straight(u)
            u0 = U0["ffn"]
            with sp.Fori(0, KF // 2) as j:
                for h, wv in enumerate((w_gate, w_up)):
                    lo_due = sp.snap(j * 2 + (u0 + h - 1))
                    c0 = sp.snap(j * 256)
                    sp.wait_ge(w_lo_made, lo_due)
                    s = (u0 + h) % 2
                    sp.dma_start(slot(stage, s, 8, 256), wv[:, :, bass.ds(c0, 256)]).then_inc(w_landed[s], 16)
            sp.dma_start(gf_b[:, :], A["norm_final_g"].rearrange("(a d) -> a d", a=1).broadcast_to([P, D])
                         ).then_inc(gf_landed, 16)
            u0 = U0["down"]
            with sp.Fori(0, DOWN_GROUPS // 2) as j:
                for gg in range(2):
                    c0 = sp.snap(j * 512 + gg * 256)
                    for i in range(3):
                        lo_due = sp.snap(j * 6 + (u0 + 3 * gg + i - 1))
                        sp.wait_ge(w_lo_made, lo_due)
                        s = (u0 + 3 * gg + i) % 2
                        k0 = sum(DOWN_K[:i])
                        sp.dma_start(slot(stage, s, DOWN_K[i], 256),
                                     w_down[:, k0:k0 + DOWN_K[i], bass.ds(c0, 256)]).then_inc(w_landed[s], 16)
            for u in range(U0["q2"], NU):
                if u == U0["za"] + 1:
                    sp.dma_start(wg_in[:, :, :], A["sg_w_2"].rearrange("a g i j -> i (a g) j")).then_inc(wg_landed, 16)
                if u == U0["u2"] + 2:
                    sp.wait_ge(win_pv_done, WIN_PIECES)
                    sp.wait_ge(a_turned, 8)
                    sp.dma_start(sgb_b[:, :, :].rearrange("p g i -> p (g i)"),
                                 A["sg_b_2"].rearrange("a g i -> a (g i)").broadcast_to([P, D])
                                 ).then_inc(sgb_landed, 16)
                    sp.dma_start(lng_b[:, :], A["sg_ln_g_2"].broadcast_to([P, D])).then_inc(ln_landed, 16)
                    sp.dma_start(lnb_b[:, :], A["sg_ln_b_2"].broadcast_to([P, D])).then_inc(ln_landed, 16)
                if u == U0["wo"]:
                    sp.wait_ge(vs_normed, TT)
                    sp.dma_start(lng_b[:, :], A["final_g_2"].rearrange("(a d) -> a d", a=1).broadcast_to([P, D])
                                 ).then_inc(fg_landed, 16)
                straight(u)
            ov = A["out"].rearrange("a (t p) d -> p (a t) d", p=P)
            for t in range(TT):
                for done, count in scaled_when(t, 1, fin_made, fin_made_act):
                    sp.wait_ge(done, count)
                sp.dma_start(ov[:, t, :], res[:, t, :]).then_inc(out_written, 16)
            sp.wait_ge(out_written, 16 * TT)

        def landed_count(u):
            def dmas(v):
                return 3 if U0["qn"] <= v < U0["kn"] else 2 if U0["kn"] <= v < U0["gate_b"] else 1
            return 16 * sum(dmas(v) for v in range(u % 2, u + 1, 2))

        @block.gpsimd
        def _(pool):
            pool.memset(ident[:, :], 1.0).then_inc(pool_chain, 1)
            pool.memset(tmp[:, 0, 0:P], 0.0).then_inc(pool_chain, 1)
            pool.memset(tmp[:, 1, :], 0.0).then_inc(pool_chain, 1)
            pool.memset(halfpi, math.pi / 2).then_inc(pool_chain, 1)
            pool.iota(pos_i2[:, :], pattern=[[1, S]], base=0, channel_multiplier=0).then_inc(iota_made, 1)
            pool.wait_ge(pool_chain, 4)
            pool.affine_select(out=ident[:, :], in_=ident[:, :], compare_op=ALU.is_equal, fill=0.0, base=0,
                               pattern=[[-1, P]], channel_multiplier=1).then_inc(ident_made, 1)
            pool.affine_select(out=tmp[:, 0, 0:P], in_=tmp[:, 0, 0:P], compare_op=ALU.is_ge, fill=NEG, base=0,
                               pattern=[[-1, P]], channel_multiplier=1).then_inc(consts_made, 1)
            wv = tmp[:, 1, :].rearrange("p (e n) -> p e n", e=2)
            for e in range(2):
                pool.wait_ge(consts_made, 2 * e + 1)
                pool.memset(wv[CHUNK:P, e, 0:CHUNK], NEG).then_inc(consts_made, 1)
                pool.wait_ge(consts_made, 2 * e + 2)
                pool.memset(wv[0:CHUNK, e, 2 * P - CHUNK:2 * P], NEG).then_inc(consts_made, 1)

            G = nc.gpsimd
            linked = [4]

            def linked_after(ins):
                linked[0] += 1
                ins.then_inc(pool_chain, 1)
                pool.wait_ge(pool_chain, linked[0])

            v, y, t = diff_var, diff_rstd, diff_nt
            for hd in range(DH):
                pool.wait_ge(o_squared, TT * (hd + 1))
                linked_after(G.tensor_scalar(v, diff_ssq, 1.0 / DV, EPS, ALU.mult, ALU.add))
                if hd:
                    pool.wait_ge(o_scaled, TT * hd)
                linked_after(G.tensor_scalar(y.bitcast(I32), v.bitcast(I32), -0.5, float(0x5f3759df),
                                             ALU.mult, ALU.add))
                for step in range(3):
                    linked_after(G.tensor_tensor(t, y, y, ALU.mult))
                    linked_after(G.tensor_tensor(t, t, v, ALU.mult))
                    linked_after(G.tensor_scalar(t, t, -0.5, 1.5, ALU.mult, ALU.add))
                    if step < 2:
                        linked_after(G.tensor_tensor(y, y, t, ALU.mult))
                    else:
                        G.tensor_tensor(y, y, t, ALU.mult).then_inc(diff_rstd_made, 1)
                        pool.wait_ge(diff_rstd_made, hd + 1)

        @block.scalar
        def _(act):
            def hi(u):
                s = u % 2
                src, k, w = unit_source(u)
                act.wait_ge(w_landed[s], landed_count(u))
                if u >= 2:
                    act.wait_ge(w_used, u - 1)
                nc.scalar.activation(w_hi[:, s, 0:k * w], stage[:, s, 0:k * w], ACT.Copy).then_inc(w_hi_made, 1)

            def bank(u, m):
                g = group_of(u)
                if m == 0:
                    act.wait_ge(first_bank_full, g + 1)
                else:
                    act.wait_ge(w_used, u + 1)
                return ps_mm[:, 2 * (g % 2) + m, :]

            def hi_half(u, h):
                s = u % 2
                src, k, w = unit_source(u)
                act.wait_ge(w_landed[s], landed_count(u))
                if u >= 2:
                    act.wait_ge(w_used, u - 1)
                n = k * w // 2
                ins = nc.scalar.activation(w_hi[:, s, h * n:(h + 1) * n], stage[:, s, h * n:(h + 1) * n], ACT.Copy)
                if h:
                    ins.then_inc(w_hi_made, 1)

            def squares(src, out, acc, signal):
                nc.scalar.activation(out, src, ACT.Square, accum_out=acc).then_inc(signal, 1)

            def norm_hi_chunk(row, base, k):
                act.wait_ge(norm_turned, base + k + 1)
                nc.scalar.activation(act_hi[:, k, :], side_bank(k), ACT.Copy,
                                     scale=col[:, ROW0[row] + k:ROW0[row] + k + 1]).then_inc(norm_hi, 1)

            def norm_hi_chunks(row, base):
                for k in range(KD):
                    norm_hi_chunk(row, base, k)

            def gate_bank(u, m, c):
                nc.scalar.activation(gates[:, c, :], bank(u, m), ACT.Tanh, scale=0.5,
                                     bias=hcol[:, ROW0["b_gate"] + c:ROW0["b_gate"] + c + 1]).then_inc(bank_free_act, 1)

            def scale_tiles(out, src, c0=0, signal=norm_scaled_act):
                for t, n in ((1, D), (3, D // 2)):
                    nc.scalar.activation(out[:, t, 0:n], src[:, t, 0:n], ACT.Copy, scale=rstd[:, c0 + t:c0 + t + 1]
                                         ).then_inc(signal, 1)

            def half_scale(m, made, out, src, signal):
                act.wait_ge(rstd_made, made)
                t, n = ((1, D), (3, D // 2))[m]
                nc.scalar.activation(out[:, t, 0:n], src[:, t, 0:n], ACT.Copy, scale=rstd[:, t:t + 1]
                                     ).then_inc(signal, 1)

            def part_squares(n0, m, i, kind, src, out, signal):
                for t in (2 * m, 2 * m + 1):
                    c = 16 * kind + 4 * i + t
                    squares(src[:, t, n0:n0 + 256], out[:, 256 * (t % 2):256 * (t % 2) + 256], part[:, c:c + 1], signal)

            for t in range(TT):
                act.wait_ge(x_landed[t], 16)
                squares(x_in[:, t, :], x_sc[:, t, :], ssq[:, t:t + 1], norm_squared)
            act.wait_ge(rstd_made, 1)
            scale_tiles(x_sc, x_in)
            act.wait_ge(cols_made, 1)
            act.wait_ge(w_landed[0], landed_count(0))
            for k in range(KD):
                cc = slice(256 * k, 256 * k + 256)
                ins = nc.scalar.activation(w_hi[:, 0, cc], stage[:, 0, cc], ACT.Copy)
                if k == KD - 1:
                    ins.then_inc(w_hi_made, 1)
                norm_hi_chunk("norm_mix_g", 0, k)
            hi(1)
            act.wait_ge(lam_summed, 1)
            nc.scalar.activation(lexp, lsum, ACT.Exp).then_inc(lam_exp, 1)
            for n, tab in enumerate((rope_m, rope_d, rope2)):
                act.wait_ge(angle_ready, n + 1)
                nc.scalar.activation(tab[:, 1, :], rt[:, 2, :], ACT.Sin).then_inc(act_chain, 1)
                nc.scalar.activation(tab[:, 0, :], rt[:, 3, :], ACT.Sin, scale=-1.0, bias=halfpi
                                     ).then_inc(sincos_made, 1)
                if n < 2:
                    hi(2 + n)
            hi(4)
            act.wait_ge(bank_free, freed(2, 1))
            for t in range(TT):
                squares(lat[:, t, 0:QR], tmp[:, 0, 0:QR], ssq[:, t:t + 1], lat_squared)
                act.wait_ge(lat_squared, 2 * t + 1)
                squares(lat[:, t, QR:QR + KVR], tmp[:, 0, 0:KVR], ssq[:, 4 + t:5 + t], lat_squared)
                act.wait_ge(lat_squared, 2 * t + 2)
            for m in range(2):
                gate_bank(3, m, m)
            hi(5)
            for m in range(2):
                gate_bank(4, m, 2 + m)
            for i in range(5):
                row = ROW0["mla_q_norm_g"] + i
                act.wait_ge(lat_turned, i + 1)
                nc.scalar.activation(lt_hi[:, i, :], side_bank(i), ACT.Copy, scale=col[:, row:row + 1]
                                     ).then_inc(lat_hi, 1)
            hi(6)
            for m in range(2):
                gate_bank(5, m, 4 + m)
            hi(7)
            for m in range(2):
                gate_bank(6, m, 6 + m)
            def spread_q(h):
                if h % 4 == 0:
                    act.wait_ge(qp_roped, h // 4 + 1)
                nc.scalar.activation(qm[MN:MQ, h, :], prob[32 * (h % 4):32 * (h % 4) + 32, 2 + h // 4, :],
                                     ACT.Copy).then_inc(q_spread, 1)

            for u in range(U0["qn"] + 1, U0["gate_b"] + 1):
                hi(u)
                v = u - 1
                if v < U0["qp"] or U0["kn"] <= v < U0["mv"]:
                    dst, i, scale = (qm, v - U0["qn"], MQ ** -0.5) if v < U0["qp"] else (km, v - U0["kn"], 1.0)
                    for m in range(2):
                        nc.scalar.activation(dst[0:MN, 4 * i + 2 * m + 1, :], bank(v, m)[MN:P, :],
                                             ACT.Copy, scale=scale).then_inc(nope_kept, 1)
                if v == U0["kn"] + 1 or v == U0["mv"]:
                    for h in range(2 * (v - U0["kn"]) - 2, 2 * (v - U0["kn"])):
                        spread_q(h)

            NP = 4 * MH
            for p in range(MLA_STEPS + 1):
                if p > LAG and (p - LAG - 1) % 4 == 3:
                    h = (p - LAG - 1) // 4
                    rr = slice((h % 2) * MV, (h % 2) * MV + MV)
                    act.wait_ge(pv_done, p - LAG)
                    nc.scalar.activation(om_hi[rr, h // 2, :], ps_o[rr, :], ACT.Copy).then_inc(o_hi_made, 1)
                if LAG <= p < NP + LAG:
                    q = p - LAG
                    n = P * (q % 4 + 1)
                    act.wait_ge(t_full, q + 1)
                    if q >= 2:
                        act.wait_ge(pv_done, q - 1)
                    nc.scalar.activation(pt[:, q % 2, 0:n], ps_t[:, 0:n], ACT.Copy).then_inc(pt_made, 1)
                if p < NP:
                    n = P * (p % 4 + 1)
                    act.wait_ge(max_made, p + 1)
                    if p in (2, 3):
                        act.wait_ge(q_spread, 4 * (p - 1))
                    if p >= 4:
                        act.wait_ge(t_full, p - 3)
                    nc.scalar.activation(prob[:, p % 4, 0:n], ps_s[:, p % 2, 0:n], ACT.Exp,
                                         bias=nmax[:, p % 4:p % 4 + 1],
                                         accum_out=rsum[:, p % 4:p % 4 + 1]).then_inc(exp_made, 1)
                if p < 2:
                    spread_q(4 + 2 * p)
                    spread_q(5 + 2 * p)
                for i, m in MLA_STREAM.banks.get(p, ()):
                    gate_bank(U0["gate_b"] + i, m, 8 + 2 * i + m)
                for h in range(2):
                    if MLA_STREAM.started(p - 1 - h) is not None:
                        hi_half(MLA_STREAM.started(p - 1 - h) + 1, h)
            for u in range(U0["dq"] + 1, U0["mrg_m"] + 1):
                hi(u)

            NP = 4 * DH
            for p in range(DIFF_STEPS + 1):
                hd, r = (p - LAG - 4) // 4, (p - LAG - 4) % 4
                if 0 <= hd < DH and r == 0:
                    act.wait_ge(diff_pv_done, 4 * hd + 4)
                    act.wait_ge(diff_rinv_made, hd + 1)
                    if hd:
                        act.wait_ge(o_turned, hd)
                    for t in range(TT):
                        c = 4 * (hd % 2) + t
                        nc.scalar.activation(o_sb[:, t * P:(t + 1) * P], ps_o[:, t * P:(t + 1) * P], ACT.Copy,
                                             scale=diff_rinv[:, c:c + 1]).then_inc(o_copied, 1)
                if 0 <= hd < DH and r == 3:
                    act.wait_ge(o_turned, hd + 1)
                    nc.scalar.activation(od_hi[:, hd, :], ps_t[:, :], ACT.Copy,
                                         scale=col[:, ROW0["diff_subln_g"]:ROW0["diff_subln_g"] + 1]
                                         ).then_inc(od_hi_made, 1)
                if LAG <= p < NP + LAG:
                    q = p - LAG
                    n = P * (q % 4 + 1)
                    act.wait_ge(diff_t_full, q + 1)
                    if q >= 2:
                        act.wait_ge(diff_pv_done, q - 1)
                    nc.scalar.activation(pt[:, q % 2, 0:n], ps_t[:, 0:n], ACT.Copy).then_inc(diff_pt_made, 1)
                if p < NP:
                    n = P * (p % 4 + 1)
                    for e, out in enumerate((prob[:, p % 4, 0:n], p2[:, p % 2, 0:n])):
                        act.wait_ge(diff_max_made, 2 * p + e + 1)
                        if e == 0 and p >= 4:
                            act.wait_ge(diff_t_full, p - 3)
                        if e == 1 and p >= 2:
                            act.wait_ge(diff_p_ready, p - 1)
                        b = 2 * (p % 4) + e
                        c = 8 * e + p % 8
                        nc.scalar.activation(out, ps_s[:, e, 0:n], ACT.Exp, bias=nmax[:, b:b + 1],
                                             accum_out=diff_sum[:, c:c + 1]).then_inc(diff_exp_made, 1)
                if 0 <= hd < DH and r == 0:
                    for t in range(TT):
                        act.wait_ge(o_copied, 4 * hd + t + 1)
                        squares(o_sb[:, t * P:(t + 1) * P], o_sq[:, t * P:(t + 1) * P], diff_ssq[:, t:t + 1], o_squared)
                if DIFF_STREAM.started(p - 1) is not None:
                    hi(DIFF_STREAM.started(p - 1) + 1)
            for c in range(-1, 8):
                if c % 2 and c < 7:
                    hi(U0["mrg_d"] + (c + 1) // 2 + 1)
                if c >= 0:
                    act.wait_ge(merged, c + 1)
                    nc.scalar.activation(act_hi[:, c, :], gates[:, c, :], ACT.Copy, scale=0.5).then_inc(merged_hi, 1)
            def hi_at(u, s, count, k, w):
                act.wait_ge(w_landed[s], count)
                act.wait_ge(w_used, u - 1)
                nc.scalar.activation(w_hi[:, s, 0:k * w], stage[:, s, 0:k * w], ACT.Copy).then_inc(w_hi_made, 1)

            uf = U0["ffn"]
            lc = {uf % 2: landed_count(uf - 2) + 16, (uf + 1) % 2: landed_count(uf - 1) + 16}

            for i in range(4):
                u = U0["out"] + i
                if i < 3:
                    hi(u + 1)
                else:
                    hi_at(uf, uf % 2, lc[uf % 2], 8, 256)
                for m in range(2):
                    act.wait_ge(bank_free, freed(u, m))
                    part_squares(256 * i, m, i, 0, res, tmp[:, m, :], norm_squared)
                    act.wait_ge(norm_squared, TT + 4 * i + 2 * m + 2)
                    if i == 3:
                        half_scale(m, 2 + m, n_sc, res, norm_scaled_act)
            norm_hi_chunks("norm_ffn_g", KD)
            with act.Fori(0, KF // 2) as j:
                s0, s1 = uf % 2, (uf + 1) % 2
                hi_at(j * 2 + (uf + 1), s1, j * 16 + lc[s1], 8, 256)
                for m in range(2):
                    if m == 0:
                        act.wait_ge(first_bank_full, j * 2 + (uf + 1))
                    else:
                        act.wait_ge(w_used, j * 2 + (uf + 1))
                    act.wait_ge(w_lo_made, j * 2 + (uf + 2))
                    nc.scalar.activation(sl[:, m, :], ps_mm[:, 2 * (uf % 2) + m, :], ACT.Silu
                                         ).then_inc(bank_free_act, 1)
                with_next = j * 2 + (uf + 2)
                hi_at(with_next, s0, j * 16 + (lc[s0] + 16), 8, 256)
                for m in range(2):
                    act.wait_ge(bank_free, j * 2 + freed(uf + 1, m))
                    nc.scalar.activation(h_hi[:, bass.ds(j * 2 + m, 1), :], sl[:, m:m + 1, :], ACT.Copy
                                         ).then_inc(h_hi_made, 1)
            ud = U0["down"]
            ld = {ud % 2: landed_count(ud), (ud + 1) % 2: landed_count(ud + 1)}
            gd = group_of(ud)
            with act.Fori(0, DOWN_GROUPS // 2) as j:
                for i in range(1, 7):
                    s = (ud + i) % 2
                    kk = DOWN_K[i % 3] if i < 6 else 8
                    cnt = ld[s] + 16 * ((i - (s != ud % 2)) // 2)
                    hi_at(j * 6 + (ud + i), s, j * 48 + cnt, kk, 256)
                    if i % 3 == 0:
                        gg = i // 3 - 1
                        for m in range(2):
                            for kind, src in enumerate((res, act_y)):
                                if kind == 0:
                                    act.wait_ge(bank_free, j * 4 + dve_freed(gd + gg, m))
                                else:
                                    act.wait_ge(x_gained, j * 4 + (2 * gg + m + 1))
                                for t in (2 * m, 2 * m + 1):
                                    nc.scalar.activation(
                                        tmp[:, kind, 256 * (t % 2):256 * (t % 2) + 256],
                                        src[:, t, bass.ds(j * 512 + 256 * gg, 256)], ACT.Square,
                                        accum_out=part[:, bass.ds(j * 8 + (16 * kind + 4 * gg + t), 1)]
                                        ).then_inc(down_squared, 1)
                            act.wait_ge(down_squared, j * 16 + (8 * gg + 4 * m + 4))
            act.wait_ge(rstd_made, 4)
            scale_tiles(n_sc, act_y, 4)
            norm_hi_chunks("norm_g_2", 2 * KD)
            uq2 = U0["q2"]
            hi(uq2 + 1)
            for i in range(4):
                for m in range(2):
                    if m:
                        hi(uq2 + i + 2)
                    n = 2 * i + m
                    act.wait_ge(q2_roped, n + 1)
                    for e in range(2):
                        rr = slice(e * AD, e * AD + AD)
                        nc.scalar.activation(q_split[rr, 2 * n + e, :], prob2[rr, m, :], ACT.Copy
                                             ).then_inc(q2_hi_made, 1)

            def z_bank(u, m):
                if u > U0["zs"]:
                    act.wait_ge(bank_free, freed(u - 1, m))
                nc.scalar.activation(tmp[:, m, :], bank(u, m), ACT.Tanh, scale=0.5
                                     ).then_inc(z_tanh, 1)

            act.wait_ge(k_roped, 1)
            for g in range(AG):
                for e in range(2):
                    nc.scalar.activation(k_hi[e * AD:e * AD + AD, g, :], kv[g * AD:g * AD + AD, 1, :], ACT.Copy
                                         ).then_inc(k_hi_made, 1)
            for i in range(4):
                u = U0["za"] + i
                hi(u + 1)
                for m in range(2):
                    nc.scalar.activation(gz[:, 2 * i + m, :], bank(u, m), ACT.Silu).then_inc(bank_free_act, 1)
            NP = WIN_PIECES
            for p in range(WIN_STEPS + 1):
                if LAG <= p < NP + LAG:
                    q = p - LAG
                    act.wait_ge(win_t_full, q + 1)
                    if q >= 2:
                        act.wait_ge(win_pv_done, q - 1)
                    if q // 8:
                        nc.scalar.activation(pt2[:, q % 2, :], ps_t[:, :], ACT.Copy).then_inc(win_pt_made, 1)
                    else:
                        nc.scalar.activation(pt2[:, q % 2, :].rearrange("p (e n) -> p e n", e=2)[:, :, P:2 * P],
                                             ps_t[:, :].rearrange("p (e n) -> p e n", e=2)[:, :, P:2 * P], ACT.Copy
                                             ).then_inc(win_pt_made, 1)
                if p < NP:
                    b = p // 8
                    act.wait_ge(win_max_made, p + 1)
                    if p >= 4:
                        act.wait_ge(win_t_full, p - 3)
                    for e in range(2):
                        j0 = 0 if b else P
                        j = 16 * (b % 2) + window_head(p % 8, e)
                        nc.scalar.activation(prob2[:, p % 4, e * 256 + j0:e * 256 + 256],
                                             ps_s[:, p % 2, e * 256 + j0:e * 256 + 256], ACT.Exp,
                                             bias=nm2[:, j:j + 1], accum_out=rs2[:, j:j + 1]
                                             ).then_inc(win_exp_made, 1)
                if p >= 1 and (p - 1) % 4 == 3 and p - 1 < NP:
                    act.wait_ge(sink_diff, (p - 1) // 4 + 1)
                    nc.scalar.activation(esink, dsink, ACT.Exp).then_inc(sink_exp, 1)
                for i, m in WIN_STREAM.banks.get(p, ()):
                    z_bank(U0["zs"] + i, m)
                for h in range(2):
                    if WIN_STREAM.started(p - 1 - h) is not None:
                        hi_half(WIN_STREAM.started(p - 1 - h) + 1, h)
            for i in range(4):
                u = U0["u2"] + i
                hi(u + 1)
                for m in range(2):
                    c = 2 * i + m
                    act.wait_ge(bank_free, freed(u - 1, m))
                    nc.scalar.activation(tmp[:, m, :], bank(u, m), ACT.Gelu
                                         ).then_inc(gelu_made, 1)
                act.wait_ge(a_gated, 8)
                for c in (2 * i, 2 * i + 1):
                    nc.scalar.activation(at_hi[:, c, :], gz[:, c, :], ACT.Copy).then_inc(at_hi_made, 1)
            for i in range(4):
                u = U0["vs"] + i
                hi(u + 1)
                for m in range(2):
                    nc.scalar.activation(vs[:, 2 * m:2 * m + 2, 256 * i:256 * i + 256],
                                         bank(u, m).rearrange("p (t n) -> p t n", t=2),
                                         ACT.Gelu).then_inc(gelu_made, 1)
            hi(U0["ga"] + 1)
            act.wait_ge(vs_summed, 1)
            for t in range(TT):
                nc.scalar.activation(tmp[:, :, :].rearrange("p a n -> p (a n)"), vs[:, t, :], ACT.Square,
                                     bias=nmean[:, t:t + 1],
                                     accum_out=ssq[:, t:t + 1]).then_inc(vs_squared, 1)
                act.wait_ge(vs_squared, t + 1)

            def sig_bank(u, m, dst, c, row):
                nc.scalar.activation(dst[:, c, :], bank(u, m), ACT.Sigmoid,
                                     bias=col[:, row:row + 1]).then_inc(bank_free_act, 1)

            act.wait_ge(at_lo_made, KD)
            for i in range(4):
                u = U0["ga"] + i
                if i:
                    hi(u + 1)
                for m in range(2):
                    sig_bank(u, m, gz, 2 * i + m, ROW0["b_merge_2"] + 2 * i + m)
            for u in range(U0["att"] + 1, U0["gs"] + 1):
                hi(u)
            for g in range(8):
                u, m = U0["gs"] + g // 2, g % 2
                if m == 0:
                    hi(u + 1)
                act.wait_ge(mix_gated, g + 1)
                nc.scalar.activation(at_hi[:, g, :], tmp[:, g % 2, :], ACT.Copy).then_inc(sg_hi_made, 1)
                sig_bank(u, m, gu, g, ROW0["b_merge_2"] + 8 + g)
            for i in range(4):
                u = U0["sgo"] + i
                hi(u + 1)
                for m in range(2):
                    c = 2 * i + m
                    act.wait_ge(y_sum, c + 1)
                    nc.scalar.activation(act_hi[:, c, :], gu[:, c, :], ACT.Copy).then_inc(y_hi_made, 1)
            for i in range(4):
                u = U0["wo"] + i
                if u + 1 < NU:
                    hi(u + 1)
                for m in range(2):
                    act.wait_ge(bank_free, freed(u, m))
                    part_squares(256 * i, m, i, 0, res, tmp[:, m, :], fin_squared)
                    act.wait_ge(fin_squared, 4 * i + 2 * m + 2)
                    if i == 3:
                        act.wait_ge(x_gained, 8 + 2 * i + m + 1)
                        half_scale(m, 5 + m, res, vs, fin_made_act)

        @block.vector
        def _(dve):
            V = nc.vector
            chain = [0]

            def link(ins):
                chain[0] += 1
                ins.then_inc(dve_chain, 1)
                return chain[0]

            def after(n):
                dve.wait_ge(dve_chain, n)

            def lo(u):
                s = u % 2
                src, k, w = unit_source(u)
                dve.wait_ge(w_hi_made, u + 1)
                V.tensor_tensor(w_lo[:, s, 0:k * w], stage[:, s, 0:k * w], w_hi[:, s, 0:k * w].bitcast(F32),
                                ALU.subtract).then_inc(w_lo_made, 1)

            def lo_half(u, h):
                s = u % 2
                src, k, w = unit_source(u)
                dve.wait_ge(w_hi_made, u + 1)
                n = k * w // 2
                ins = V.tensor_tensor(w_lo[:, s, h * n:(h + 1) * n], stage[:, s, h * n:(h + 1) * n],
                                      w_hi[:, s, h * n:(h + 1) * n].bitcast(F32), ALU.subtract)
                if h:
                    ins.then_inc(w_lo_made, 1)

            def bank(u, m):
                g = group_of(u)
                if m == 0:
                    dve.wait_ge(first_bank_full, g + 1)
                else:
                    dve.wait_ge(w_used, u + 1)
                return ps_mm[:, 2 * (g % 2) + m, :]

            def rsqrt_of(n, made=None, c0=0):
                v, y, t = var[:, c0:c0 + n], rstd[:, c0:c0 + n], newton[:, c0:c0 + n]
                after(link(V.tensor_scalar(y.bitcast(I32), v.bitcast(I32), -0.5, float(0x5f3759df),
                                           ALU.mult, ALU.add)))
                for step in range(3):
                    after(link(V.tensor_tensor(t, y, y, ALU.mult)))
                    after(link(V.scalar_tensor_tensor(out=t, in0=t, scalar=-0.5, in1=v, op0=ALU.mult, op1=ALU.mult)))
                    ins = V.scalar_tensor_tensor(out=y, in0=t, scalar=1.5, in1=y, op0=ALU.add, op1=ALU.mult)
                    if step == 2 and made is not None:
                        ins.then_inc(rstd_made, 1)
                        dve.wait_ge(rstd_made, made)
                    else:
                        after(link(ins))

            def rsqrt(n, scale, made=None, c0=0):
                after(link(V.tensor_scalar(var[:, c0:c0 + n], ssq[:, c0:c0 + n], scale, EPS, ALU.mult, ALU.add)))
                rsqrt_of(n, made, c0)

            def add_parts(kinds=1):
                after(link(V.tensor_reduce(ssq[:, 0:4 * kinds],
                                           part[:, 0:16 * kinds].rearrange("p (c i t) -> p c t i", c=kinds, i=4),
                                           AX.X, ALU.add)))

            def half_norm(m, signal, due, made, out, src, scaled):
                dve.wait_ge(signal, due)
                after(link(V.tensor_reduce(ssq[:, 2 * m:2 * m + 2],
                                           part[:, 0:16].rearrange("p (i t) -> p t i", i=4)[:, 2 * m:2 * m + 2, :],
                                           AX.X, ALU.add)))
                rsqrt(2, 1.0 / D, made, 2 * m)
                for t, n in (((0, 0),), ((2, 0), (3, D // 2)))[m]:
                    V.tensor_scalar(out[:, t, n:D], src[:, t, n:D], rstd[:, t:t + 1], None, ALU.mult
                                    ).then_inc(scaled, 1)

            def norm_lo_chunk(row, base, k):
                dve.wait_ge(norm_hi, base + k + 1)
                V.scalar_tensor_tensor(out=act_lo[:, k, :], in0=side_bank(k),
                                       scalar=col[:, ROW0[row] + k:ROW0[row] + k + 1],
                                       in1=act_hi[:, k, :].bitcast(F32), op0=ALU.mult, op1=ALU.subtract
                                       ).then_inc(norm_lo, 1)

            def norm_lo_chunks(row, base):
                for k in range(KD):
                    norm_lo_chunk(row, base, k)

            def token_rows(ap, w):
                return ap[:, 0:2 * w].rearrange("p (t n) -> p t n", t=2)

            dve.wait_ge(ident_made, 1)
            link(V.tensor_copy(ident_r[:, :], ident[:, :]))
            dve.wait_ge(consts_made, 5)
            link(V.tensor_copy(causal_r[:, :], tmp[:, 0, 0:P]))
            after(link(V.tensor_copy(window_r[:, :, :], tmp[:, 1, :].rearrange("p (e n) -> p e n", e=2))))
            dve.wait_ge(cols_turned, 1)
            after(link(V.tensor_copy(col[:, :], ps_t[:, 0:NROWS])))
            after(link(V.tensor_scalar(col[:, ROW0["diff_subln_g"]:ROW0["diff_subln_g"] + 1],
                                       col[:, ROW0["diff_subln_g"]:ROW0["diff_subln_g"] + 1], 1.0 - LAMBDA_INIT, None,
                                       ALU.mult)))
            V.tensor_scalar(hcol[:, :], col[:, :], 0.5, None, ALU.mult).then_inc(cols_made, 1)
            def scale_tiles(out, src, c0=0, signal=norm_scaled):
                for t, n in ((0, 0), (2, 0), (3, D // 2)):
                    V.tensor_scalar(out[:, t, n:D], src[:, t, n:D], rstd[:, c0 + t:c0 + t + 1], None, ALU.mult
                                    ).then_inc(signal, 1)

            dve.wait_ge(norm_squared, TT)
            rsqrt(TT, 1.0 / D, made=1)
            scale_tiles(x_sc, x_in)
            for k in range(KD):
                dve.wait_ge(norm_hi, k + 1)
                ins = V.tensor_tensor(w_lo[:, 0, 256 * k:256 * k + 256], stage[:, 0, 256 * k:256 * k + 256],
                                      w_hi[:, 0, 256 * k:256 * k + 256].bitcast(F32), ALU.subtract)
                if k == KD - 1:
                    ins.then_inc(w_lo_made, 1)
                norm_lo_chunk("norm_mix_g", 0, k)
            dve.wait_ge(lam_landed, 64)
            lt = lamv[:, :, :].rearrange("p (a b) n -> p a b n", b=2)
            after(link(V.tensor_tensor(lt[:, :, 0, :], lt[:, :, 0, :], lt[:, :, 1, :], ALU.mult)))
            V.tensor_reduce(lsum, lt[:, :, 0, :], AX.X, ALU.add).then_inc(lam_summed, 1)
            lo(1)

            def angles(n, table_row, pos):
                two_pi = 2.0 * math.pi
                c1 = 6.28125
                c2 = math.floor((two_pi - c1) * 2 ** 17) / 2 ** 17
                c3 = math.floor((two_pi - c1 - c2) * 2 ** 26) / 2 ** 26
                c4 = two_pi - c1 - c2 - c3
                magic = 1.5 * 2 ** 23
                if n >= 1:
                    dve.wait_ge(sincos_made, n)
                ang, kk, r, ar = rt[:, 0, :], rt[:, 1, :], rt[:, 2, :], rt[:, 3, :]
                after(link(V.tensor_scalar(ang, pos, freq[:, table_row:table_row + 1], None, ALU.mult)))
                after(link(V.tensor_scalar(kk, ang, 1.0 / two_pi, magic, ALU.mult, ALU.add)))
                after(link(V.tensor_scalar(kk, kk, magic, None, ALU.subtract)))
                prev = ang
                for c in (c1, c2, c3, c4):
                    after(link(V.scalar_tensor_tensor(out=r, in0=kk, scalar=-c, in1=prev, op0=ALU.mult, op1=ALU.add)))
                    prev = r
                after(link(V.tensor_scalar(r, r, 3.1415925, -3.1415925, ALU.min, ALU.max)))
                V.scalar_tensor_tensor(out=ar, in0=r, scalar=-1.0, in1=r, op0=ALU.mult, op1=ALU.max
                                       ).then_inc(angle_ready, 1)

            dve.wait_ge(pos_landed, 16)
            dve.wait_ge(freq_landed, 16)
            after(link(V.tensor_copy(pos_f[:, 0, :], pos_i[:, :])))
            angles(0, 0, pos_f[:, 0, :])

            def keep_latents(u):
                w = 256 if u < 2 else LAT - 512
                for m in range(2):
                    V.tensor_copy(lat[:, 2 * m:2 * m + 2, 256 * u:256 * u + w], token_rows(bank(u, m), w)
                                  ).then_inc(bank_free, 1)

            keep_latents(0)
            lo(2)
            dve.wait_ge(lam_exp, 1)
            after(link(V.tensor_tensor(neglam, lexp[:, 1:2], lexp[:, 0:1], ALU.subtract)))
            link(V.tensor_scalar(neglam, neglam, LAMBDA_INIT, None, ALU.subtract))
            angles(1, 1, pos_f[:, 0, :])
            keep_latents(1)
            lo(3)
            dve.wait_ge(iota_made, 1)
            after(link(V.tensor_copy(pos_f[:, 1, :], pos_i2[:, :])))
            angles(2, 1, pos_f[:, 1, :])
            keep_latents(2)
            lo(4)
            dve.wait_ge(lat_squared, 8)
            after(link(V.tensor_scalar(ssq[:, 0:4], ssq[:, 0:4], KVR / QR, None, ALU.mult)))
            rsqrt(8, 1.0 / KVR)
            for t in range(TT):
                V.tensor_scalar(lat[:, t, 0:QR], lat[:, t, 0:QR], rstd[:, t:t + 1], None, ALU.mult
                                ).then_inc(lat_scaled, 1)
                V.tensor_scalar(lat[:, t, QR:QR + KVR], lat[:, t, QR:QR + KVR], rstd[:, 4 + t:5 + t], None, ALU.mult
                                ).then_inc(lat_scaled, 1)
            lo(5)
            for i in range(5):
                row = ROW0["mla_q_norm_g"] + i
                dve.wait_ge(lat_hi, i + 1)
                V.scalar_tensor_tensor(out=lt_lo[:, i, :], in0=side_bank(i), scalar=col[:, row:row + 1],
                                       in1=lt_hi[:, i, :].bitcast(F32), op0=ALU.mult, op1=ALU.subtract
                                       ).then_inc(lat_lo, 1)
            swap16 = [i ^ 16 for i in range(32)]
            swap8 = [i ^ 8 if i < 16 else i for i in range(32)]

            lo(6)
            dve.wait_ge(lat_turned, 6)
            rr = slice(MN, MQ)
            src = side_bank(5)[MN:MQ, :]
            t = tmp[rr, 1, :]
            after(link(V.stream_shuffle(t, src, swap16)))
            after(link(V.tensor_tensor(t, t, rope_m[rr, 1, :], ALU.mult)))
            after(link(V.tensor_tensor(tmp[rr, 0, :], src, rope_m[rr, 0, :], ALU.mult)))
            after(link(V.tensor_tensor(tmp[rr, 0, :], tmp[rr, 0, :], t, ALU.add)))
            for h in range(MH):
                V.tensor_copy(km[MN:MQ, h, :], tmp[rr, 0, :]).then_inc(kpe_spread, 1)
            lo(7)
            dve.wait_ge(kpe_spread, MH)

            def rope_bank(u, m, dst, tab, swap, scale=1.0, signal=None, count=None):
                src = bank(u, m)
                t = tmp[:, m, :]
                c0 = link(V.stream_shuffle(t, src, swap))
                V.scalar_tensor_tensor(out=dst, in0=src, scalar=scale, in1=tab[:, 0, :], op0=ALU.mult, op1=ALU.mult
                                       ).then_inc(bank_free, 1)
                after(c0)
                after(link(V.scalar_tensor_tensor(out=t, in0=t, scalar=scale, in1=tab[:, 1, :], op0=ALU.mult,
                                                  op1=ALU.mult)))
                dve.wait_ge(bank_free, freed(u, m))
                if signal is not None:
                    V.tensor_tensor(dst, dst, t, ALU.add).then_inc(signal, 1)
                    dve.wait_ge(signal, count)
                else:
                    after(link(V.tensor_tensor(dst, dst, t, ALU.add)))

            for u in range(U0["qn"], U0["mv"]):
                if u != U0["kn"]:
                    lo(u + 1)
                for m in range(2):
                    if u == U0["qp"]:
                        rope_bank(u, m, prob[:, 2 + m, :], rope_m, swap16, MQ ** -0.5, qp_roped, m + 1)
                        if m == 0:
                            lo(u + 2)
                        continue
                    src = bank(u, m)
                    if u < U0["qp"]:
                        i = u - U0["qn"]
                        dve.wait_ge(nope_kept, 2 * i + m + 1)
                        V.tensor_scalar(qm[0:MN, 4 * i + 2 * m, :], src[0:MN, :], MQ ** -0.5, None, ALU.mult
                                        ).then_inc(bank_free, 1)
                    else:
                        i = u - U0["kn"]
                        dve.wait_ge(nope_kept, 4 + 2 * i + m + 1)
                        V.tensor_copy(km[0:MN, 4 * i + 2 * m, :], src[0:MN, :]).then_inc(bank_free, 1)
            for i in range(2):
                u = U0["mv"] + i
                if i == 0:
                    lo(u + 1)
                for m in range(2):
                    V.tensor_copy(vm[:, 2 * m:2 * m + 2, 256 * i:256 * i + 256], token_rows(bank(u, m), 256)
                                  ).then_inc(bank_free, 1)

            NP = 4 * MH
            for p in range(MLA_STEPS + 3):
                if p < NP:
                    n = P * (p % 4 + 1)
                    b = p % 4
                    dve.wait_ge(s_full, p + 1)
                    if p >= 4:
                        dve.wait_ge(exp_made, p - 3)
                    V.tensor_reduce(nmax[:, b:b + 1], ps_s[:, p % 2, 0:n], AX.X, ALU.max, negate=True
                                    ).then_inc(max_made, 1)
                if p > LAG and (p - LAG - 1) % 4 == 3 and p - LAG - 1 < NP:
                    h = (p - LAG - 1) // 4
                    rr = slice((h % 2) * MV, (h % 2) * MV + MV)
                    dve.wait_ge(o_hi_made, h + 1)
                    V.tensor_tensor(om_lo[rr, h // 2, :], ps_o[rr, :], om_hi[rr, h // 2, :].bitcast(F32), ALU.subtract
                                    ).then_inc(o_free, 1)
                if 1 <= p <= NP:
                    q = p - 1
                    n = P * (q % 4 + 1)
                    b = q % 4
                    dve.wait_ge(exp_made, q + 1)
                    after(link(V.reciprocal(rinv[:, b:b + 1], rsum[:, b:b + 1])))
                    V.tensor_scalar(prob[:, b, 0:n], prob[:, b, 0:n], rinv[:, b:b + 1], None, ALU.mult
                                    ).then_inc(p_ready, 1)
                if p < 2:
                    lo_half(U0["gate_b"], p)
                for h in range(2):
                    if MLA_STREAM.started(p - 3 - h) is not None:
                        lo_half(MLA_STREAM.started(p - 3 - h) + 1, h)

            for name, dst in (("dq", dq), ("dk", dk)):
                for i in range(2):
                    u = U0[name] + i
                    lo(u + 1)
                    for m in range(2):
                        rope_bank(u, m, dst[:, 2 * i + m, :], rope_d, swap8, DD ** -0.5 if name == "dq" else 1.0)
            for i in range(2):
                u = U0["dv"] + i
                lo(u + 1)
                for m in range(2):
                    V.tensor_copy(dv[:, 2 * m:2 * m + 2, 256 * i:256 * i + 256], token_rows(bank(u, m), 256)
                                  ).then_inc(bank_free, 1)

            def gated(u, m, c):
                V.scalar_tensor_tensor(out=gates[:, c, :], in0=gates[:, c, :], scalar=1.0, in1=bank(u, m),
                                       op0=ALU.add, op1=ALU.mult).then_inc(bank_free, 1)

            NP = 4 * DH
            for p in range(DIFF_STEPS + 1):
                hd, r = (p - LAG - 4) // 4, (p - LAG - 4) % 4
                if 0 <= hd < DH and r == 3:
                    dve.wait_ge(od_hi_made, hd + 1)
                    V.scalar_tensor_tensor(out=od_lo[:, hd, :], in0=ps_t[:, :],
                                           scalar=col[:, ROW0["diff_subln_g"]:ROW0["diff_subln_g"] + 1],
                                           in1=od_hi[:, hd, :].bitcast(F32), op0=ALU.mult, op1=ALU.subtract
                                           ).then_inc(od_made, 1)
                if p < NP:
                    n = P * (p % 4 + 1)
                    for e in range(2):
                        b = 2 * (p % 4) + e
                        dve.wait_ge(diff_s_full, 2 * p + e + 1)
                        if p >= 4:
                            dve.wait_ge(diff_exp_made, 2 * (p - 4) + e + 1)
                        V.tensor_reduce(nmax[:, b:b + 1], ps_s[:, e, 0:n], AX.X, ALU.max, negate=True
                                        ).then_inc(diff_max_made, 1)
                if 1 <= p <= NP:
                    q = p - 1
                    n = P * (q % 4 + 1)
                    b, c = q % 4, q % 8
                    dve.wait_ge(diff_exp_made, 2 * q + 2)
                    after(link(V.reciprocal(rinv[:, b:b + 1], diff_sum[:, 8 + c:9 + c])))
                    after(link(V.scalar_tensor_tensor(out=mix[:, b:b + 1], in0=rinv[:, b:b + 1], scalar=neglam,
                                                      in1=diff_sum[:, c:c + 1], op0=ALU.mult, op1=ALU.mult)))
                    V.scalar_tensor_tensor(out=prob[:, b, 0:n], in0=p2[:, q % 2, 0:n],
                                           scalar=mix[:, b:b + 1], in1=prob[:, b, 0:n], op0=ALU.mult,
                                           op1=ALU.add).then_inc(diff_p_ready, 1)
                    if b == 3:
                        c = 4 * (q // 4 % 2)
                        V.reciprocal(diff_rinv[:, c:c + 4], diff_sum[:, c:c + 4]).then_inc(diff_rinv_made, 1)
                if 0 <= hd < DH and r == 2:
                    dve.wait_ge(diff_rstd_made, hd + 1)
                    for t in range(TT):
                        V.tensor_scalar(o_sb[:, t * P:t * P + P], o_sb[:, t * P:t * P + P], diff_rstd[:, t:t + 1], None,
                                        ALU.mult).then_inc(o_scaled, 1)
                for i, m in DIFF_STREAM.banks.get(p, ()):
                    gated(U0["mrg_m"] + i, m, 2 * i + m)
                if DIFF_STREAM.started(p - 2) is not None:
                    lo(DIFF_STREAM.started(p - 2) + 1)
            for c in range(-1, 8):
                if c >= 0:
                    u, m = U0["mrg_d"] + c // 2, c % 2
                    gated(u, m, 8 + c)
                    dve.wait_ge(bank_free, freed(u, m))
                    V.tensor_tensor(gates[:, c, :], gates[:, c, :], gates[:, 8 + c, :], ALU.add).then_inc(merged, 1)
                    dve.wait_ge(merged_hi, c + 1)
                    V.scalar_tensor_tensor(out=act_lo[:, c, :], in0=gates[:, c, :], scalar=0.5,
                                           in1=act_hi[:, c, :].bitcast(F32), op0=ALU.mult, op1=ALU.subtract
                                           ).then_inc(merged_lo, 1)
                if c % 2 and c < 7:
                    lo(U0["mrg_d"] + (c + 1) // 2 + 1)

            def add_residual(m, ps, n0):
                r = res[:, 2 * m:2 * m + 2, bass.ds(n0, 256)]
                return V.tensor_tensor(r, token_rows(ps, 256), r, ALU.add)

            def lo_at(u, s, k, w):
                dve.wait_ge(w_hi_made, u + 1)
                V.tensor_tensor(w_lo[:, s, 0:k * w], stage[:, s, 0:k * w], w_hi[:, s, 0:k * w].bitcast(F32),
                                ALU.subtract).then_inc(w_lo_made, 1)

            uf = U0["ffn"]
            dve.wait_ge(res_landed, 16 * TT)
            for i in range(4):
                u = U0["out"] + i
                if u + 1 < U0["ffn"]:
                    lo(u + 1)
                else:
                    lo_at(uf, uf % 2, 8, 256)
                for m in range(2):
                    add_residual(m, bank(u, m), 256 * i).then_inc(bank_free, 1)
                    if i == 3:
                        half_norm(m, norm_squared, TT + 12 + 2 * m + 2, 2 + m, n_sc, res, norm_scaled)
            norm_lo_chunks("norm_ffn_g", KD)

            with dve.Fori(0, KF // 2) as j:
                lo_at(j * 2 + (uf + 1), (uf + 1) % 2, 8, 256)
                lo_at(j * 2 + (uf + 2), uf % 2, 8, 256)
                for m in range(2):
                    if m == 0:
                        dve.wait_ge(first_bank_full, j * 2 + (uf + 2))
                    else:
                        dve.wait_ge(w_used, j * 2 + (uf + 2))
                    dve.wait_ge(bank_free_act, j * 2 + (m + 1))
                    V.tensor_tensor(sl[:, m, :], ps_mm[:, 2 * ((uf + 1) % 2) + m, :], sl[:, m, :], ALU.mult
                                    ).then_inc(bank_free, 1)
                    dve.wait_ge(h_hi_made, j * 2 + (m + 1))
                    V.tensor_tensor(h_lo[:, bass.ds(j * 2 + m, 1), :], sl[:, m:m + 1, :],
                                    h_hi[:, bass.ds(j * 2 + m, 1), :].bitcast(F32), ALU.subtract
                                    ).then_inc(h_lo_made, 1)
            ud = U0["down"]
            gd = group_of(ud)
            dve.wait_ge(gf_landed, 16)
            with dve.Fori(0, DOWN_GROUPS // 2) as j:
                for gg in range(2):
                    for i in range(1, 4):
                        ii = 3 * gg + i
                        kk = DOWN_K[i % 3]
                        lo_at(j * 6 + (ud + ii), (ud + ii) % 2, kk, 256)
                    for m in range(2):
                        if m == 0:
                            dve.wait_ge(first_bank_full, j * 2 + (gd + gg + 1))
                        else:
                            dve.wait_ge(w_used, j * 6 + (ud + 3 * gg + 3))
                        r = res[:, 2 * m:2 * m + 2, bass.ds(j * 512 + gg * 256, 256)]
                        V.tensor_tensor(r, token_rows(ps_mm[:, 2 * ((gd + gg) % 2) + m, :], 256), r, ALU.add
                                        ).then_inc(bank_free, 1)
                        dve.wait_ge(bank_free, j * 4 + (dve_freed(gd + gg, m)))
                        V.tensor_tensor(act_y[:, 2 * m:2 * m + 2, bass.ds(j * 512 + gg * 256, 256)], r,
                                        gf_b[:, bass.ds(j * 512 + gg * 256, 256)].unsqueeze(1).broadcast_to([P, 2, 256]),
                                        ALU.mult).then_inc(x_gained, 1)
            dve.wait_ge(down_squared, 32)
            add_parts(2)
            after(link(V.tensor_scalar(var[:, 0:4], ssq[:, 0:4], 1.0 / D, EPS, ALU.mult, ALU.add)))
            after(link(V.tensor_scalar(var[:, 4:8], var[:, 0:4], EPS, None, ALU.mult)))
            after(link(V.scalar_tensor_tensor(out=var[:, 4:8], in0=ssq[:, 4:8], scalar=1.0 / D, in1=var[:, 4:8],
                                              op0=ALU.mult, op1=ALU.add)))
            rsqrt_of(8, made=4)
            scale_tiles(n_sc, act_y, 4)
            norm_lo_chunks("norm_g_2", 2 * KD)
            def q_rests(n):
                for e in range(2):
                    rr, other = slice(e * AD, e * AD + AD), slice((1 - e) * AD, (1 - e) * AD + AD)
                    dve.wait_ge(q2_hi_made, 2 * n + e + 1)
                    V.tensor_tensor(q_split[other, 2 * n + e, :], prob2[rr, n % 2, :],
                                    q_split[rr, 2 * n + e, :].bitcast(F32), ALU.subtract).then_inc(q2_lo_made, 1)

            dve.wait_ge(norm_turned, 3 * KD)
            for i in range(4):
                u = U0["q2"] + i
                lo(u + 1)
                for m in range(2):
                    n = 2 * i + m
                    if n >= 2:
                        dve.wait_ge(q2_lo_made, 2 * (n - 1))
                    rope_bank(u, m, prob2[:, m, :], rope2, swap8, AD ** -0.5, q2_roped, n + 1)
                    if n:
                        q_rests(n - 1)
            u = U0["kv2"]
            lo(u + 1)
            rope_bank(u, 0, kv[:, 1, :], rope2, swap8, 1.0, k_roped, 1)
            q_rests(7)
            V.tensor_copy(kv[:, 0, :], bank(u, 1)).then_inc(bank_free, 1)

            def z_bank(u, m, c, n):
                dve.wait_ge(z_tanh, n + 1)
                V.scalar_tensor_tensor(out=gu[:, c, :], in0=tmp[:, m, :], scalar=1.0, in1=bank(u, m), op0=ALU.add,
                                       op1=ALU.mult).then_inc(bank_free, 1)

            for i in range(4):
                u = U0["za"] + i
                lo(u + 1)
                if i == 0:
                    dve.wait_ge(v_turned, 1)
                    V.tensor_copy(v2[:, :, :], ps_t[:, :].rearrange("p (t n) -> p t n", t=TT)).then_inc(v2_made, 1)
                    for g in range(AG):
                        dve.wait_ge(k_hi_made, 2 * g + 2)
                        for e in range(2):
                            V.tensor_tensor(k_lo[e * AD:e * AD + AD, g, :], kv[g * AD:g * AD + AD, 1, :],
                                            k_hi[g * AD:g * AD + AD, g, :].bitcast(F32), ALU.subtract
                                            ).then_inc(k_lo_made, 1)
                V.scalar_tensor_tensor(out=res[:, i, :], in0=res[:, i, :], scalar=rstd[:, i:i + 1], in1=gf_b[:, :],
                                       op0=ALU.mult, op1=ALU.mult).then_inc(x3_made, 1)
                if i == 3:
                    dve.wait_ge(x3_made, TT)
                    for hb in range(2):
                        dve.wait_ge(wg_turned, hb + 1)
                        link(V.tensor_copy(wg_t[:, 4 * hb:4 * hb + 4, :],
                                           (ps_t, ps_o)[hb][:, :].rearrange("p (g n) -> p g n", g=4)))
                    after(chain[0])
                    V.memset(wg_t[CHUNK:P, :, 0:CHUNK], 0.0).then_inc(wg_made, 1)
            NP = WIN_PIECES
            dve.wait_ge(sink_landed, 16)
            after(link(V.tensor_scalar(nsinkb, sinkb, -1.0, None, ALU.mult)))
            for p in range(WIN_STEPS + 2):
                if p >= LAG + 2 and (p - LAG - 2) % 4 == 3 and p - LAG - 2 < NP:
                    g8 = (p - LAG - 2) // 4
                    b, c0 = g8 // 2, 4 * (g8 % 2)
                    dve.wait_ge(a_turned, g8 + 1)
                    if g8 == 0:
                        dve.wait_ge(bank_free_act, act_freed(group_of(U0["za"]) + 3, 1))
                    g = gz[:, c0:c0 + 4, b * P:b * P + P]
                    V.tensor_tensor(g, ps_t[:, :].rearrange("p (c n) -> p c n", c=4), g, ALU.mult
                                    ).then_inc(a_gated, 1)
                if p < NP:
                    b, i = p // 8, p % 8
                    h = window_head(i, 0)
                    j = 16 * (b % 2) + h
                    j0 = 0 if b else P
                    dve.wait_ge(win_s_full, p + 1)
                    mx = nmax[:, 2 * (p % 4):2 * (p % 4) + 2]
                    after(link(V.tensor_reduce(mx, ps_s[:, p % 2, :].rearrange("p (e n) -> p e n", e=2)[:, :, j0:256],
                                               AX.X, ALU.max, negate=True)))
                    V.tensor_tensor(nm2[:, j:j + 3:2], mx, nsinkb[:, h:h + 3:2], ALU.min).then_inc(win_max_made, 1)
                if p >= 1 and (p - 1) % 4 == 3 and p - 1 < NP:
                    g8 = (p - 1) // 4
                    jj = 16 * (g8 // 2 % 2) + 8 * (g8 % 2)
                    if g8:
                        dve.wait_ge(sink_exp, g8)
                    V.tensor_tensor(dsink, sinkb[:, 8 * (g8 % 2):8 * (g8 % 2) + 8], nm2[:, jj:jj + 8], ALU.add
                                    ).then_inc(sink_diff, 1)
                if p >= LAG and (p - LAG) % 4 == 3 and p - LAG < NP:
                    g8 = (p - LAG) // 4
                    jj = 16 * (g8 // 2 % 2) + 8 * (g8 % 2)
                    dve.wait_ge(sink_exp, g8 + 1)
                    after(link(V.tensor_tensor(den2, rs2[:, jj:jj + 8], esink, ALU.add)))
                    after(link(V.reciprocal(rden2, den2)))
                if p >= LAG + 1 and (p - LAG - 1) % 4 == 3 and p - LAG - 1 < NP:
                    g8 = (p - LAG - 1) // 4
                    dve.wait_ge(win_pv_done, 4 * g8 + 4)
                    V.tensor_tensor(a_tok[:, g8 % 2, :].rearrange("p (h n) -> p h n", h=8),
                                    ps_o[:, :].rearrange("p (h n) -> p h n", h=8),
                                    rden2.unsqueeze(2).broadcast_to([P, 8, AD]), ALU.mult).then_inc(a_kept, 1)
                for i, m in WIN_STREAM.banks.get(p, ()):
                    z_bank(U0["zs"] + i, m, 2 * i + m, 2 * i + m)
                for h in range(2):
                    if WIN_STREAM.started(p - 3 - h) is not None:
                        lo_half(WIN_STREAM.started(p - 3 - h) + 1, h)
            for i in range(4):
                u = U0["u2"] + i
                lo(u + 1)
                for m in range(2):
                    c = 2 * i + m
                    dve.wait_ge(gelu_made, c + 1)
                    V.scalar_tensor_tensor(out=gu[:, c, :], in0=tmp[:, m, :], scalar=0.5, in1=gu[:, c, :],
                                           op0=ALU.mult, op1=ALU.mult).then_inc(bank_free, 1)
                for c in (2 * i, 2 * i + 1):
                    dve.wait_ge(at_hi_made, c + 1)
                    V.tensor_tensor(at_lo[:, c, :], gz[:, c, :], at_hi[:, c, :].bitcast(F32), ALU.subtract
                                    ).then_inc(at_lo_made, 1)
            for i in range(4):
                u = U0["vs"] + i
                lo(u + 1)
                for m in range(2):
                    dve.wait_ge(gelu_made, 8 + 2 * i + m + 1)
                    V.tensor_reduce(vsum[:, 4 * i + 2 * m:4 * i + 2 * m + 2],
                                    vs[:, 2 * m:2 * m + 2, 256 * i:256 * i + 256], AX.X, ALU.add
                                    ).then_inc(bank_free, 1)
            dve.wait_ge(bank_free, freed(U0["ga"] - 1, 1))
            after(link(V.tensor_reduce(mean, vsum.rearrange("p (i t) -> p t i", i=4), AX.X, ALU.add)))
            after(link(V.tensor_scalar(mean, mean, 1.0 / D, None, ALU.mult)))
            V.tensor_scalar(nmean, mean, -1.0, None, ALU.mult).then_inc(vs_summed, 1)
            lo(U0["ga"] + 1)

            def layer_norm(t):
                c0 = link(V.tensor_scalar(vs[:, t, :], vs[:, t, :], mean[:, t:t + 1], rstd[:, t:t + 1], ALU.subtract,
                                          ALU.mult))
                after(c0)
                after(link(V.tensor_tensor(vs[:, t, :], vs[:, t, :], lng_b[:, :], ALU.mult)))
                V.tensor_tensor(vs[:, t, :], vs[:, t, :], lnb_b[:, :], ALU.add).then_inc(vs_normed, 1)

            dve.wait_ge(vs_squared, TT)
            rsqrt(TT, 1.0 / D)
            dve.wait_ge(ln_landed, 32)
            for i in range(4):
                u = U0["ga"] + i
                if i:
                    lo(u + 1)
                layer_norm(i)
            for i in range(4):
                u = U0["att"] + i
                lo(u + 1)
                for m in range(2):
                    c = 2 * i + m
                    dve.wait_ge(bank_free_act, act_freed(group_of(U0["ga"]) + i, m))
                    V.tensor_tensor(gz[:, c, :], bank(u, m), gz[:, c, :], ALU.mult).then_inc(bank_free, 1)
            dve.wait_ge(sgb_landed, 16)
            for g in range(8):
                if g % 2 == 0:
                    lo(U0["gs"] + g // 2 + 1)
                dve.wait_ge(mix_full, g + 1)
                tb = tmp[:, g % 2, :]
                if g >= 2:
                    dve.wait_ge(sg_lo_made, g - 1)
                after(link(V.tensor_tensor(tb.rearrange("p (b n) -> p b n", b=TT),
                                           side_bank(g).rearrange("p (b n) -> p b n", b=TT),
                                           sgb_b[:, g:g + 1, :].broadcast_to([P, TT, P]), ALU.add)))
                V.tensor_tensor(tb, tb, gu[:, g, :], ALU.mult).then_inc(mix_gated, 1)
                dve.wait_ge(sg_hi_made, g + 1)
                V.tensor_tensor(at_lo[:, g, :], tb, at_hi[:, g, :].bitcast(F32), ALU.subtract).then_inc(sg_lo_made, 1)
            for i in range(4):
                u = U0["sgo"] + i
                lo(u + 1)
                for m in range(2):
                    c = 2 * i + m
                    dve.wait_ge(bank_free_act, act_freed(group_of(U0["gs"]) + i, m))
                    V.tensor_tensor(gu[:, c, :], bank(u, m), gu[:, c, :], ALU.mult).then_inc(bank_free, 1)
                    dve.wait_ge(bank_free, freed(u, m))
                    V.tensor_tensor(gu[:, c, :], gu[:, c, :], gz[:, c, :], ALU.add).then_inc(y_sum, 1)
                    dve.wait_ge(y_hi_made, c + 1)
                    V.tensor_tensor(act_lo[:, c, :], gu[:, c, :], act_hi[:, c, :].bitcast(F32), ALU.subtract
                                    ).then_inc(y_lo_made, 1)
            for i in range(4):
                u = U0["wo"] + i
                if u + 1 < NU:
                    lo(u + 1)
                if i == 0:
                    dve.wait_ge(fg_landed, 16)
                for m in range(2):
                    add_residual(m, bank(u, m), 256 * i).then_inc(bank_free, 1)
                    dve.wait_ge(bank_free, freed(u, m))
                    V.tensor_tensor(vs[:, 2 * m:2 * m + 2, 256 * i:256 * i + 256],
                                    res[:, 2 * m:2 * m + 2, 256 * i:256 * i + 256],
                                    lng_b[:, 256 * i:256 * i + 256].unsqueeze(1).broadcast_to([P, 2, 256]), ALU.mult
                                    ).then_inc(x_gained, 1)
                    if i == 3:
                        dve.wait_ge(x_gained, 8 + 2 * i + m + 1)
                        half_norm(m, fin_squared, 12 + 2 * m + 2, 5 + m, res, vs, fin_made)

        @block.tensor
        def _(pe):
            T = nc.tensor
            PASSES = ((0, 0), (0, 1), (1, 0))

            def bank_due(g, m):
                if g >= 2:
                    if g - 2 in ACT_FREED:
                        pe.wait_ge(bank_free_act, act_freed(g - 2, m))
                    else:
                        pe.wait_ge(bank_free, dve_freed(g - 2, m))

            def unit(u, s, bank_slot, due, kind, k, w, acts, a=0, b=None, kacts=None, start=True, stop=True,
                     chunk_waits=None, w_by_chunk=False):
                per = 3 * k if kind == "F" else 6 * k
                b = 2 * per if b is None else b
                if a == 0 and not w_by_chunk:
                    pe.wait_ge(w_lo_made, u + 1)
                order = range(a, b)
                if chunk_waits is not None:
                    order = sorted(order, key=lambda n: (n % (3 * k)) // 3)
                    due(0)
                    due(1)
                full_at = [max(i for i, n in enumerate(order) if n // per == m) if any(n // per == m for n in order)
                           else None for m in range(2)]
                seen = 0
                for i, n in enumerate(order):
                    m, r = n // per, n % per
                    kk = (n % (3 * k)) // 3
                    if chunk_waits is not None and kk == seen:
                        pe.wait_ge(chunk_waits[0], chunk_waits[1] + kk + 1)
                        seen += 1
                    if r == 0 and start and chunk_waits is None:
                        due(m)
                    if kind == "F":
                        kk, (wp, ap) = r // 3, PASSES[r % 3]
                        wt = slot((w_hi, w_lo)[wp], s, k, w)
                        ins = T.matmul(ps_mm[:, 2 * bank_slot + m, :], wt[:, kk, m * P:(m + 1) * P],
                                       acts[ap][:, kk, :], start=(r == 0), stop=(r == per - 1),
                                       skip_group_check=chunk_waits is not None)
                    else:
                        tt, r2 = r // (3 * k), r % (3 * k)
                        kk, (wp, ap) = r2 // 3, PASSES[r2 % 3]
                        t = 2 * m + tt
                        wt = slot((w_hi, w_lo)[wp], s, k, w)
                        k0 = kacts or 0
                        first = r == 0 if kacts is not None or chunk_waits is not None else r2 == 0
                        ins = T.matmul(ps_mm[:, 2 * bank_slot + m, tt * w:(tt + 1) * w],
                                       acts[ap][:, k0 + kk, t * P:(t + 1) * P], wt[:, kk, :],
                                       start=first and start, stop=(r2 == 3 * k - 1) and stop,
                                       skip_group_check=kacts is not None or chunk_waits is not None)
                    if i == full_at[1] and b == 2 * per:
                        ins.then_inc(w_used, 1)
                    elif i == full_at[0] and b >= per and stop:
                        ins.then_inc(first_bank_full, 1)

            acts_x = (act_hi, act_lo)

            def straight(u, kind, acts, a=0, b=None, chunk_waits=None, w_by_chunk=False):
                src, k, w = unit_source(u)
                g = group_of(u)
                unit(u, u % 2, g % 2, lambda m: bank_due(g, m), kind, k, w, acts, a, b,
                     chunk_waits=chunk_waits, w_by_chunk=w_by_chunk)

            def stream(st, p, acts):
                a, b = st.cuts[p], st.cuts[p + 1]
                while a < b:
                    i = a // st.per
                    e = min(b, (i + 1) * st.per)
                    straight(U0[st.name] + i, "F", acts, a - i * st.per, e - i * st.per)
                    a = e

            def keep_warm(n):
                for _ in range(n):
                    T.matmul(ps_o[:, :], ident_r[:, :], window_r[:, :, :].rearrange("p e n -> p (e n)"),
                             start=True, stop=True)

            def turn_chunks(src, n, base):
                for t in range(TT):
                    for done, count in scaled_when(t, n, norm_scaled, norm_scaled_act):
                        pe.wait_ge(done, count)
                    for k in range(4):
                        ins = T.transpose(side_bank(k)[:, t * P:(t + 1) * P], src[:, t, k * P:(k + 1) * P],
                                          ident[:, :])
                        if t == TT - 1:
                            ins.then_inc(norm_turned, 1)
                for k in range(4, KD):
                    pe.wait_ge(norm_lo, base + k - 3)
                    for t in range(TT):
                        ins = T.transpose(side_bank(k)[:, t * P:(t + 1) * P], src[:, t, k * P:(k + 1) * P], ident[:, :])
                    ins.then_inc(norm_turned, 1)

            pe.wait_ge(dve_chain, 3)
            keep_warm(8)
            pe.wait_ge(ident_made, 1)
            pe.wait_ge(rows_landed, 16 * len(ROWS))
            T.transpose(ps_t[:, 0:NROWS], rows[0:NROWS, :], ident[0:NROWS, 0:NROWS]).then_inc(cols_turned, 1)
            pe.wait_ge(cols_made, 1)
            keep_warm(4)
            turn_chunks(x_sc, 1, 0)
            straight(0, "T", acts_x, chunk_waits=(norm_lo, 0), w_by_chunk=True)
            for u in range(1, 3):
                straight(u, "T", acts_x)
            straight(3, "F", acts_x)
            straight(4, "F", acts_x)
            pe.wait_ge(lat_scaled, 2 * TT)
            for i in range(6):
                if i >= 4:
                    pe.wait_ge(lat_lo, i - 3)
                for t in range(TT):
                    if i < 5:
                        ins = T.transpose(side_bank(i)[:, t * P:(t + 1) * P], lat[:, t, i * P:(i + 1) * P], ident[:, :])
                    else:
                        ins = T.transpose(side_bank(i)[0:MQ, t * P:(t + 1) * P], lat[:, t, LAT - MQ:LAT], ident[:, :])
                ins.then_inc(lat_turned, 1)
            straight(5, "F", acts_x)
            straight(6, "F", acts_x)
            lat_q = (lt_hi[:, 0:3, :], lt_lo[:, 0:3, :])
            lat_kv = (lt_hi[:, 3:5, :], lt_lo[:, 3:5, :])
            pe.wait_ge(lat_lo, 5)
            for i in range(3):
                straight(U0["qn"] + i, "F", lat_q)
            for i in range(2):
                straight(U0["kn"] + i, "F", lat_kv)
            for i in range(2):
                straight(U0["mv"] + i, "T", lat_kv)

            pe.wait_ge(bank_free, freed(U0["mv"] - 1, 1))
            pe.wait_ge(kpe_spread, MH)
            NP = 4 * MH
            for p in range(MLA_STEPS):
                if p < NP:
                    h, t = p // 4, p % 4
                    n = P * (t + 1)
                    if p >= 2:
                        pe.wait_ge(exp_made, p - 1)
                    if t == 0:
                        pe.wait_ge(q_spread, h + 1)
                    sb_ = ps_s[:, p % 2, :]
                    T.matmul(sb_[:, 0:n], qm[0:MQ, h, t * P:(t + 1) * P], km[0:MQ, h, 0:n], start=True, stop=False)
                    T.matmul(sb_[:, n - P:n], ident_r[:, :], causal_r[:, :], start=False, stop=True
                             ).then_inc(s_full, 1)
                q = p - LAG
                if q >= 0:
                    t = q % 4
                    pe.wait_ge(p_ready, q + 1)
                    if q >= 1:
                        pe.wait_ge(pt_made, q)
                    for j in range(t + 1):
                        ins = T.transpose(ps_t[:, j * P:(j + 1) * P], prob[:, q % 4, j * P:(j + 1) * P], ident[:, :])
                    ins.then_inc(t_full, 1)
                stream(MLA_STREAM, p, acts_x)
                if q >= 0:
                    h, t = q // 4, q % 4
                    if q == 0:
                        pe.wait_ge(bank_free, freed(U0["gate_b"] - 1, 1))
                    pe.wait_ge(pt_made, q + 1)
                    if t == 0 and h:
                        pe.wait_ge(o_free, h)
                    rr = slice((h % 2) * MV, (h % 2) * MV + MV)
                    for j in range(t + 1):
                        ins = T.matmul(ps_o[rr, t * P:(t + 1) * P], vm[:, j, h * MV:(h + 1) * MV],
                                       pt[:, q % 2, j * P:(j + 1) * P], start=(j == 0), stop=(j == t))
                    ins.then_inc(pv_done, 1)
            for name, kind in (("dq", "F"), ("dk", "F"), ("dv", "T")):
                for i in range(2):
                    straight(U0[name] + i, kind, acts_x)

            pe.wait_ge(bank_free, freed(U0["mrg_m"] - 1, 1))
            pe.wait_ge(o_free, MH)
            om = (om_hi, om_lo)
            NP = 4 * DH
            for p in range(DIFF_STEPS):
                if p < NP:
                    h, t = p // 4, p % 4
                    n = P * (t + 1)
                    for e in range(2):
                        if p >= 1:
                            pe.wait_ge(diff_exp_made, 2 * (p - 1) + e + 1)
                        rr = slice(e * DD, e * DD + DD)
                        T.matmul(ps_s[:, e, 0:n], dq[rr, h, t * P:(t + 1) * P], dk[rr, h, 0:n], start=True, stop=False)
                        T.matmul(ps_s[:, e, n - P:n], ident_r[:, :], causal_r[:, :], start=False, stop=True
                                 ).then_inc(diff_s_full, 1)
                q = p - LAG
                if 0 <= q < NP:
                    t = q % 4
                    pe.wait_ge(diff_p_ready, q + 1)
                    if q >= 1:
                        pe.wait_ge(diff_pt_made, q)
                    if q >= 7 and (q - 7) % 4 == 0:
                        pe.wait_ge(od_made, (q - 7) // 4 + 1)
                    for j in range(t + 1):
                        ins = T.transpose(ps_t[:, j * P:(j + 1) * P], prob[:, q % 4, j * P:(j + 1) * P], ident[:, :])
                    ins.then_inc(diff_t_full, 1)
                stream(DIFF_STREAM, p, om)
                if 0 <= q < NP:
                    h, t = q // 4, q % 4
                    pe.wait_ge(diff_pt_made, q + 1)
                    if t == 0 and h:
                        pe.wait_ge(o_copied, 4 * h)
                    for j in range(t + 1):
                        ins = T.matmul(ps_o[:, t * P:(t + 1) * P], pt[:, q % 2, j * P:(j + 1) * P],
                                       dv[:, j, h * DV:(h + 1) * DV], start=(j == 0), stop=(j == t))
                    ins.then_inc(diff_pv_done, 1)
                if q >= 6 and (q - 6) % 4 == 0:
                    hd = (q - 6) // 4
                    pe.wait_ge(o_scaled, 4 * hd + 4)
                    pe.wait_ge(diff_pt_made, min(q + 1, NP))
                    for t in range(TT):
                        ins = T.transpose(ps_t[:, t * P:(t + 1) * P], o_sb[:, t * P:(t + 1) * P], ident[:, :])
                    ins.then_inc(o_turned, 1)
            for i in range(4):
                straight(U0["mrg_d"] + i, "F", (od_hi, od_lo), chunk_waits=(od_made, 0) if i == 0 else None)
            for i in range(4):
                straight(U0["out"] + i, "T", acts_x, chunk_waits=(merged_lo, 0) if i == 0 else None)
            keep_warm(6)
            turn_chunks(n_sc, 2, KD)
            uf = U0["ffn"]
            for h in range(2):
                unit(uf + h, (uf + h) % 2, (uf + h) % 2, lambda m: bank_due(uf + h, m), "F", 8, 256, acts_x,
                     chunk_waits=(norm_lo, KD) if h == 0 else None)
            with pe.Fori(1, KF // 2) as j:
                for h in range(2):
                    def due(m):
                        if h == 0:
                            pe.wait_ge(bank_free_act, j * 2 + (m - 1))
                        else:
                            pe.wait_ge(bank_free, j * 2 + (freed(uf + 1, m) - 2))
                    unit(j * 2 + (uf + h), (uf + h) % 2, (uf + h) % 2, due, "F", 8, 256, acts_x)
            pe.wait_ge(bank_free_act, act_freed(group_of(U0["down"]) - 2, 1))
            pe.wait_ge(h_lo_made, sum(DOWN_K[:2]))
            ud = U0["down"]
            gd = group_of(ud)
            with pe.Fori(0, DOWN_GROUPS // 2) as j:
                for gg in range(2):
                    for i in range(3):
                        n = ud + 3 * gg + i
                        if i == 2:
                            pe.wait_ge(h_lo_made, KF)
                        def due(m):
                            pe.wait_ge(bank_free, j * 4 + (dve_freed(gd, m) + 2 * gg - 4))
                        unit(j * 6 + n, n % 2, (gd + gg) % 2, due, "T", DOWN_K[i], 256, (h_hi, h_lo),
                             kacts=sum(DOWN_K[:i]), start=(i == 0), stop=(i == 2))
            keep_warm(18)
            turn_chunks(n_sc, 3, 2 * KD)
            for i in range(4):
                straight(U0["q2"] + i, "F", acts_x, chunk_waits=(norm_lo, 2 * KD) if i == 0 else None)
            straight(U0["kv2"], "F", acts_x)
            straight(U0["za"], "F", acts_x)
            pe.wait_ge(bank_free, freed(U0["kv2"], 1))
            for t in range(TT):
                ins = T.transpose(ps_t[:, t * P:(t + 1) * P], kv[:, 0, t * P:(t + 1) * P], ident[:, :])
            ins.then_inc(v_turned, 1)
            for i in range(1, 4):
                straight(U0["za"] + i, "F", acts_x)
                if i == 3:
                    pe.wait_ge(wg_landed, 16)
                    pe.wait_ge(v2_made, 1)
                    for hb in range(2):
                        for g in range(4):
                            ins = T.transpose((ps_t, ps_o)[hb][:, g * P:(g + 1) * P], wg_in[:, 4 * hb + g, :],
                                              ident[:, :])
                        ins.then_inc(wg_turned, 1)
            pe.wait_ge(k_lo_made, 4)
            pe.wait_ge(q2_lo_made, AH)
            NP = WIN_PIECES
            for p in range(WIN_STEPS):
                if p < NP:
                    b, i = p // 8, p % 8
                    if p >= 2:
                        pe.wait_ge(win_exp_made, 2 * (p - 1))
                    j0 = 0 if b else P
                    k0 = (b - 1) * P if b else 0
                    ends = slice(0, 4, 3) if b else slice(3, 4)
                    T.matmul(ps_s[:, p % 2, :].rearrange("p (e c n) -> p e c n", e=2, c=4)[:, :, ends, :],
                             ident_r[:, :], window_r[:, :, :].rearrange("p e (c n) -> p e c n", c=4)[:, :, ends, :],
                             start=True, stop=False, skip_group_check=True)
                    rr = slice((i % 2) * AD, (i % 2) * AD + AD)
                    for e in range(2):
                        h = window_head(i, e)
                        out = ps_s[:, p % 2, e * 256 + j0:e * 256 + 256]
                        T.matmul(out, q_split[:, h, b * P:(b + 1) * P], k_hi[:, i // 4, k0:(b + 1) * P],
                                 start=False, stop=False, skip_group_check=True)
                        ins = T.matmul(out, q_split[rr, h, b * P:(b + 1) * P], k_lo[rr, i // 4, k0:(b + 1) * P],
                                       start=False, stop=(e == 1), skip_group_check=True)
                    ins.then_inc(win_s_full, 1)
                q = p - LAG
                if 0 <= q < NP:
                    if q == 0:
                        pe.wait_ge(wg_made, 1)
                    pe.wait_ge(win_exp_made, 2 * (q + 1))
                    if q >= 1:
                        pe.wait_ge(win_pt_made, q)
                    if q >= 5 and (q - 5) % 4 == 0:
                        pe.wait_ge(a_gated, (q - 5) // 4 + 1)
                    for e in range(2):
                        for kb in range(0 if q // 8 else 1, 2):
                            c = (2 * e + kb) * P
                            ins = T.transpose(ps_t[:, c:c + P], prob2[:, q % 4, c:c + P], ident[:, :])
                    ins.then_inc(win_t_full, 1)
                stream(WIN_STREAM, p, acts_x)
                if q >= 4 and q % 4 == 0:
                    g8 = (q - 4) // 4
                    pe.wait_ge(a_kept, g8 + 1)
                    pe.wait_ge(win_pt_made, min(q + 1, NP))
                    for c in range(4):
                        ins = T.transpose(ps_t[:, c * P:(c + 1) * P], a_tok[:, g8 % 2, c * P:(c + 1) * P], ident[:, :])
                    ins.then_inc(a_turned, 1)
                if 0 <= q < NP:
                    b, i = q // 8, q % 8
                    pe.wait_ge(win_pt_made, q + 1)
                    if q % 4 == 0 and q:
                        pe.wait_ge(a_kept, q // 4)
                    for e in range(2):
                        o = window_head(i % 4, e) * AD
                        for kb in range(0 if b else 1, 2):
                            c = (2 * e + kb) * P
                            ins = T.matmul(ps_o[:, o:o + AD], pt2[:, q % 2, c:c + P],
                                           v2[:, b - 1 + kb, (i // 4) * AD:(i // 4 + 1) * AD],
                                           start=(kb == (0 if b else 1)), stop=(kb == 1))
                    ins.then_inc(win_pv_done, 1)
            for i in range(4):
                straight(U0["u2"] + i, "F", acts_x)
            for i in range(4):
                straight(U0["vs"] + i, "T", acts_x)
            for i in range(4):
                straight(U0["ga"] + i, "F", acts_x)
            pe.wait_ge(at_lo_made, KD)
            for i in range(4):
                straight(U0["att"] + i, "F", (at_hi, at_lo))
            pe.wait_ge(vs_normed, TT)
            for g in range(8):
                if g >= 4:
                    pe.wait_ge(sg_lo_made, g - 3)
                for b in range(TT):
                    ins = T.matmul(side_bank(g)[:, b * P:(b + 1) * P], vs[:, b, g * P:(g + 1) * P], wg_t[:, g, :],
                                   start=True, stop=True)
                ins.then_inc(mix_full, 1)
                straight(U0["gs"] + g // 2, "F", acts_x, 24 * (g % 2), 24 * (g % 2) + 24)
            pe.wait_ge(sg_lo_made, 8)
            for i in range(4):
                straight(U0["sgo"] + i, "F", (at_hi, at_lo))
            for i in range(4):
                straight(U0["wo"] + i, "T", acts_x, chunk_waits=(y_lo_made, 0) if i == 0 else None)


_INS = ["x", "positions", "norm_mix_g", "w_in", "b_gate", "mla_q_norm_g", "mla_w_uq", "mla_kv_norm_g", "mla_w_ukv",
        "diff_lambda_q1", "diff_lambda_k1", "diff_lambda_q2", "diff_lambda_k2", "diff_subln_g", "w_branch_mla",
        "w_branch_diff", "w_out", "norm_ffn_g", "w_ffn_gate", "w_ffn_up", "w_ffn_down", "norm_final_g", "norm_g_2",
        "w_in_2", "b_merge_2", "att_sinks_2", "sg_w_2", "sg_b_2", "sg_ln_g_2", "sg_ln_b_2", "w_att_out_2",
        "w_sg_out_2", "w_o_2", "final_g_2"]


def rope_frequencies():
    import numpy as np

    f = np.zeros((P, 2), np.float32)
    theta = np.float64(500000.0)
    for i in range(MR // 2):
        w = np.float32(theta ** (-2.0 * i / MR))
        for r in range(0, P, MR):
            f[r + i, 0], f[r + MR // 2 + i, 0] = -w, w
    rot = DD // 4
    for i in range(rot // 2):
        w = np.float32(theta ** (-2.0 * i / rot))
        for r in (0, DD):
            f[r + i, 1], f[r + rot // 2 + i, 1] = -w, w
    return f


def kernel(**inputs):
    import numpy as np
    import concourse.bacc as bacc
    from concourse.bass_utils import run_bass_kernel_spmd

    nc = bacc.Bacc("TRN2", target_bir_lowering=False, num_devices=1)
    arrays, aps = {}, {}
    for name in _INS:
        a = np.ascontiguousarray(inputs[name])
        arrays[f"in_{name}"] = a
        aps[name] = nc.dram_tensor(f"in_{name}", a.shape, mybir.dt.from_np(a.dtype), kind="ExternalInput").ap()
    arrays["rope_freq"] = rope_frequencies()
    aps["rope_freq"] = nc.dram_tensor("rope_freq", (P, 2), F32, kind="ExternalInput").ap()
    aps["out"] = nc.dram_tensor("out", (1, S, D), F32, kind="ExternalOutput").ap()
    build(nc, aps)
    r = run_bass_kernel_spmd(nc, [arrays], core_ids=[0])
    return r.results[0]["out"]
```
